# Optimizing a Trainium2 kernel written in Bass

```python
import jax, jax.numpy as jnp
from jax import lax
import numpy as np

D_MODEL = 1024
BATCH = 1
SEQ = 128
DEPTH = 2
DEC_BATCH = 1
DEC_SEQ = 512
PAST_LEN = 128

GRID_W = 64
CHUNK = 128
EPS = 1e-6
GMLP_GROUPS = 4
GMLP_W = 256
CONV_W = 256
CONV_K = 31
RET_HEADS = 4
RET_DK = 64
RET_DV = 64
RET_W = RET_HEADS * RET_DV
MLA_HEADS = 4
MLA_Q_LORA = 192
MLA_KV_LORA = 128
MLA_NOPE = 64
MLA_ROPE = 32
MLA_V = 64
MLA_W = MLA_HEADS * MLA_V
MIX_W = GMLP_W + CONV_W + RET_W + MLA_W
ROPE_THETA = 10000.0
N_EXPERTS = 16
EXPERT_FF = 1024
EC_CAPACITY = 2
IN_SIZES = (GMLP_W, GMLP_W, CONV_W, CONV_W, RET_HEADS * RET_DK, RET_HEADS * RET_DK, RET_W, RET_W, RET_W, MLA_Q_LORA, MLA_KV_LORA, MLA_ROPE)
IN_W = sum(IN_SIZES)
F32 = jnp.float32

kernel_name = 'hybrid_prefix_diffusion_trunk'

def rms_norm(x, g):
    xf = x.astype(F32)
    y = xf * lax.rsqrt(jnp.mean(xf * xf, axis=-1, keepdims=True) + EPS)
    return y.astype(x.dtype) * g

def layer_norm(x, g, b):
    xf = x.astype(F32)
    mu = jnp.mean(xf, axis=-1, keepdims=True)
    var = jnp.mean(jnp.square(xf - mu), axis=-1, keepdims=True)
    return ((xf - mu) * lax.rsqrt(var + EPS)).astype(x.dtype) * g + b

def head_group_norm(o, g):
    of = o.astype(F32)
    mu = jnp.mean(of, axis=-1, keepdims=True)
    var = jnp.mean(jnp.square(of - mu), axis=-1, keepdims=True)
    y = ((of - mu) * lax.rsqrt(var + EPS)).astype(o.dtype)
    return y.reshape(o.shape[0], o.shape[1], -1) * g

def chunk_spatial_gating(u, v, g, w_s, b_s):
    bsz, n, _ = v.shape
    v = rms_norm(v, g).reshape(bsz, n // CHUNK, CHUNK, GMLP_GROUPS, GMLP_W // GMLP_GROUPS)
    mixed = jnp.einsum('hij,bcjhd->bcihd', w_s, v) + b_s.T[None, None, :, :, None]
    return u * mixed.reshape(bsz, n, GMLP_W)

def conformer_conv(a, gt, w_dw, b_dw, ln_g, ln_b, w_pw):
    y = a * jax.nn.sigmoid(gt)
    y = lax.conv_general_dilated(y, w_dw[:, None, :], window_strides=(1,), padding=[(CONV_K // 2, CONV_K // 2)], dimension_numbers=('NWC', 'WIO', 'NWC'), feature_group_count=CONV_W) + b_dw
    return jax.nn.silu(layer_norm(y, ln_g, ln_b)) @ w_pw

def retention_scan(q, k, v, log2_1m_gamma, s0):
    bsz, n, h, dk = q.shape
    nc = n // CHUNK
    dt = q.dtype
    lg = jnp.log1p(-jnp.exp2(log2_1m_gamma.astype(F32)))
    pos = jnp.arange(CHUNK, dtype=F32)
    diff = pos[:, None] - pos[None, :]
    intra = jnp.where(diff >= 0, jnp.exp(jnp.maximum(diff, 0.0) * lg[:, None, None]), 0.0).astype(dt)
    q_dec = jnp.exp((pos + 1.0) * lg[:, None]).astype(dt)
    k_dec = jnp.exp((CHUNK - 1.0 - pos) * lg[:, None]).astype(dt)
    c_dec = jnp.exp(CHUNK * lg).astype(dt)[None, :, None, None]
    qc = q.reshape(bsz, nc, CHUNK, h, dk)
    kc = k.reshape(bsz, nc, CHUNK, h, dk)
    vc = v.reshape(bsz, nc, CHUNK, h, -1)
    scores = jnp.einsum('bcihd,bcjhd->bchij', qc, kc) * intra
    inner = jnp.einsum('bchij,bcjhe->bcihe', scores, vc)
    kv = jnp.einsum('bcjhd,hj,bcjhe->cbhde', kc, k_dec, vc)

    def step(s, kv_c):
        return c_dec * s + kv_c, s

    s_fin, s_prev = lax.scan(step, s0.astype(dt), kv)
    cross = jnp.einsum('bcihd,cbhde,hi->bcihe', qc, s_prev, q_dec)
    return (inner + cross).reshape(bsz, n, h, -1), s_fin

def bidirectional_retention(q, k, v, gate_f, gate_b, p_f, p_b, gn_g, s0_f, s0_b):
    o_f, s_f = retention_scan(q, k, v, p_f, s0_f)
    o_b, s_b = retention_scan(q[:, ::-1], k[:, ::-1], v[:, ::-1], p_b, s0_b)
    y = jax.nn.silu(gate_f) * head_group_norm(o_f, gn_g) + jax.nn.silu(gate_b) * head_group_norm(o_b[:, ::-1], gn_g)
    return y, s_f, s_b

def axial_rope_tables(n):
    rows = n // GRID_W
    row = jnp.repeat(jnp.arange(rows, dtype=F32), GRID_W)
    col = jnp.tile(jnp.arange(GRID_W, dtype=F32), rows)
    inv = ROPE_THETA ** (-jnp.arange(0, MLA_ROPE // 2, 2, dtype=F32) / (MLA_ROPE // 2))
    ra = row[:, None] * inv
    ca = col[:, None] * inv
    ang = jnp.concatenate([ra, ra, ca, ca], axis=-1)
    return jnp.cos(ang), jnp.sin(ang)

def apply_axial_rope(x, cos, sin):
    x1, x2, x3, x4 = jnp.split(x, 4, axis=-1)
    rot = jnp.concatenate([-x2, x1, -x4, x3], axis=-1)
    return x * cos.astype(x.dtype) + rot * sin.astype(x.dtype)

def block_softmax_attention(q, k, v):
    bsz, n, h, dk = q.shape
    scale = dk ** -0.5
    qb = q.reshape(bsz, n // CHUNK, CHUNK, h, dk).transpose(1, 0, 2, 3, 4)

    def one_block(qblk):
        s = jnp.einsum('bqhd,bkhd->bhqk', qblk, k).astype(F32) * scale
        p = jax.nn.softmax(s, axis=-1).astype(v.dtype)
        return jnp.einsum('bhqk,bkhd->bqhd', p, v)

    o = lax.map(one_block, qb)
    return o.transpose(1, 0, 2, 3, 4).reshape(bsz, n, h * v.shape[-1])

def mla_expand(ckv, kpe, w_ukv):
    bsz, m, _ = ckv.shape
    kv = (ckv @ w_ukv).reshape(bsz, m, MLA_HEADS, MLA_NOPE + MLA_V)
    k = jnp.concatenate([kv[..., :MLA_NOPE], jnp.broadcast_to(kpe[:, :, None, :], (bsz, m, MLA_HEADS, MLA_ROPE))], axis=-1)
    return k, kv[..., MLA_NOPE:]

def latent_attention(cq, ckv_raw, kpe, q_norm_g, w_uq, kv_norm_g, w_ukv, rope, ctx_ckv, ctx_kpe):
    bsz, n, _ = cq.shape
    q = (rms_norm(cq, q_norm_g) @ w_uq).reshape(bsz, n, MLA_HEADS, MLA_NOPE + MLA_ROPE)
    ckv = rms_norm(ckv_raw, kv_norm_g)
    if rope is None:
        k_ckv, k_pe = ckv, kpe
    else:
        cos, sin = rope
        q = jnp.concatenate([q[..., :MLA_NOPE], apply_axial_rope(q[..., MLA_NOPE:], cos[:, None], sin[:, None])], axis=-1)
        k_ckv = jnp.concatenate([ctx_ckv, ckv], axis=1)
        k_pe = jnp.concatenate([ctx_kpe, apply_axial_rope(kpe, cos, sin)], axis=1)
    k, v = mla_expand(k_ckv, k_pe, w_ukv)
    return block_softmax_attention(q, k, v), ckv, kpe

def expert_choice_ffn(h, router, w_gate, w_up, w_down):
    bsz, n, d = h.shape
    cap = EC_CAPACITY * n // N_EXPERTS
    aff = jax.nn.softmax((h @ router).astype(F32), axis=-1)
    gate, idx = lax.top_k(jnp.swapaxes(aff, 1, 2), cap)

    def per_request(hb, gb, ib):
        xe = hb[ib]
        a = jnp.einsum('ecd,edf->ecf', xe, w_gate)
        b = jnp.einsum('ecd,edf->ecf', xe, w_up)
        ye = jnp.einsum('ecf,efd->ecd', jax.nn.silu(a) * b, w_down) * gb[..., None].astype(hb.dtype)
        return jnp.zeros_like(hb).at[ib.reshape(-1)].add(ye.reshape(-1, d))

    return jax.vmap(per_request)(h, gate, idx)

def trunk_layer(x, mod, lw, rope=None, ctx=None):
    bsz, n, _ = x.shape
    sh1, sc1, g1, sh2, sc2, g2 = jnp.split(mod[:, None, :], 6, axis=-1)
    h = rms_norm(x, lw['norm1_g']) * (1 + sc1) + sh1
    splits = np.cumsum(IN_SIZES)[:-1].tolist()
    u, vg, ca, cg, rq, rk, rv, rgf, rgb, cq, ckv_raw, kpe = jnp.split(h @ lw['w_in'], splits, axis=-1)
    y_a = chunk_spatial_gating(u, vg, lw['sg_norm_g'], lw['sg_w'], lw['sg_b'])
    y_b = conformer_conv(ca, cg, lw['conv_w'], lw['conv_b'], lw['conv_ln_g'], lw['conv_ln_b'], lw['conv_pw'])
    rq = rq.reshape(bsz, n, RET_HEADS, RET_DK)
    rk = rk.reshape(bsz, n, RET_HEADS, RET_DK) * (RET_DK ** -0.5)
    rv = rv.reshape(bsz, n, RET_HEADS, RET_DV)
    if ctx is None:
        s0 = jnp.zeros((bsz, RET_HEADS, RET_DK, RET_DV), x.dtype)
        s0_f, s0_b, ctx_ckv, ctx_kpe = s0, s0, None, None
    else:
        ctx_ckv, ctx_kpe, ret = ctx
        s0_f, s0_b = ret[:, 0], ret[:, 1]
    y_c, s_f, s_b = bidirectional_retention(rq, rk, rv, rgf, rgb, lw['ret_decay_f'], lw['ret_decay_b'], lw['ret_gn_g'], s0_f, s0_b)
    y_d, ckv, kpe = latent_attention(cq, ckv_raw, kpe, lw['q_norm_g'], lw['w_uq'], lw['kv_norm_g'], lw['w_ukv'], rope, ctx_ckv, ctx_kpe)
    x = x + g1 * (jnp.concatenate([y_a, y_b, y_c, y_d], axis=-1) @ lw['w_out'])
    h2 = rms_norm(x, lw['norm2_g']) * (1 + sc2) + sh2
    x = x + g2 * expert_choice_ffn(h2, lw['router'], lw['w_gate'], lw['w_up'], lw['w_down'])
    return x, ckv, kpe, jnp.stack([s_f, s_b], axis=1)

def setup_inputs(seed: int = 0) -> dict:
    key = jax.random.key(seed)
    keys = jax.random.split(key, 40)

    def nrm(i, shape, scale=1.0):
        return jax.random.normal(keys[i], shape, F32) * scale

    def gain(i, shape):
        return 1.0 + nrm(i, shape, 0.02)

    L = DEPTH
    head_idx = jnp.arange(RET_HEADS, dtype=F32)
    return {
        'x_prompt': nrm(0, (BATCH, SEQ, D_MODEL)),
        'x_sample': nrm(1, (DEC_BATCH, DEC_SEQ, D_MODEL)),
        'cache_mla_ckv': nrm(2, (DEC_BATCH, DEPTH, PAST_LEN, MLA_KV_LORA)),
        'cache_mla_kpe': nrm(3, (DEC_BATCH, DEPTH, PAST_LEN, MLA_ROPE)),
        'state_ret': nrm(4, (DEC_BATCH, DEPTH, 2, RET_HEADS, RET_DK, RET_DV)),
        'c': nrm(5, (DEC_BATCH, D_MODEL)),
        'c_ctx': nrm(6, (D_MODEL,)),
        'w_mod': nrm(7, (L, D_MODEL, 6 * D_MODEL), 0.5 * D_MODEL ** -0.5),
        'b_mod': nrm(8, (L, 6 * D_MODEL), 0.02),
        'norm1_g': gain(9, (L, D_MODEL)),
        'w_in': nrm(10, (L, D_MODEL, IN_W), D_MODEL ** -0.5),
        'sg_norm_g': gain(11, (L, GMLP_W)),
        'sg_w': nrm(12, (L, GMLP_GROUPS, CHUNK, CHUNK), CHUNK ** -0.5),
        'sg_b': nrm(13, (L, GMLP_GROUPS, CHUNK), 0.02),
        'conv_w': nrm(14, (L, CONV_K, CONV_W), CONV_K ** -0.5),
        'conv_b': nrm(15, (L, CONV_W), 0.02),
        'conv_ln_g': gain(16, (L, CONV_W)),
        'conv_ln_b': nrm(17, (L, CONV_W), 0.02),
        'conv_pw': nrm(18, (L, CONV_W, CONV_W), CONV_W ** -0.5),
        'ret_decay_f': -5.0 - head_idx + nrm(19, (L, RET_HEADS), 0.1),
        'ret_decay_b': -5.0 - head_idx + nrm(20, (L, RET_HEADS), 0.1),
        'ret_gn_g': gain(21, (L, RET_W)),
        'q_norm_g': gain(22, (L, MLA_Q_LORA)),
        'w_uq': nrm(23, (L, MLA_Q_LORA, MLA_HEADS * (MLA_NOPE + MLA_ROPE)), MLA_Q_LORA ** -0.5),
        'kv_norm_g': gain(24, (L, MLA_KV_LORA)),
        'w_ukv': nrm(25, (L, MLA_KV_LORA, MLA_HEADS * (MLA_NOPE + MLA_V)), MLA_KV_LORA ** -0.5),
        'w_out': nrm(26, (L, MIX_W, D_MODEL), MIX_W ** -0.5),
        'norm2_g': gain(27, (L, D_MODEL)),
        'router': nrm(28, (L, D_MODEL, N_EXPERTS), D_MODEL ** -0.5),
        'w_gate': nrm(29, (L, N_EXPERTS, D_MODEL, EXPERT_FF), D_MODEL ** -0.5),
        'w_up': nrm(30, (L, N_EXPERTS, D_MODEL, EXPERT_FF), D_MODEL ** -0.5),
        'w_down': nrm(31, (L, N_EXPERTS, EXPERT_FF, D_MODEL), EXPERT_FF ** -0.5),
        'final_norm_g': gain(32, (D_MODEL,)),
    }

def reference(x_prompt, x_sample, cache_mla_ckv, cache_mla_kpe, state_ret, c, c_ctx, w_mod, b_mod, norm1_g, w_in, sg_norm_g, sg_w, sg_b, conv_w, conv_b, conv_ln_g, conv_ln_b, conv_pw, ret_decay_f, ret_decay_b, ret_gn_g, q_norm_g, w_uq, kv_norm_g, w_ukv, w_out, norm2_g, router, w_gate, w_up, w_down, final_norm_g):
    rope = axial_rope_tables(x_sample.shape[1])
    xp, xs = x_prompt, x_sample
    ckvs, kpes, rets = [], [], []
    for l in range(DEPTH):
        lw = dict(norm1_g=norm1_g[l], w_in=w_in[l], sg_norm_g=sg_norm_g[l], sg_w=sg_w[l], sg_b=sg_b[l],
                  conv_w=conv_w[l], conv_b=conv_b[l], conv_ln_g=conv_ln_g[l], conv_ln_b=conv_ln_b[l], conv_pw=conv_pw[l],
                  ret_decay_f=ret_decay_f[l], ret_decay_b=ret_decay_b[l], ret_gn_g=ret_gn_g[l],
                  q_norm_g=q_norm_g[l], w_uq=w_uq[l], kv_norm_g=kv_norm_g[l], w_ukv=w_ukv[l],
                  w_out=w_out[l], norm2_g=norm2_g[l], router=router[l], w_gate=w_gate[l], w_up=w_up[l], w_down=w_down[l])
        mod_ctx = (jax.nn.silu(c_ctx) @ w_mod[l] + b_mod[l])[None, :]
        mod_lat = jax.nn.silu(c) @ w_mod[l] + b_mod[l]
        xp, ckv, kpe, st = trunk_layer(xp, mod_ctx, lw)
        ckvs.append(ckv)
        kpes.append(kpe)
        rets.append(st)
        xs = trunk_layer(xs, mod_lat, lw, rope, (cache_mla_ckv[:, l], cache_mla_kpe[:, l], state_ret[:, l]))[0]
    y_prompt = rms_norm(xp, final_norm_g)
    y_sample = rms_norm(xs, final_norm_g)
    return (y_prompt, y_sample, jnp.stack(ckvs, axis=1), jnp.stack(kpes, axis=1), jnp.stack(rets, axis=1))


_drawn_inputs = setup_inputs


def setup_inputs(seed=0):
    import zlib

    import numpy as np

    out = dict(_drawn_inputs(seed))
    spreads = {}
    factors = {'cache_mla_ckv': 6.823,
     'cache_mla_kpe': 8.0,
     'sg_norm_g': 8.0,
     'sg_b': 8.0,
     'conv_b': 8.0,
     'conv_ln_g': 8.0,
     'conv_ln_b': 8.0,
     'ret_gn_g': 8.0,
     'q_norm_g': 8.0,
     'kv_norm_g': 2.667,
     'norm2_g': 6.535,
     'final_norm_g': 2.726}
    for name, (base, spread) in spreads.items():
        noise = np.random.default_rng([zlib.crc32(name.encode()), seed]).standard_normal(out[name].shape)
        drawn = base * np.exp(spread * noise) if base else spread * noise
        out[name] = __import__('jax').numpy.asarray(drawn.astype(out[name].dtype))
    for name, factor in factors.items():
        out[name] = (out[name] * factor).astype(out[name].dtype)
    return out
```

```python
from contextlib import ExitStack

import concourse.bass as bass
from concourse import mybir
import numpy as np

F32 = mybir.dt.float32
ALU = mybir.AluOpType
ACT = mybir.ActivationFunctionType
AX = mybir.AxisListType

P = 128
D = 1024
KD = D // P
DEPTH = 2
TS, TP = 4, 1
NT = TS + TP
CTX = TS
NTOK = NT * P
NKEY = NTOK + P
SAMPLE, PROMPT = TS * P, TP * P
HEADS = 4
GW = 256
NG = GW // P
TAPS = 31
PAD = TAPS // 2
CROW = SAMPLE + PROMPT + 4 * PAD
CVAL = CROW - 2 * PAD
CPROMPT = SAMPLE + 2 * PAD
QL, KL, ROPE, NOPE, QK = 192, 128, 32, 64, 96
MLA_IN = QL + KL + ROPE
EXPERTS, FF = 16, 1024
KF = FF // P
CAPS, CAPP = 64, 16
SLOTS = CAPS + CAPP
EPS = 1e-6
ATT_SCALE = float(QK) ** -0.5

IN_AT = dict(u=0, vg=256, ca=512, cg=768, rq=1024, rk=1280, rv=1536, rgf=1792, rgb=2048, mla_a=2304, mla_b=2560)
MLA_B = QL + KL + ROPE - GW

UNITS = [("mod", i) for i in range(8)] + [("in", "mla_a"), ("in", "mla_b")]
for _n, _g in enumerate(["", "ca", "cg", "u", "vg", "rq", "rk", "rv"]):
    UNITS += ([("in", _g)] if _g else []) + [("mod", 8 + 2 * _n), ("mod", 9 + 2 * _n)]
UNITS += [("in", "rgf"), ("in", "rgb")] + [("out", i) for i in range(4)]
NSTREAM = 3
NUNIT = len(UNITS)
assert NUNIT % NSTREAM == 0

BLOCKS = [(h, t) for h in range(HEADS) for t in range(TS)] + [("ctx", CTX)]
BLOCKS_AFTER = {"rq": 3, "rk": 3, "rv": 3, "rgf": 3, "rgb": 5}

STEPS = ["mod:0-8", "norm1", "in:mla", "mod:8-10", "in:ca", "mod:10-12", "in:cg", "mod:12-14", "latents", "mla_q", "mla_kv",
         "in:u", "mod:14-16", "in:vg", "mod:16-18", "conv_mean"]
_b = 0
for _n, _g in enumerate(["rq", "rk", "rv", "rgf", "rgb"]):
    STEPS += [f"in:{_g}"] + ([f"mod:{18 + 2 * _n}-{20 + 2 * _n}"] if _n < 3 else [])
    STEPS += {"rq": ["conv_var", "mix"], "rk": ["conv_out"], "rv": ["ret_tables"]}.get(_g, [])
    STEPS += [f"att:{_i}" for _i in range(_b, _b + BLOCKS_AFTER[_g])]
    _b += BLOCKS_AFTER[_g]
STEPS += ["att_end", "rows_g1", "retention", "out_proj", "norm2", "router", "rows_g2"]

TOKEN_MAJOR = ("vg", "rv", "rgf", "rgb")
W_JOBS, T_JOBS, N_JOBS = [], [], []
for _s in STEPS:
    _k, _, _a = _s.partition(":")
    if _k == "mod":
        N_JOBS += [f"mod.{_i}" for _i in range(*map(int, _a.split("-")))]
    elif _k in ("norm1", "norm2"):
        T_JOBS += [f"{_k}.{i}" for i in range(KD + 2)]
    elif _k == "in":
        W_JOBS += ["mla_a.s", "mla_a.p", "mla_b"] if _a == "mla" else [f"{_a}.s", f"{_a}.p"] if _a in TOKEN_MAJOR else [f"{_a}.0", f"{_a}.1"]
        T_JOBS += ["ktok.0", "ktok.1", "ktok.p"] if _a == "rk" else []
    elif _k == "latents":
        T_JOBS += ["cq.0", "cq.1", "cq.p", "ckv.0", "ckv.1", "kpe.0", "kpe.1"]
    elif _k == "mla_q":
        W_JOBS += ["q.0", "q.1", "q.2"]
        T_JOBS += [f"qh.{h}" for h in range(HEADS)] + ["qh.p"]
    elif _k == "mla_kv":
        W_JOBS += [f"kh.{h}" for h in range(HEADS)] + ["v.0", "v.1"]
    elif _k == "mix":
        W_JOBS += ["mix.0", "mix.1"]
    elif _k == "conv_mean":
        W_JOBS += ["mean"]
    elif _k == "conv_var":
        N_JOBS += ["var"]
        W_JOBS += ["cstd"]
    elif _k == "conv_out":
        W_JOBS += ["pw.0", "pw.1"]
    elif _k == "att":
        W_JOBS += [f"s.{_a}"]
    elif _k == "rows_g1":
        W_JOBS += ["g1.s", "g1.p"]
    elif _k == "retention":
        N_JOBS += [f"kv.{t}" for t in range(NT)]
        for _t in range(NT):
            W_JOBS += [f"rs.{_t}"]
            if _t:
                W_JOBS += [f"ro.{_t - 1}"]
        W_JOBS += [f"ro.{NT - 1}"]
        T_JOBS += ["yc.0", "yc.1", "yc.p"]
    elif _k == "out_proj":
        W_JOBS += [f"o.{u}.{h}" for u in range(4) for h in "sp"]
    elif _k == "router":
        N_JOBS += ["logits"]
        T_JOBS += ["afft.s", "afft.p", "slots"]
    elif _k == "rows_g2":
        W_JOBS += ["g2"]
    if _k == "att" and int(_a) >= 1 or _k == "att_end":
        _i = int(_a) - 1 if _k == "att" else len(BLOCKS) - 1
        T_JOBS += [f"pt.{_i}", f"pt.{_i}b"] if _i < len(BLOCKS) - 1 else [f"pt.{_i}"]
        N_JOBS += [f"pv.{_i}"]
    if _k == "att_end":
        T_JOBS += ["yd.0", "yd.1", "yd.p"]
for _jobs in (W_JOBS, T_JOBS, N_JOBS):
    if len(_jobs) % 2:
        _jobs.append("spare")

FRONT = 4
COMBINE = NT * 2
T_EXPERT = FRONT + 2 + COMBINE
T_MOE = EXPERTS * T_EXPERT

LAST_JOB = {("in", g): (f"{g}.p" if g in TOKEN_MAJOR else f"{g}.1") for g in IN_AT}
LAST_JOB[("in", "mla_a")], LAST_JOB[("in", "mla_b")] = "mla_a.p", "mla_b"
LAST_JOB.update({("out", i): f"o.{i}.p" for i in range(4)})
LAST_JOB.update({("mod", i): f"mod.{i}" for i in range(24)})

PARAMS = dict(n1g=KD, n2g=KD, bmod=48, router=KD * EXPERTS, sgg=NG, convb=NG, lng=NG, lnb=NG, gng=NG, dec=12,
              convw=NG * TAPS, sgb=NG * P, sgw=HEADS * P, pw=NG * GW, qg=QL, kvg=KL, wuq=2 * HEADS * QK,
              wukv=HEADS * 2 * NOPE, cache=KL + ROPE, s0=2 * NG * NOPE)
CONSTS = dict(ident=P, mean=P, expo=2 * P, mask=2 * P, qpos=2 * P, kpos=2, cos=TS * HEADS * ROPE,
              sin=TS * HEADS * ROPE, iota=SLOTS, eps=1)


def spans(sizes):
    out, at = {}, 0
    for name, n in sizes.items():
        out[name] = (at, at + n)
        at += n
    return out, at


PAT, NPARAM = spans(PARAMS)
CAT, NCONST = spans(CONSTS)
NSMALL = 384
KEPT = PAT["router"][1]


START = 1


class Jobs:

    def __init__(self, jobs, moe, per_expert, done, out):
        self.at = {j: i for i, j in enumerate(jobs)}
        self.dense, self.layer, self.expert, self.done_sem, self.out_sem = len(jobs), len(jobs) + moe, per_expert, done, out
        assert len(self.at) == len(jobs) and self.layer % 2 == 0 and per_expert % 2 == 0

    def index(self, job):
        return self.at[job] if isinstance(job, str) else self.dense + job

    def buf(self, job):
        return self.index(job) % 2

    def full(self, l, job, e=0):
        return l * self.layer + e * self.expert + self.index(job)

    def half(self, l, job, e=0):
        return l * (self.layer // 2) + e * (self.expert // 2) + self.index(job) // 2

    def claim(self, pe, l, job, e=0):
        pe.wait_ge(self.out_sem[self.buf(job)], START + self.half(l, job, e))

    def finish(self, ins):
        ins.then_inc(self.done_sem, 1)

    def wait(self, eng, l, job, e=0):
        eng.wait_ge(self.done_sem, START + self.full(l, job, e) + 1)

    def take(self, ins, job):
        ins.then_inc(self.out_sem[self.buf(job)], 1)

    def taken(self, eng, l, job, e=0):
        eng.wait_ge(self.out_sem[self.buf(job)], START + self.half(l, job, e) + 1)

    def layers_taken(self, eng, l):
        for s in self.out_sem:
            eng.wait_ge(s, START + l * (self.layer // 2))

    def layers_done(self, eng, l):
        eng.wait_ge(self.done_sem, START + l * self.layer)

    def start(self, eng):
        for s in (self.done_sem, *self.out_sem):
            eng.sem_inc(s, START)


class Chain:

    def __init__(self, eng, sem, per_layer):
        self.eng, self.sem, self.per_layer = eng, sem, per_layer
        self.base, self.n = 0, 0

    def start_layer(self, l, before=0):
        self.base, self.n = l * self.per_layer + before, 0

    def mark(self, ins):
        ins.then_inc(self.sem, 1)
        self.n += 1
        return self.n

    def wait(self, n):
        self.eng.wait_ge(self.sem, self.base + n)

    def link(self, ins):
        self.wait(self.mark(ins))

    def end_layer(self):
        if self.n != self.per_layer:
            raise ValueError(f"the links of a layer are {self.n}, not {self.per_layer}")


DVE_LINKS = 158


def build(nc, io):
    ctx = ExitStack()
    with ctx:
        def sb(name, n):
            return ctx.enter_context(nc.sbuf_tensor(name, [P, n], F32))[:, :]

        def sem(name):
            return ctx.enter_context(nc.semaphore(name))

        def carve(region, at, *dims, parts=(0, P)):
            n = int(np.prod(dims))
            v = region[parts[0]:parts[1], at:at + n]
            names = " ".join(f"d{i}" for i in range(len(dims)))
            return v.rearrange(f"p ({names}) -> p {names}", **{f"d{i}": d for i, d in enumerate(dims)}) if len(dims) > 1 else v

        x = carve(sb("x", NT * D), 0, NT, D)
        xn_r = sb("xn_yt", NT * D)
        xn = carve(xn_r, 0, NT, D)
        yT = carve(xn_r, 0, KD, NTOK)
        h_r = sb("ht", KD * NTOK)
        hT = carve(h_r, 0, KD, NTOK)
        stream_r = sb("stream", NSTREAM * KD * GW)
        stream = carve(stream_r, 0, NSTREAM, KD, GW)
        RING = 12
        ring_r = sb("ring", RING * 2 * D)
        ring = carve(ring_r, 0, RING, 2, D)
        par_r = sb("param_cols", NPARAM)
        con_r = sb("const_cols", NCONST)

        def par(name, *dims, parts=(0, P)):
            return carve(par_r, PAT[name][0], *(dims or (PARAMS[name],)), parts=parts)

        def con(name, *dims, parts=(0, P)):
            return carve(con_r, CAT[name][0], *(dims or (CONSTS[name],)), parts=parts)

        ident, mean_w = con("ident"), con("mean")
        ctxt = carve(sb("ctx_tok", NT * (KL + ROPE)), 0, NT, KL + ROPE)
        sT = carve(sb("cond_cols", KD * 2), 0, KD, 2)
        modT = carve(sb("mod_cols", 48 * 2), 0, 48, 2)
        A1 = carve(sb("scale1", KD * 2), 0, KD, 2)
        A2 = carve(sb("scale2", KD * 2), 0, KD, 2)
        small_r = sb("stats", NSMALL)
        _at = [0]

        def small(*dims):
            v = carve(small_r, _at[0], *dims)
            _at[0] += int(np.prod(dims))
            assert _at[0] <= NSMALL
            return v

        ss, std, rstd = small(NT), small(NT), small(NT)
        mss, mstd, mrstd = small(2, NT), small(2, NT), small(2, NT)
        vss, vstd, vrstd = small(NT), small(NT), small(NT)
        css, cstd, crstd = small(NT), small(NT), small(NT)
        lgt = small(6, 12)
        kd, cdec = small(2 * HEADS), small(2, NG)
        nmax, rsum, rinv = small(2, HEADS), small(2, HEADS), small(2, HEADS)
        amax, asum, arec = small(NT), small(NT), small(NT)
        affc, gate = small(NT), small(1)
        rsums, rvar, rdev, rrstd = small(NT, 8), small(NT, 8), small(NT, 8), small(NT, 8)
        top8, spare = small(8), small(2)

        r_at = [0]

        def room(n):
            r_at[0] += n
            assert r_at[0] <= RING * 2 * D
            return r_at[0] - n

        MLA0 = room(NT * MLA_IN)
        mla = carve(ring_r, MLA0, NT, MLA_IN)
        ydt = carve(ring_r, MLA0, NT, GW)
        LAT0 = room(HEADS * NTOK + HEADS * NKEY + 6 * GW + NKEY)
        qhT = carve(ring_r, LAT0, HEADS, NTOK, parts=(0, QK))
        khT = carve(ring_r, LAT0 + HEADS * NTOK, HEADS, NKEY)
        vall = carve(ring_r, LAT0 + HEADS * (NTOK + NKEY), 6, GW)
        ckvT = carve(ring_r, LAT0 + HEADS * (NTOK + NKEY) + 6 * GW, NKEY)
        kdk = carve(ring_r, LAT0, 2, NT, GW)
        otok = carve(ring_r, LAT0 + 2 * NT * GW, NT, 2 * GW)
        osq = carve(ring_r, LAT0 + 4 * NT * GW, NT, 2 * GW)
        QT0 = room(NG * NTOK)
        cqT = carve(ring_r, QT0, NG, NTOK)
        qT = carve(ring_r, QT0, NG, NTOK)
        UV0 = room(2 * NG * NTOK)
        uT = carve(ring_r, UV0, NG, NTOK)
        vg = carve(ring_r, UV0 + NG * NTOK, NT, GW)
        prob = carve(ring_r, UV0, 2, NTOK)
        probT = carve(ring_r, UV0 + 2 * NTOK, 2, NTOK)
        sm = carve(ring_r, UV0, 2, 2, 2 * GW)
        GL0 = room(NG * CROW)
        glu = carve(ring_r, GL0, NG, CROW)
        csq = carve(ring_r, GL0, NG, NTOK)
        CA0 = room(NG * CVAL)
        cacc = carve(ring_r, CA0, NG, CVAL)
        zT = carve(ring_r, CA0, NG, NTOK)
        kvs = carve(ring_r, CA0, NT, 2, NG * NOPE)
        lat_sq = carve(ring_r, UV0, NT, QL + KL)
        rot_k = carve(ring_r, UV0 + NT * (QL + KL), TS, ROPE)
        rot_q = carve(ring_r, UV0, TS * HEADS, ROPE)
        CS0 = room(NG * NTOK)
        cscr = carve(ring_r, CS0, NG, NTOK)
        qdec = carve(ring_r, CS0, 2, NG, P)
        yct = carve(ring_r, CS0, NT, GW)
        KT0 = room(2 * NG * NTOK)
        kT = carve(ring_r, KT0, NG, NTOK)
        ktok = carve(ring_r, KT0 + NG * NTOK, NT, GW)
        qtok = carve(ring_r, KT0, NT, HEADS * QK)
        RV0 = room(3 * NT * GW)
        rv = carve(ring_r, RV0, NT, GW)
        gates = carve(ring_r, RV0 + NT * GW, 2, NT, GW)
        g1b = carve(h_r, 0, 2, D)
        qTd = carve(h_r, 2 * D, 2, NG, SAMPLE)
        otmp = carve(h_r, 2 * D, TS * GW)
        otmp_p = carve(h_r, 2 * D + TS * GW, GW)
        sret = carve(h_r, 2 * D + 2 * NG * SAMPLE, TS, 2, NG, NOPE)
        masks = carve(ring_r, GL0, 2, 2, NG * P)
        Afull, Bfull = carve(h_r, 0, KD, SLOTS), carve(h_r, KD * SLOTS, KD, SLOTS)
        g2b = carve(h_r, 2 * KD * SLOTS, D)
        ye = carve(h_r, 2 * KD * SLOTS + D, D)
        hmT = carve(h_r, 2 * KD * SLOTS + 2 * D, KF, SLOTS)
        work = carve(h_r, 2 * KD * SLOTS + 2 * D, NTOK, parts=(0, EXPERTS))
        S = carve(par_r, KEPT, NT, SLOTS)
        G = carve(par_r, KEPT + NT * SLOTS, NTOK)
        xeT = carve(par_r, KEPT + NT * SLOTS + NTOK, KD, SLOTS)
        cum = carve(par_r, KEPT + NT * SLOTS + NTOK, NTOK, parts=(0, EXPERTS))
        hm = carve(par_r, KEPT + NT * SLOTS + NTOK + KD * SLOTS, FF)
        assert KEPT + NT * SLOTS + NTOK + KD * SLOTS + FF <= NPARAM
        slotT = carve(h_r, 2 * KD * SLOTS + 2 * D + KF * SLOTS, NT, EXPERTS)
        aff = carve(h_r, 2 * KD * SLOTS + 2 * D + KF * SLOTS + NT * EXPERTS, NT, EXPERTS)

        psW = ctx.enter_context(nc.psum_tensor("wide", [P, 2, 1024], F32))[:, :, :]
        psT = ctx.enter_context(nc.psum_tensor("turned", [P, 2, 512], F32))[:, :, :]
        psN = ctx.enter_context(nc.psum_tensor("narrow", [P, 2, 512], F32))[:, :, :]

        W = Jobs(W_JOBS, 0, 0, sem("wide_done"), [sem("wide_out0"), sem("wide_out1")])
        T = Jobs(T_JOBS, T_MOE, T_EXPERT, sem("turned_done"), [sem("turned_out0"), sem("turned_out1")])
        N = Jobs(N_JOBS, 0, 0, sem("narrow_done"), [sem("narrow_out0"), sem("narrow_out1")])
        s_consts, s_x, s_cond = sem("consts_landed"), sem("x_landed"), sem("cond_landed")
        s_params = sem("params_landed")
        s_unit = [sem(f"unit_landed{i}") for i in range(NSTREAM)]
        s_slot = [sem(f"slot_landed{i}") for i in range(RING)]
        s_gu_used, s_dn_used = sem("gateup_used"), sem("down_used")
        s_cond_ready, s_passed = sem("cond_ready"), sem("waits_passed")
        s_dve = sem("vector_step")
        s_mixed = sem("spatial_out")
        s_sq, s_std, s_xn, s_scale = sem("squares_ready"), sem("std_ready"), sem("xn_ready"), sem("scale_ready")
        s_mss, s_mstd, s_lat, s_qrot = sem("latent_squares"), sem("latent_std"), sem("latents_ready"), sem("queries_rotated")
        s_ctx_out = sem("ctx_stored")
        s_pads, s_sig, s_conv, s_csq = sem("pads_ready"), sem("conv_gate"), sem("conv_ready"), sem("conv_squares")
        s_cstd, s_crs, s_zin, s_z = sem("conv_std"), sem("conv_rstd"), sem("conv_normed"), sem("conv_silu")
        s_vss, s_vstd, s_vn = sem("spatial_squares"), sem("spatial_std"), sem("spatial_normed")
        s_nmax = sem("score_max")
        s_dec, s_dexp, s_dlog, s_lg = sem("decay_in"), sem("decay_exp"), sem("decay_log"), sem("log_decay")
        s_tab, s_msk = sem("decay_tables"), sem("masks_ready")
        s_kdk, s_qtd, s_sret = sem("k_decayed"), sem("q_decayed"), sem("states_ready")
        s_ocen, s_osq, s_ovar, s_ostd, s_yc = sem("ret_centred"), sem("ret_squares"), sem("ret_var"), sem("ret_std"), sem("ret_out")
        s_res, s_st_out = sem("residual_added"), sem("state_stored")
        s_lexp, s_aff = sem("logit_exp"), sem("affinity_ready")
        s_slotcode, s_full = sem("slotcode_ready"), sem("affine_ready")
        s_S, s_xe, s_silu, s_hm, s_ye = sem("select_ready"), sem("gathered"), sem("silu_ready"), sem("hidden_ready"), sem("expert_out")
        s_y, s_ystored, s_fg = sem("y_ready"), sem("y_stored"), sem("final_gain_landed")

        RINGS = ((W, W_JOBS), (T, T_JOBS), (N, N_JOBS))

        def bank(R, job, rows=P):
            return {id(W): psW, id(T): psT, id(N): psN}[id(R)][0:rows, R.buf(job), :]

        mod_h = io["w_mod"].rearrange("l (k p) n -> l p k n", p=P)
        in_h = io["w_in"].rearrange("l (k p) n -> l p k n", p=P)
        out_h = io["w_out"].rearrange("l (k p) n -> l p k n", p=P)
        down_h = io["w_down"].rearrange("l e (k p) n -> l e p k n", p=P)

        block = ctx.enter_context(nc.Block())

        def settle(eng):
            eng.sem_inc(s_passed, 1)

        @block.sync
        def _(sp):
            for R, _jobs in RINGS:
                R.start(sp)
            for s in (s_silu, s_hm, s_ye):
                sp.sem_inc(s, START)
            sp.dma_start(sT.rearrange("p k s -> p (k s)"), io["cond"]).then_inc(s_cond, 16)
            sp.dma_start(con_r, io["consts"]).then_inc(s_consts, 16)
            sp.dma_start(x[:, 0:TS, :], io["x_sample"][0].rearrange("(t p) d -> p t d", p=P)).then_inc(s_x, 16)
            sp.dma_start(x[:, CTX, :], io["x_prompt"][0]).then_inc(s_x, 16)

            sp.wait_ge(s_consts, 16)

            def load_unit(l, n):
                kind, which = UNITS[n]
                if n < NSTREAM:
                    W.layers_done(sp, l)
                else:
                    before = UNITS[n - NSTREAM]
                    (N if before[0] == "mod" else W).wait(sp, l, LAST_JOB[before])
                settle(sp)
                lo = {"mod": lambda: which * GW, "out": lambda: which * GW, "in": lambda: IN_AT[which]}[kind]()
                w = MLA_B if which == "mla_b" else GW
                src = {"mod": mod_h, "in": in_h, "out": out_h}[kind][bass.ds(l, 1), :, :, lo:lo + w]
                sp.dma_start(stream[:, n % NSTREAM, :, 0:w], src.rearrange("l p k n -> (l p) k n")).then_inc(s_unit[n % NSTREAM], 16)

            def load_gateup(l, e, k):
                for i, w in enumerate(("w_gate", "w_up")):
                    src = io[w][bass.ds(l, 1), bass.ds(e, 1), k * P:(k + 1) * P, :]
                    sp.dma_start(ring[:, k, i, :], src.rearrange("l e p n -> (l e p) n")).then_inc(s_slot[k], 16)

            def load_down(l, e, j):
                src = down_h[bass.ds(l, 1), bass.ds(e, 1), :, 2 * j:2 * j + 2, :]
                sp.dma_start(ring[:, KD + j, :, :], src.rearrange("l e p k n -> (l e p) k n")).then_inc(s_slot[KD + j], 16)

            with sp.Fori(0, DEPTH) as l:
                for n in range(NSTREAM):
                    load_unit(l, n)
                T.layers_taken(sp, l)
                settle(sp)
                sp.dma_start(par_r, io["params"][bass.ds(l, 1)].rearrange("l p n -> (l p) n")).then_inc(s_params, 16)
                for n in range(NSTREAM, NUNIT):
                    load_unit(l, n)
                W.wait(sp, l, "o.0.s")
                sp.wait_ge(s_ctx_out, 32 * l + 32)
                sp.wait_ge(s_st_out, 32 * l + 32)
                settle(sp)
                for k in range(KD):
                    load_gateup(l, 0, k)
                for j in range(4):
                    load_down(l, 0, j)
                with sp.Fori(1, EXPERTS) as e:
                    for k in range(KD):
                        sp.wait_ge(s_gu_used, (l * EXPERTS + e) * KD + k - (KD - 1))
                        settle(sp)
                        load_gateup(l, e, k)
                    for j in range(4):
                        sp.wait_ge(s_dn_used, (l * EXPERTS + e) * 4 + j - 3)
                        settle(sp)
                        load_down(l, e, j)
            W.layers_done(sp, DEPTH)
            sp.dma_start(stream_r[:, 0:D], io["final_g"].partition_broadcast(P)).then_inc(s_fg, 16)
            sp.wait_ge(s_y, NT)
            sp.dma_start(io["y_sample"][0].rearrange("(t p) d -> p t d", p=P), xn[:, 0:TS, :]).then_inc(s_ystored, 16)
            sp.dma_start(io["y_prompt"][0], xn[:, CTX, :]).then_inc(s_ystored, 16)
            sp.wait_ge(s_ystored, 32)

        @block.tensor
        def _(pe):
            mm = nc.tensor.matmul
            unit_no = [0]

            def next_unit(l):
                n = unit_no[0]
                unit_no[0] += 1
                pe.wait_ge(s_unit[n % NSTREAM], (l * (NUNIT // NSTREAM) + n // NSTREAM + 1) * 16)
                return stream[:, n % NSTREAM, :, :]

            def mod_unit(l, u):
                job = f"mod.{u}"
                w = next_unit(l)
                N.claim(pe, l, job)
                for c in range(NG):
                    for k in range(KD):
                        ins = mm(psN[:, N.buf(job), 2 * c:2 * c + 2], w[:, k, c * P:(c + 1) * P], sT[:, k, :], start=(k == 0), stop=(k == KD - 1))
                N.finish(ins)

            def transposes(l, job, outs_ins):
                T.claim(pe, l, job)
                settle(pe)
                for o, i in outs_ins:
                    ins = nc.tensor.transpose(o, i, ident[0:i.shape[0], 0:i.shape[0]])
                T.finish(ins)

            def norm(l, which):
                for k in range(KD):
                    job = f"{which}.{k}"
                    if k == 0:
                        pe.wait_ge(s_xn, l * 2 * NT + (NT if which == "norm2" else 0) + TS)
                    o = bank(T, job)
                    transposes(l, job, [(o[:, t * P:(t + 1) * P], xn[:, t, k * P:(k + 1) * P]) for t in range(TS)])
                for i in range(2):
                    job = f"{which}.{KD + i}"
                    if i == 0:
                        pe.wait_ge(s_xn, l * 2 * NT + (NT if which == "norm2" else 0) + NT)
                    o = bank(T, job)
                    transposes(l, job, [(o[:, j * P:(j + 1) * P], xn[:, CTX, (4 * i + j) * P:(4 * i + j + 1) * P]) for j in range(4)])

            def feature_major(l, g):
                w = next_unit(l)
                for c in range(NG):
                    job = f"{g}.{c}"
                    W.claim(pe, l, job)
                    o = bank(W, job)
                    for lo, hi in ((SAMPLE, NTOK), (0, SAMPLE)):
                        for k in range(KD):
                            ins = mm(o[:, lo:hi], w[:, k, c * P:(c + 1) * P], hT[:, k, lo:hi], start=(k == 0), stop=(k == KD - 1))
                    W.finish(ins)

            def token_major(l, g, width=GW, src=hT, jobs=None):
                w = next_unit(l)
                for job, tiles in (jobs or ((f"{g}.s", range(TS)), (f"{g}.p", [CTX]))):
                    W.claim(pe, l, job)
                    o = bank(W, job)
                    for n, t in enumerate(tiles):
                        for k in range(KD):
                            ins = mm(o[:, n * width:(n + 1) * width], src[:, k, t * P:(t + 1) * P], w[:, k, 0:width], start=(k == 0), stop=(k == KD - 1))
                    W.finish(ins)

            def latents(l):
                pe.wait_ge(s_lat, l + 1)
                for c, n in ((0, P), (1, QL - P)):
                    o = bank(T, f"cq.{c}", n)
                    transposes(l, f"cq.{c}", [(o[:, t * P:(t + 1) * P], mla[:, t, c * P:c * P + n]) for t in range(TS)])
                o = bank(T, "cq.p")
                transposes(l, "cq.p", [(o[0:n, c * P:(c + 1) * P], mla[:, CTX, c * P:c * P + n]) for c, n in ((0, P), (1, QL - P))])
                cache = par("cache")
                rows = [ctxt[:, t, :] for t in range(TS)] + [cache, ctxt[:, CTX, :]]
                for name, lo, m in (("ckv", 0, KL), ("kpe", KL + ROPE - QK, QK)):
                    o = bank(T, f"{name}.0", m)
                    transposes(l, f"{name}.0", [(o[:, t * P:(t + 1) * P], rows[t][:, lo:lo + m]) for t in range(TS)])
                    o = bank(T, f"{name}.1", m)
                    transposes(l, f"{name}.1", [(o[:, t * P:(t + 1) * P], rows[TS + t][:, lo:lo + m]) for t in range(2)])

            def mla_q(l):
                wuq = par("wuq", 2, HEADS * QK)
                T.taken(pe, l, "cq.p")
                T.taken(pe, l, "cq.1")
                for j, tiles in enumerate(((0, 1), (2, 3), (4,))):
                    W.claim(pe, l, f"q.{j}")
                    o = bank(W, f"q.{j}")
                    for n, t in enumerate(tiles):
                        mm(o[:, n * 512:n * 512 + HEADS * QK], cqT[:, 0, t * P:(t + 1) * P], wuq[:, 0, :], start=True, stop=False)
                        ins = mm(o[:, n * 512:n * 512 + HEADS * QK], cqT[0:QL - P, 1, t * P:(t + 1) * P], wuq[0:QL - P, 1, :], start=False, stop=True)
                    W.finish(ins)

            def turn_q(l):
                pe.wait_ge(s_qrot, l + 1)
                W.taken(pe, l, "q.2")
                for h in range(HEADS):
                    o = bank(T, f"qh.{h}", QK)
                    transposes(l, f"qh.{h}", [(o[:, t * P:(t + 1) * P], qtok[:, t, h * QK:(h + 1) * QK]) for t in range(TS)])
                o = bank(T, "qh.p", QK)
                transposes(l, "qh.p", [(o[:, h * P:(h + 1) * P], qtok[:, CTX, h * QK:(h + 1) * QK]) for h in range(HEADS)])

            def mla_kv(l):
                wukv = par("wukv", HEADS, 2, NOPE)
                T.taken(pe, l, "ckv.0")
                T.taken(pe, l, "ckv.1")
                for h in range(HEADS):
                    W.claim(pe, l, f"kh.{h}")
                    o = bank(W, f"kh.{h}", NOPE)
                    mm(o[:, 0:512], wukv[:, h, 0, :], ckvT[:, 0:512], start=True, stop=True)
                    W.finish(mm(o[:, 512:NKEY], wukv[:, h, 0, :], ckvT[:, 512:NKEY], start=True, stop=True))
                for j, tiles in enumerate(((0, 1, 2, 3), (4, 5))):
                    W.claim(pe, l, f"v.{j}")
                    o = bank(W, f"v.{j}")
                    for n, t in enumerate(tiles):
                        ins = mm(o[:, n * GW:(n + 1) * GW].rearrange("p (h d) -> p h d", h=HEADS), ckvT[:, t * P:(t + 1) * P], wukv[:, :, 1, :], start=True, stop=True)
                    W.finish(ins)

            def mix(l):
                sgw = par("sgw", HEADS, P)
                pe.wait_ge(s_vn, l + 1)
                for c in range(NG):
                    W.claim(pe, l, f"mix.{c}")
                    o = bank(W, f"mix.{c}")
                    for t in range(NT):
                        for half in range(2):
                            h = 2 * c + half
                            ins = mm(o[half * 64:half * 64 + 64, t * P:(t + 1) * P], vg[:, t, h * 64:(h + 1) * 64], sgw[:, h, :], start=True, stop=True)
                    W.finish(ins)

            def conv_mean(l):
                pe.wait_ge(s_conv, l + 1)
                W.claim(pe, l, "mean")
                o = bank(W, "mean")
                for dst, lo, n in ((0, 0, SAMPLE), (SAMPLE, CPROMPT, PROMPT)):
                    for c in range(NG):
                        ins = mm(o[:, dst:dst + n], mean_w, cacc[:, c, lo:lo + n], start=(c == 0), stop=(c == NG - 1))
                W.finish(ins)

            def conv_var(l):
                pe.wait_ge(s_csq, l + 1)
                N.claim(pe, l, "var")
                o = bank(N, "var")
                for t in range(NT):
                    for c in range(NG):
                        ins = mm(o[:, t:t + 1], csq[:, c, t * P:(t + 1) * P], mean_w[:, 0:1], start=(c == 0), stop=(c == NG - 1))
                N.finish(ins)
                pe.wait_ge(s_crs, l + 1)
                W.claim(pe, l, "cstd")
                o = bank(W, "cstd")
                for t in range(NT):
                    ins = mm(o[:, t * P:(t + 1) * P], crstd[:, t:t + 1].broadcast_to([P, P]), ident, start=True, stop=True)
                W.finish(ins)

            def conv_out(l):
                pw = par("pw", NG, GW)
                pe.wait_ge(s_z, 2 * l + 2)
                for c in range(NG):
                    W.claim(pe, l, f"pw.{c}")
                    o = bank(W, f"pw.{c}")
                    for lo, hi in ((0, SAMPLE), (SAMPLE, NTOK)):
                        for k in range(NG):
                            ins = mm(o[:, lo:hi], pw[:, k, c * P:(c + 1) * P], zT[:, k, lo:hi], start=(k == 0), stop=(k == NG - 1))
                    W.finish(ins)

            def scores(l, i):
                h, t = BLOCKS[i]
                job = f"s.{i}"
                if i == 0:
                    for j in ("qh.3", "qh.p"):
                        T.taken(pe, l, j)
                    for j in ("v.0", "v.1"):
                        W.taken(pe, l, j)
                W.claim(pe, l, job)
                o = bank(W, job)
                if h == "ctx":
                    for h in range(HEADS):
                        ins = mm(o[:, h * P:(h + 1) * P], qhT[:, h, CTX * P:NTOK], khT[0:QK, h, NKEY - P:NKEY], start=True, stop=True)
                else:
                    mm(o[:, 0:512], qhT[:, h, t * P:(t + 1) * P], khT[0:QK, h, 0:512], start=True, stop=True)
                    ins = mm(o[:, 512:640], qhT[:, h, t * P:(t + 1) * P], khT[0:QK, h, 512:640], start=True, stop=True)
                W.finish(ins)

            def turn_probs(l, i):
                pr = prob[:, i % 2, :]
                W.taken(pe, l, f"s.{i}")
                o = bank(T, f"pt.{i}")
                transposes(l, f"pt.{i}", [(o[:, j * P:(j + 1) * P], pr[:, j * P:(j + 1) * P]) for j in range(4)])
                if BLOCKS[i][0] != "ctx":
                    o = bank(T, f"pt.{i}b")
                    transposes(l, f"pt.{i}b", [(o[:, 0:P], pr[:, 4 * P:5 * P])])

            def weigh_values(l, i):
                h, t = BLOCKS[i]
                job = f"pv.{i}"
                T.taken(pe, l, f"pt.{i}")
                if h != "ctx":
                    T.taken(pe, l, f"pt.{i}b")
                N.claim(pe, l, job)
                o = bank(N, job)
                pt = probT[:, i % 2, :]
                if h == "ctx":
                    for h in range(HEADS):
                        ins = mm(o[:, h * 64:(h + 1) * 64], pt[:, h * P:(h + 1) * P], vall[:, 5, h * 64:(h + 1) * 64], start=True, stop=True)
                else:
                    for j in range(5):
                        ins = mm(o[:, 0:64], pt[:, j * P:(j + 1) * P], vall[:, j, h * 64:(h + 1) * 64], start=(j == 0), stop=(j == 4))
                N.finish(ins)

            def turn_rows(l, name, rows):
                for c in range(NG):
                    o = bank(T, f"{name}.{c}")
                    transposes(l, f"{name}.{c}", [(o[:, t * P:(t + 1) * P], rows[:, t, c * P:(c + 1) * P]) for t in range(TS)])
                o = bank(T, f"{name}.p")
                transposes(l, f"{name}.p", [(o[:, c * P:(c + 1) * P], rows[:, CTX, c * P:(c + 1) * P]) for c in range(NG)])

            def turn_k(l):
                W.taken(pe, l, "rk.0")
                W.taken(pe, l, "rk.1")
                for i in range(2):
                    o = bank(T, f"ktok.{i}")
                    transposes(l, f"ktok.{i}", [(o[:, (2 * n + c) * P:(2 * n + c + 1) * P], kT[:, c, (2 * i + n) * P:(2 * i + n + 1) * P])
                                                 for n in range(2) for c in range(NG)])
                o = bank(T, "ktok.p")
                transposes(l, "ktok.p", [(o[:, c * P:(c + 1) * P], kT[:, c, SAMPLE:NTOK]) for c in range(NG)])

            def rows_g1(l):
                N.taken(pe, l, "mod.10")
                N.taken(pe, l, "mod.11")
                for s, job in ((1, "g1.s"), (0, "g1.p")):
                    W.claim(pe, l, job)
                    o = bank(W, job)
                    for k in range(KD):
                        ins = mm(o[:, k * P:(k + 1) * P], modT[:, 2 * KD + k, s:s + 1].broadcast_to([P, P]), ident, start=True, stop=True)
                    W.finish(ins)

            def retention(l):
                pe.wait_ge(s_kdk, 2 * l + 2)
                W.taken(pe, l, "rv.s")
                W.taken(pe, l, "rv.p")
                for t in range(NT):
                    N.claim(pe, l, f"kv.{t}")
                    o = bank(N, f"kv.{t}")
                    dirs = [d for d in range(2) if t == CTX or (t < TS - 1 if d == 0 else t > 0)]
                    for d in dirs:
                        for c in range(NG):
                            for half in range(2):
                                h = 2 * c + half
                                at = (d * NG + c) * 64
                                ins = mm(o[half * 64:half * 64 + 64, at:at + 64], kdk[:, d, t, h * 64:(h + 1) * 64], rv[:, t, h * 64:(h + 1) * 64], start=True, stop=True)
                    N.finish(ins)

                def ret_scores(t):
                    W.claim(pe, l, f"rs.{t}")
                    o = bank(W, f"rs.{t}")
                    for half in range(2):
                        for c in range(NG):
                            p = slice(half * 64, half * 64 + 64)
                            ins = mm(o[:, half * 512 + c * P:half * 512 + (c + 1) * P], kT[p, c, t * P:(t + 1) * P], qT[p, c, t * P:(t + 1) * P], start=True, stop=True)
                    W.finish(ins)

                def ret_out(t):
                    W.taken(pe, l, f"rs.{t}")
                    if t == 0:
                        pe.wait_ge(s_qtd, 2 * l + 2)
                        pe.wait_ge(s_sret, l + 1)
                    W.claim(pe, l, f"ro.{t}")
                    o = bank(W, f"ro.{t}")
                    for half in range(2):
                        for d in range(2):
                            for c in range(NG):
                                h = 2 * c + half
                                p = slice(half * 64, half * 64 + 64)
                                out = o[:, half * 512 + (d * NG + c) * 64:half * 512 + (d * NG + c + 1) * 64]
                                ins = mm(out, sm[:, t % 2, d, half * GW + c * P:half * GW + (c + 1) * P], rv[:, t, h * 64:(h + 1) * 64], start=True, stop=(t == CTX))
                                if t != CTX:
                                    first = t == (0 if d == 0 else TS - 1)
                                    st = par("s0", 2, NG, NOPE)[p, d, c, :] if first else sret[p, t, d, c, :]
                                    ins = mm(out, qTd[p, d, c, t * P:(t + 1) * P], st, start=False, stop=True)
                    W.finish(ins)

                for t in range(NT):
                    ret_scores(t)
                    if t:
                        ret_out(t - 1)
                ret_out(NT - 1)
                pe.wait_ge(s_yc, l + 1)
                turn_rows(l, "yc", yct)

            def out_proj(l):
                for j in ("yc.1", "yc.p"):
                    T.taken(pe, l, j)
                pe.wait_ge(s_mixed, 2 * l + 2)
                for u in range(4):
                    token_major(l, None, src=yT, jobs=((f"o.{u}.s", range(TS)), (f"o.{u}.p", [CTX])))

            def router(l):
                rt = par("router", KD, EXPERTS)
                T.taken(pe, l, f"norm2.{KD}")
                T.taken(pe, l, f"norm2.{KD + 1}")
                N.claim(pe, l, "logits")
                o = bank(N, "logits")
                for t in range(NT):
                    for k in range(KD):
                        ins = mm(o[:, t * EXPERTS:(t + 1) * EXPERTS], hT[:, k, t * P:(t + 1) * P], rt[:, k, :], start=(k == 0), stop=(k == KD - 1))
                N.finish(ins)

            def choose(l):
                pe.wait_ge(s_aff, l + 1)
                o = bank(T, "afft.s", EXPERTS)
                transposes(l, "afft.s", [(o[:, t * P:(t + 1) * P], aff[:, t, :]) for t in range(TS)])
                o = bank(T, "afft.p", EXPERTS)
                transposes(l, "afft.p", [(o[:, 0:P], aff[:, CTX, :])])

            def turn_slots(l):
                pe.wait_ge(s_slotcode, 2 * l + 2)
                o = bank(T, "slots")
                transposes(l, "slots", [(o[:, t * EXPERTS:(t + 1) * EXPERTS], work[:, t * P:(t + 1) * P]) for t in range(NT)])

            def rows_g2(l):
                W.claim(pe, l, "g2")
                o = bank(W, "g2")
                for k in range(KD):
                    mm(o[0:CAPS, k * P:(k + 1) * P], modT[:, 5 * KD + k, 1:2].broadcast_to([P, CAPS]), ident, start=True, stop=True)
                    ins = mm(o[CAPS:SLOTS, k * P:(k + 1) * P], modT[:, 5 * KD + k, 0:1].broadcast_to([P, CAPP]), ident, start=True, stop=True)
                W.finish(ins)

            def gather(l, e, at, n):
                pe.wait_ge(s_S, n + 1)
                for i in range(2):
                    T.claim(pe, l, at + i, e)
                    o = bank(T, at + i)
                    for k in range(4):
                        for t in range(NT):
                            ins = mm(o[:, k * SLOTS:(k + 1) * SLOTS], xn[:, t, (4 * i + k) * P:(4 * i + k + 1) * P], S[:, t, :], start=(t == 0), stop=(t == NT - 1))
                    T.finish(ins)

            def turn_selection(l, e, at):
                T.claim(pe, l, at, e)
                o = bank(T, at, SLOTS)
                for t in range(TS):
                    ins = nc.tensor.transpose(o[:, t * P:(t + 1) * P], S[:, t, :], ident)
                T.finish(ins)
                T.claim(pe, l, at + 1, e)
                o = bank(T, at + 1, SLOTS)
                nc.tensor.transpose(o[:, 0:P], S[:, CTX, :], ident)
                for t in range(NT):
                    ins = mm(o[:, P:P + 1], S[:, t, :], affc[:, t:t + 1], start=(t == 0), stop=(t == NT - 1))
                T.finish(ins)

            def expert(l, e, n, last):
                pe.wait_ge(s_xe, 2 * n + 2)
                pe.wait_ge(s_silu, START + 2 * n)
                pe.wait_ge(s_hm, START + 2 * n)
                for k in range(KD):
                    pe.wait_ge(s_slot[k], (n + 1) * 32)
                    for i in range(2):
                        for half in range(2):
                            ins = mm(psW[0:SLOTS, i, half * 512:(half + 1) * 512], xeT[:, k, :], ring[:, k, i, half * 512:(half + 1) * 512], start=(k == 0), stop=(k == KD - 1))
                    ins.then_inc(s_gu_used, 1)
                at = FRONT
                if not last:
                    gather(l, e, at, n + 1)
                    at += 2
                for i in range(2):
                    pe.wait_ge(s_hm, START + 2 * n + i + 1)
                    T.claim(pe, l, at + i, e)
                    settle(pe)
                    o = bank(T, at + i)
                    for k in range(4):
                        ins = nc.tensor.transpose(o[:, k * SLOTS:(k + 1) * SLOTS], hm[0:SLOTS, (4 * i + k) * P:(4 * i + k + 1) * P], ident[0:SLOTS, 0:SLOTS])
                    T.finish(ins)
                pe.wait_ge(s_ye, START + 2 * n)
                for i in range(2):
                    T.taken(pe, l, at + i, e)
                at += 2
                for j in range(4):
                    pe.wait_ge(s_slot[KD + j], (n + 1) * 16)
                    for i in range(2):
                        k = 2 * j + i
                        for half in range(2):
                            ins = mm(psN[0:SLOTS, half, :], hmT[:, k, :], ring[:, KD + j, i, half * 512:(half + 1) * 512], start=(k == 0), stop=(k == KF - 1))
                    ins.then_inc(s_dn_used, 1)
                for i in (2, 3):
                    T.taken(pe, l, i, e)
                for j in range(COMBINE):
                    half, t = divmod(j, NT)
                    if t == 0:
                        pe.wait_ge(s_ye, START + 2 * n + half + 1)
                    T.claim(pe, l, at + j, e)
                    T.finish(mm(bank(T, at + j), G[0:SLOTS, t * P:(t + 1) * P], ye[0:SLOTS, half * 512:(half + 1) * 512], start=True, stop=True))
                if not last:
                    turn_selection(l, e, at + COMBINE)

            pe.wait_ge(s_consts, 16)
            pe.wait_ge(s_cond_ready, 1)
            with pe.Fori(0, DEPTH) as l:
                unit_no[0] = 0
                for s in STEPS:
                    kind, _, arg = s.partition(":")
                    if kind == "mod":
                        for u in range(*map(int, arg.split("-"))):
                            mod_unit(l, u)
                            if u == 8:
                                pe.wait_ge(s_params, 16 * l + 16)
                    elif kind in ("norm1", "norm2"):
                        norm(l, kind)
                    elif kind == "in":
                        if arg == "mla":
                            for k in range(KD + 2):
                                T.taken(pe, l, f"norm1.{k}") if k >= KD else None
                            token_major(l, None, jobs=(("mla_a.s", range(TS)), ("mla_a.p", [CTX])))
                            token_major(l, None, width=MLA_B, jobs=(("mla_b", range(NT)),))
                        elif arg in TOKEN_MAJOR:
                            token_major(l, arg)
                        else:
                            feature_major(l, arg)
                        if arg == "rk":
                            turn_k(l)
                    elif kind == "latents":
                        latents(l)
                    elif kind == "mla_q":
                        mla_q(l)
                    elif kind == "mla_kv":
                        mla_kv(l)
                        turn_q(l)
                    elif kind == "mix":
                        mix(l)
                    elif kind == "conv_mean":
                        conv_mean(l)
                    elif kind == "conv_var":
                        conv_var(l)
                    elif kind == "conv_out":
                        conv_out(l)
                    elif kind == "att":
                        i = int(arg)
                        scores(l, i)
                        if i:
                            turn_probs(l, i - 1)
                            weigh_values(l, i - 1)
                    elif kind == "att_end":
                        turn_probs(l, len(BLOCKS) - 1)
                        weigh_values(l, len(BLOCKS) - 1)
                        N.taken(pe, l, f"pv.{len(BLOCKS) - 1}")
                        N.taken(pe, l, f"pv.{len(BLOCKS) - 2}")
                        turn_rows(l, "yd", ydt)
                    elif kind == "rows_g1":
                        rows_g1(l)
                    elif kind == "retention":
                        retention(l)
                    elif kind == "out_proj":
                        out_proj(l)
                    elif kind == "router":
                        router(l)
                    elif kind == "rows_g2":
                        rows_g2(l)
                        choose(l)
                        turn_slots(l)
                for R, jobs in RINGS:
                    if "spare" in R.at:
                        R.claim(pe, l, "spare")
                        R.finish(mm(bank(R, "spare")[:, 0:2], ident, ident[:, 0:2], start=True, stop=True))
                n0 = l * EXPERTS
                gather(l, 0, 0, n0)
                turn_selection(l, 0, 2)
                with pe.Fori(0, EXPERTS - 1) as e:
                    expert(l, e, n0 + e, False)
                expert(l, EXPERTS - 1, n0 + EXPERTS - 1, True)

        @block.scalar
        def _(act):
            A = nc.scalar.activation
            def out(R, l, job, dst, src, func=ACT.Identity, **kw):
                R.wait(act, l, job)
                R.take(A(dst, src, func, **kw), job)

            def norm_squares(n):
                for t in range(NT):
                    ins = A(xn[:, t, :], x[:, t, :], ACT.Square, accum_out=ss[:, t:t + 1])
                ins.then_inc(s_sq, 1)
                act.wait_ge(s_sq, n + 1)
                A(std, ss, ACT.Sqrt, scale=1.0 / D, bias=con("eps")).then_inc(s_std, 1)

            def norm_out(l, which, scale, shift):
                act.wait_ge(s_scale, 2 * l + (2 if which == "norm2" else 1))
                for k in range(0, KD, 2):
                    out(T, l, f"{which}.{k}", hT[:, k, 0:SAMPLE], bank(T, f"{which}.{k}"), scale=scale[:, k, 1:2], bias=shift[:, k, 1:2])
                job = f"{which}.{KD}"
                T.wait(act, l, job)
                for k in range(4):
                    ins = A(hT[:, k, SAMPLE:NTOK], bank(T, job)[:, k * P:(k + 1) * P], ACT.Identity, scale=scale[:, k, 0:1], bias=shift[:, k, 0:1])
                T.take(ins, job)

            def mod_out(l, u):
                job = f"mod.{u}"
                N.wait(act, l, job)
                for c in range(NG):
                    j = NG * u + c
                    ins = A(modT[:, j, :], bank(N, job)[:, 2 * c:2 * c + 2], ACT.Identity, bias=par("bmod")[:, j:j + 1])
                N.take(ins, job)

            def rows_out(l, g, dst, func=ACT.Identity):
                out(W, l, f"{g}.s", dst[:, 0:TS, :], bank(W, f"{g}.s").rearrange("p (t n) -> p t n", t=TS), func)
                out(W, l, f"{g}.p", dst[:, CTX, :], bank(W, f"{g}.p")[:, 0:GW], func)

            def turned_rows_out(l, name, chunk, gain=None):
                for c in range(NG):
                    kw = {} if gain is None else dict(scale=gain[:, c:c + 1])
                    out(T, l, f"{name}.{c}", yT[:, chunk + c, 0:SAMPLE], bank(T, f"{name}.{c}"), **kw)
                T.wait(act, l, f"{name}.p")
                for c in range(NG):
                    kw = {} if gain is None else dict(scale=gain[:, c:c + 1])
                    ins = A(yT[:, chunk + c, SAMPLE:NTOK], bank(T, f"{name}.p")[:, c * P:(c + 1) * P], ACT.Identity, **kw)
                T.take(ins, f"{name}.p")

            def decays(l):
                A(lgt[:, 0, :], par("dec"), ACT.Exp, scale=float(np.log(2.0))).then_inc(s_dexp, 1)
                act.wait_ge(s_dec, l + 1)
                A(lgt[:, 4, :], lgt[:, 1, :], ACT.Ln).then_inc(s_dlog, 1)

            def ret_tables(l):
                act.wait_ge(s_lg, l + 1)
                lg = lgt[:, 5, :]
                A(kd, kd, ACT.Exp)
                A(cdec.rearrange("p a b -> p (a b)"), lg[:, 8:12], ACT.Exp, scale=float(P))
                for d in range(2):
                    for c in range(NG):
                        for half in range(2):
                            h = 2 * c + half
                            A(masks[:, d, half, c * P:(c + 1) * P], con("expo", 2, P)[:, d, :], ACT.Exp, scale=lg[:, d * HEADS + h:d * HEADS + h + 1])
                        ins = A(qdec[:, d, c, :], con("qpos", 2, P)[:, d, :], ACT.Exp, scale=lg[:, 8 + NG * d + c:9 + NG * d + c])
                ins.then_inc(s_tab, 1)

            def softmax_exp(l, i):
                h, t = BLOCKS[i]
                job = f"s.{i}"
                act.wait_ge(s_nmax, l * len(BLOCKS) + i + 1)
                if i >= 2:
                    T.wait(act, l, f"pt.{i - 2}b")
                o = bank(W, job)
                if h == "ctx":
                    for h in range(HEADS):
                        ins = A(prob[:, i % 2, h * P:(h + 1) * P], o[:, h * P:(h + 1) * P], ACT.Exp, scale=ATT_SCALE, bias=nmax[:, i % 2, h:h + 1], accum_out=rsum[:, i % 2, h:h + 1])
                else:
                    ins = A(prob[:, i % 2, :], o[:, 0:NTOK], ACT.Exp, scale=ATT_SCALE, bias=nmax[:, i % 2, 0:1], accum_out=rsum[:, i % 2, 0:1])
                W.take(ins, job)

            def last_prob_out(l, i):
                if BLOCKS[i][0] == "ctx":
                    return
                if i >= 2:
                    N.wait(act, l, f"pv.{i - 2}")
                out(T, l, f"pt.{i}b", probT[:, i % 2, 4 * P:5 * P], bank(T, f"pt.{i}b")[:, 0:P])

            act.wait_ge(s_cond, 16)
            A(sT.rearrange("p k s -> p (k s)"), sT.rearrange("p k s -> p (k s)"), ACT.Silu).then_inc(s_cond_ready, 1)
            act.wait_ge(s_consts, 16)
            act.wait_ge(s_x, 32)
            with act.Fori(0, DEPTH) as l:
                T.layers_taken(act, l)
                norm_squares(2 * l)
                act.wait_ge(s_params, 16 * l + 16)
                decays(l)
                for s in STEPS:
                    kind, _, arg = s.partition(":")
                    if kind == "mod":
                        for u in range(*map(int, arg.split("-"))):
                            mod_out(l, u)
                    elif kind == "norm1":
                        norm_out(l, "norm1", A1, modT[:, 0:KD, :])
                    elif kind == "in":
                        if arg == "mla":
                            out(W, l, "mla_a.s", mla[:, 0:TS, 0:GW], bank(W, "mla_a.s").rearrange("p (t n) -> p t n", t=TS))
                            out(W, l, "mla_a.p", mla[:, CTX, 0:GW], bank(W, "mla_a.p")[:, 0:GW])
                            out(W, l, "mla_b", mla[:, :, GW:MLA_IN], bank(W, "mla_b")[:, 0:NT * MLA_B].rearrange("p (t n) -> p t n", t=NT))
                        elif arg == "ca":
                            for c in range(NG):
                                job = f"ca.{c}"
                                W.wait(act, l, job)
                                A(glu[:, c, PAD:PAD + SAMPLE], bank(W, job)[:, 0:SAMPLE], ACT.Identity)
                                W.take(A(glu[:, c, CPROMPT + PAD:CPROMPT + PAD + PROMPT], bank(W, job)[:, SAMPLE:NTOK], ACT.Identity), job)
                        elif arg == "cg":
                            for c in range(NG):
                                out(W, l, f"cg.{c}", cscr[:, c, :], bank(W, f"cg.{c}")[:, 0:NTOK], ACT.Sigmoid)
                        elif arg in ("u", "rq", "rk"):
                            dst = dict(u=uT, rq=qT, rk=kT)[arg]
                            for c in range(NG):
                                out(W, l, f"{arg}.{c}", dst[:, c, :], bank(W, f"{arg}.{c}")[:, 0:NTOK])
                            if arg == "rk":
                                for i in range(2):
                                    out(T, l, f"ktok.{i}", ktok[:, 2 * i:2 * i + 2, :], bank(T, f"ktok.{i}").rearrange("p (t n) -> p t n", t=2))
                                out(T, l, "ktok.p", ktok[:, CTX, :], bank(T, "ktok.p")[:, 0:GW])
                        elif arg == "vg":
                            rows_out(l, "vg", vg)
                            act.wait_ge(s_vss, l + 1)
                            A(vstd, vss, ACT.Sqrt, scale=1.0 / GW, bias=con("eps")).then_inc(s_vstd, 1)
                        elif arg == "rv":
                            rows_out(l, "rv", rv)
                        elif arg in ("rgf", "rgb"):
                            rows_out(l, arg, gates[:, int(arg == "rgb")], ACT.Silu)
                        if arg == "mla":
                            act.wait_ge(s_mss, l + 1)
                            A(mstd[:, 0, :], mss[:, 0, :], ACT.Sqrt, scale=1.0 / QL, bias=con("eps"))
                            A(mstd[:, 1, :], mss[:, 1, :], ACT.Sqrt, scale=1.0 / KL, bias=con("eps")).then_inc(s_mstd, 1)
                    elif kind == "latents":
                        act.wait_ge(s_lat, l + 1)
                        act.dma_start(io["new_ckv"][0, bass.ds(l, 1)].rearrange("l p n -> (l p) n"), ctxt[:, CTX, 0:KL]).then_inc(s_ctx_out, 16)
                        act.dma_start(io["new_kpe"][0, bass.ds(l, 1)].rearrange("l p n -> (l p) n"), ctxt[:, CTX, KL:KL + ROPE]).then_inc(s_ctx_out, 16)
                        out(T, l, "cq.0", cqT[:, 0, 0:SAMPLE], bank(T, "cq.0"))
                        out(T, l, "cq.1", cqT[0:QL - P, 1, 0:SAMPLE], bank(T, "cq.1", QL - P))
                        T.wait(act, l, "cq.p")
                        A(cqT[:, 0, SAMPLE:NTOK], bank(T, "cq.p")[:, 0:P], ACT.Identity)
                        T.take(A(cqT[0:QL - P, 1, SAMPLE:NTOK], bank(T, "cq.p", QL - P)[:, P:2 * P], ACT.Identity), "cq.p")
                        out(T, l, "ckv.0", ckvT[:, 0:512], bank(T, "ckv.0"))
                        out(T, l, "ckv.1", ckvT[:, 512:NKEY], bank(T, "ckv.1")[:, 0:NKEY - 512])
                        for i, (lo, hi) in enumerate(((0, 512), (512, NKEY))):
                            src = bank(T, f"kpe.{i}")[NOPE:QK, 0:hi - lo].unsqueeze(1).broadcast_to([ROPE, HEADS, hi - lo])
                            out(T, l, f"kpe.{i}", khT[NOPE:QK, :, lo:hi], src)
                    elif kind == "mla_q":
                        for j, n in enumerate((2, 2, 1)):
                            src = bank(W, f"q.{j}").rearrange("p (t n) -> p t n", t=2)[:, 0:n, 0:HEADS * QK]
                            out(W, l, f"q.{j}", qtok[:, 2 * j:2 * j + n, :], src)
                    elif kind == "mla_kv":
                        for h in range(HEADS):
                            out(W, l, f"kh.{h}", khT[0:NOPE, h, :], bank(W, f"kh.{h}", NOPE)[:, 0:NKEY])
                        for j, n in enumerate((4, 2)):
                            out(W, l, f"v.{j}", vall[:, 4 * j:4 * j + n, :], bank(W, f"v.{j}")[:, 0:n * GW].rearrange("p (t n) -> p t n", t=n))
                        for h in range(HEADS):
                            out(T, l, f"qh.{h}", qhT[:, h, 0:SAMPLE], bank(T, f"qh.{h}", QK))
                        out(T, l, "qh.p", qhT[:, :, SAMPLE:NTOK], bank(T, "qh.p", QK).rearrange("p (h n) -> p h n", h=HEADS))
                    elif kind == "conv_mean":
                        W.taken(act, l, "mean")
                        A(csq, cscr, ACT.Square).then_inc(s_csq, 1)
                    elif kind == "conv_var":
                        out(N, l, "var", cstd, bank(N, "var")[:, 0:NT], ACT.Sqrt, bias=con("eps"))
                        W.taken(act, l, "cstd")
                        for c in range(NG):
                            A(zT[:, c, :], cscr[:, c, :], ACT.Silu, scale=par("lng")[:, c:c + 1], bias=par("lnb")[:, c:c + 1]).then_inc(s_z, 1)
                    elif kind == "conv_out":
                        for c in range(NG):
                            out(W, l, f"pw.{c}", yT[:, NG + c, :], bank(W, f"pw.{c}")[:, 0:NTOK])
                    elif kind == "ret_tables":
                        ret_tables(l)
                    elif kind == "att":
                        i = int(arg)
                        softmax_exp(l, i)
                        if i:
                            last_prob_out(l, i - 1)
                    elif kind == "att_end":
                        turned_rows_out(l, "yd", 3 * NG)
                    elif kind == "rows_g1":
                        for s_, job in ((1, "g1.s"), (0, "g1.p")):
                            out(W, l, job, g1b[:, s_, :], bank(W, job))
                    elif kind == "retention":
                        for t in range(NT):
                            out(N, l, f"kv.{t}", kvs[:, t], bank(N, f"kv.{t}")[:, 0:2 * NG * NOPE].rearrange("p (d n) -> p d n", d=2)) if t == CTX else None
                            if t != CTX:
                                N.wait(act, l, f"kv.{t}")
                                ds_ = [d for d in range(2) if (t < TS - 1 if d == 0 else t > 0)]
                                lo, hi = ds_[0] * NG * NOPE, (ds_[-1] + 1) * NG * NOPE
                                N.take(A(kvs[:, t].rearrange("p d n -> p (d n)")[:, lo:hi], bank(N, f"kv.{t}")[:, lo:hi], ACT.Identity), f"kv.{t}")
                        N.taken(act, l, f"kv.{CTX}")
                        for d in range(2):
                            dst = io["new_state"][0, bass.ds(l, 1), d].rearrange("l (c f) k e -> (l f k) c e", f=2)
                            act.dma_start(dst, kvs[:, CTX, d].rearrange("p (c e) -> p c e", c=NG)).then_inc(s_st_out, 16)
                        for t in range(NT):
                            out(W, l, f"ro.{t}", otok[:, t, :].rearrange("p (f n) -> p f n", f=2), bank(W, f"ro.{t}").rearrange("p (f n) -> p f n", f=2)[:, :, 0:2 * NG * NOPE])
                            act.wait_ge(s_ocen, l * NT + t + 1)
                            A(osq[:, t, :], otok[:, t, :], ACT.Square).then_inc(s_osq, 1)
                        act.wait_ge(s_ovar, l + 1)
                        A(rdev, rvar, ACT.Sqrt, scale=1.0 / NOPE, bias=con("eps")).then_inc(s_ostd, 1)
                        turned_rows_out(l, "yc", 2 * NG, par("gng"))
                    elif kind == "norm2":
                        act.wait_ge(s_res, 8 * l + 8)
                        norm_squares(2 * l + 1)
                        norm_out(l, "norm2", A2, modT[:, 3 * KD:4 * KD, :])
                    elif kind == "router":
                        N.taken(act, l, "logits")
                        A(aff, aff, ACT.Exp).then_inc(s_lexp, 1)
                    elif kind == "rows_g2":
                        out(W, l, "g2", g2b[0:SLOTS, :], bank(W, "g2", SLOTS))
                        out(T, l, "slots", slotT, bank(T, "slots")[:, 0:NT * EXPERTS].rearrange("p (t e) -> p t e", t=NT))
                for R, jobs in RINGS:
                    if "spare" in R.at:
                        out(R, l, "spare", spare, bank(R, "spare")[:, 0:2])

                def selection_out(e, at):
                    out2(e, at, G[0:SLOTS, 0:SAMPLE], bank(T, at, SLOTS))
                    T.wait(act, l, at + 1, e)
                    A(G[0:SLOTS, SAMPLE:NTOK], bank(T, at + 1, SLOTS)[:, 0:P], ACT.Identity)
                    T.take(A(gate[0:SLOTS, :], bank(T, at + 1, SLOTS)[:, P:P + 1], ACT.Identity), at + 1)

                def out2(e, job, dst, src):
                    T.wait(act, l, job, e)
                    T.take(A(dst, src, ACT.Identity), job)

                def expert(e, n, last):
                    act.wait_ge(s_gu_used, (n + 1) * KD)
                    for i in range(2):
                        A(hm[0:SLOTS, i * 512:(i + 1) * 512], psW[0:SLOTS, 0, i * 512:(i + 1) * 512], ACT.Silu).then_inc(s_silu, 1)
                    at = FRONT + (0 if last else 2)
                    for i in range(2):
                        out2(e, at + i, hmT[:, 4 * i:4 * i + 4, :].rearrange("p k c -> p (k c)"), bank(T, at + i)[:, 0:4 * SLOTS])
                    if not last:
                        selection_out(e, at + 2 + COMBINE)

                selection_out(0, 2)
                with act.Fori(0, EXPERTS - 1) as e:
                    expert(e, l * EXPERTS + e, False)
                expert(EXPERTS - 1, l * EXPERTS + EXPERTS - 1, True)
            T.layers_taken(act, DEPTH)
            norm_squares(2 * DEPTH)

        @block.vector
        def _(dve):
            V = nc.vector
            chain = Chain(dve, s_dve, DVE_LINKS)
            link, mark = chain.link, chain.mark

            def normalised(l, n, first):
                dve.wait_ge(s_std, n + 1)
                link(V.reciprocal(rstd, std))
                for t in range(NT):
                    V.tensor_scalar(xn[:, t, :], x[:, t, :], rstd[:, t:t + 1], None, ALU.mult).then_inc(s_xn, 1)

            def scales(l, dst, sc, gain):
                V.scalar_tensor_tensor(dst, sc, 1.0, gain.unsqueeze(2).broadcast_to([P, KD, 2]), ALU.add, ALU.mult).then_inc(s_scale, 1)

            def norm_out(l, which, scale, shift):
                dve.wait_ge(s_scale, 2 * l + (2 if which == "norm2" else 1))
                for k in range(1, KD, 2):
                    job = f"{which}.{k}"
                    T.wait(dve, l, job)
                    T.take(V.tensor_scalar(hT[:, k, 0:SAMPLE], bank(T, job), scale[:, k, 1:2], shift[:, k, 1:2], ALU.mult, ALU.add), job)
                job = f"{which}.{KD + 1}"
                T.wait(dve, l, job)
                for k in range(4):
                    ins = V.tensor_scalar(hT[:, 4 + k, SAMPLE:NTOK], bank(T, job)[:, k * P:(k + 1) * P], scale[:, 4 + k, 0:1], shift[:, 4 + k, 0:1], ALU.mult, ALU.add)
                T.take(ins, job)

            def decays(l):
                dve.wait_ge(s_dexp, l + 1)
                y, u, d, z, ln, lg = (lgt[:, i, :] for i in range(6))
                V.tensor_scalar(u, y, -1.0, 1.0, ALU.mult, ALU.add).then_inc(s_dec, 1)
                dve.wait_ge(s_dec, l + 1)
                link(V.tensor_scalar(d, u, -1.0, None, ALU.add))
                link(V.tensor_scalar(z, d, 0.0, None, ALU.is_equal))
                link(V.tensor_tensor(d, d, z, ALU.subtract))
                link(V.reciprocal(d, d))
                dve.wait_ge(s_dlog, l + 1)
                link(V.tensor_tensor(d, d, ln, ALU.mult))
                link(V.tensor_tensor(d, d, z, ALU.add))
                link(V.scalar_tensor_tensor(lg, y, -1.0, d, ALU.mult, ALU.mult))
                V.tensor_scalar(kd[:, 0:HEADS], lg[:, 0:HEADS], con("kpos")[:, 0:1], None, ALU.mult)
                V.tensor_scalar(kd[:, HEADS:2 * HEADS], lg[:, HEADS:2 * HEADS], con("kpos")[:, 1:2], None, ALU.mult).then_inc(s_lg, 1)

            def latents(l):
                W.taken(dve, l, "mla_a.p")
                W.taken(dve, l, "mla_b")
                link(V.tensor_tensor(lat_sq, mla[:, :, 0:QL + KL], mla[:, :, 0:QL + KL], ALU.mult))
                V.tensor_reduce(mss[:, 0, :], lat_sq[:, :, 0:QL], AX.X, ALU.add)
                V.tensor_reduce(mss[:, 1, :], lat_sq[:, :, QL:QL + KL], AX.X, ALU.add).then_inc(s_mss, 1)
                kp = mla[:, 0:TS, QL + KL:MLA_IN]
                kpv = kp.rearrange("p t (a b e) -> p t a b e", a=2, b=2)
                sinv = con("sin", TS, HEADS, ROPE)[:, :, 0, :].rearrange("p t (a b e) -> p t a b e", a=2, b=2)
                rot = rot_k.rearrange("p t (a b e) -> p t a b e", a=2, b=2)
                for b in range(2):
                    V.tensor_tensor(rot[:, :, :, b, :], kpv[:, :, :, 1 - b, :], sinv[:, :, :, b, :], ALU.mult)
                link(V.tensor_tensor(ctxt[:, 0:TS, KL:KL + ROPE], kp, con("cos", TS, HEADS, ROPE)[:, :, 0, :], ALU.mult))
                V.tensor_tensor(ctxt[:, 0:TS, KL:KL + ROPE], ctxt[:, 0:TS, KL:KL + ROPE], rot_k, ALU.add)
                V.tensor_copy(ctxt[:, CTX, KL:KL + ROPE], mla[:, CTX, QL + KL:MLA_IN])
                dve.wait_ge(s_mstd, l + 1)
                link(V.reciprocal(mrstd, mstd))
                V.tensor_tensor(mla[:, :, 0:QL], mla[:, :, 0:QL], mrstd[:, 0, :].unsqueeze(2).broadcast_to([P, NT, QL]), ALU.mult)
                link(V.tensor_tensor(ctxt[:, :, 0:KL], mla[:, :, QL:QL + KL], mrstd[:, 1, :].unsqueeze(2).broadcast_to([P, NT, KL]), ALU.mult))
                V.tensor_tensor(mla[:, :, 0:QL], mla[:, :, 0:QL], par("qg").unsqueeze(1).broadcast_to([P, NT, QL]), ALU.mult)
                V.tensor_tensor(ctxt[:, :, 0:KL], ctxt[:, :, 0:KL], par("kvg").unsqueeze(1).broadcast_to([P, NT, KL]), ALU.mult).then_inc(s_lat, 1)

            def rotate_queries(l):
                W.taken(dve, l, "q.0")
                W.taken(dve, l, "q.1")
                q = carve(ring_r, KT0, TS * HEADS, QK)[:, :, NOPE:QK]
                qv = q.rearrange("p n (a b e) -> p n a b e", a=2, b=2)
                sin = con("sin", TS * HEADS, ROPE)
                sv, rv_ = (v.rearrange("p n (a b e) -> p n a b e", a=2, b=2) for v in (sin, rot_q))
                for a in range(2):
                    for b in range(2):
                        ins = V.tensor_tensor(rv_[:, :, a, b, :], qv[:, :, a, 1 - b, :], sv[:, :, a, b, :], ALU.mult)
                link(ins)
                link(V.tensor_tensor(q, q, con("cos", TS * HEADS, ROPE), ALU.mult))
                V.tensor_tensor(q, q, rot_q, ALU.add).then_inc(s_qrot, 1)

            def gate_conv(l):
                for c in range(NG):
                    W.taken(dve, l, f"cg.{c}")
                    for lo, n, at in ((PAD, SAMPLE, 0), (CPROMPT + PAD, PROMPT, SAMPLE)):
                        ins = V.tensor_tensor(glu[:, c, lo:lo + n], glu[:, c, lo:lo + n], cscr[:, c, at:at + n], ALU.mult)
                link(ins)

            def taps(l):
                dve.wait_ge(s_pads, l + 1)
                w = par("convw", NG, TAPS)
                last = [0, 0]
                for k in range(TAPS):
                    for c in range(NG):
                        src = glu[:, c, k:k + CVAL]
                        if k == 0:
                            last[c] = mark(V.tensor_scalar(cacc[:, c, :], src, w[:, c, 0:1], par("convb")[:, c:c + 1], ALU.mult, ALU.add))
                            continue
                        chain.wait(last[c])
                        ins = V.scalar_tensor_tensor(cacc[:, c, :], src, w[:, c, k:k + 1], cacc[:, c, :], ALU.mult, ALU.add)
                        if k == TAPS - 1 and c == NG - 1:
                            ins.then_inc(s_conv, 1)
                        else:
                            last[c] = mark(ins)

            def spatial_norm(l):
                W.taken(dve, l, "vg.s")
                W.taken(dve, l, "vg.p")
                sq = carve(ring_r, KT0 + NG * NTOK, NT, GW)
                T.wait(dve, l, "qh.p")
                link(V.tensor_tensor(sq, vg, vg, ALU.mult))
                V.tensor_reduce(vss, sq, AX.X, ALU.add).then_inc(s_vss, 1)
                dve.wait_ge(s_vstd, l + 1)
                link(V.reciprocal(vrstd, vstd))
                V.tensor_tensor(vg, vg, vrstd.unsqueeze(2).broadcast_to([P, NT, GW]), ALU.mult).then_inc(s_vn, 1)

            def conv_centre(l):
                W.wait(dve, l, "mean")
                o = bank(W, "mean")
                V.tensor_tensor(cscr[:, :, 0:SAMPLE], cacc[:, :, 0:SAMPLE], o[:, 0:SAMPLE].unsqueeze(1).broadcast_to([P, NG, SAMPLE]), ALU.subtract)
                W.take(V.tensor_tensor(cscr[:, :, SAMPLE:NTOK], cacc[:, :, CPROMPT:CPROMPT + PROMPT], o[:, SAMPLE:NTOK].unsqueeze(1).broadcast_to([P, NG, PROMPT]), ALU.subtract), "mean")

            def conv_normalise(l):
                N.taken(dve, l, "var")
                V.reciprocal(crstd, cstd).then_inc(s_crs, 1)
                W.wait(dve, l, "cstd")
                W.take(V.tensor_tensor(cscr, cscr, bank(W, "cstd")[:, 0:NTOK].unsqueeze(1).broadcast_to([P, NG, NTOK]), ALU.mult), "cstd")

            def mix_out(l):
                sgb = par("sgb", NG, P)
                W.taken(dve, l, "u.0")
                W.taken(dve, l, "u.1")
                for c in range(NG):
                    job = f"mix.{c}"
                    W.wait(dve, l, job)
                    src = bank(W, job)[:, 0:NTOK].rearrange("p (t n) -> p t n", t=NT)
                    dst = yT[:, c, :].rearrange("p (t n) -> p t n", t=NT)
                    W.take(V.scalar_tensor_tensor(dst, src, par("sgg")[:, c:c + 1], sgb[:, c, :].unsqueeze(1).broadcast_to([P, NT, P]), ALU.mult, ALU.add), job)
                for c in range(NG):
                    W.taken(dve, l, f"mix.{c}")
                    V.tensor_tensor(yT[:, c, :], yT[:, c, :], uT[:, c, :], ALU.mult).then_inc(s_mixed, 1)

            def score_max(l, i):
                h, t = BLOCKS[i]
                W.wait(dve, l, f"s.{i}")
                o = bank(W, f"s.{i}")
                nh = HEADS if h == "ctx" else 1
                src = o[:, 0:HEADS * P].rearrange("p (h n) -> p h n", h=HEADS) if h == "ctx" else o[:, 0:NTOK]
                link(V.tensor_reduce(nmax[:, i % 2, 0:nh], src, AX.X, ALU.max, negate=True))
                V.tensor_scalar(nmax[:, i % 2, 0:nh], nmax[:, i % 2, 0:nh], ATT_SCALE, None, ALU.mult).then_inc(s_nmax, 1)

            def probs_out(l, i):
                h, t = BLOCKS[i]
                nh = HEADS if h == "ctx" else 1
                W.taken(dve, l, f"s.{i}")
                inv = mark(V.reciprocal(rinv[:, i % 2, 0:nh], rsum[:, i % 2, 0:nh]))
                T.wait(dve, l, f"pt.{i}")
                if i >= 2:
                    N.wait(dve, l, f"pv.{i - 2}")
                T.take(V.tensor_copy(probT[:, i % 2, 0:4 * P], bank(T, f"pt.{i}")), f"pt.{i}")
                N.wait(dve, l, f"pv.{i}")
                chain.wait(inv)
                if h == "ctx":
                    src = bank(N, f"pv.{i}")[:, 0:GW].rearrange("p (h n) -> p h n", h=HEADS)
                    ins = V.tensor_tensor(ydt[:, CTX, :].rearrange("p (h n) -> p h n", h=HEADS), src, rinv[:, i % 2, :].unsqueeze(2).broadcast_to([P, HEADS, NOPE]), ALU.mult)
                else:
                    ins = V.tensor_scalar(ydt[:, t, h * NOPE:(h + 1) * NOPE], bank(N, f"pv.{i}")[:, 0:NOPE], rinv[:, i % 2, 0:1], None, ALU.mult)
                N.take(ins, f"pv.{i}")

            def ret_masks(l):
                dve.wait_ge(s_tab, l + 1)
                for d in range(2):
                    v = masks[:, d].rearrange("p f (c n) -> p (f c) n", c=NG)
                    V.tensor_tensor(v, v, con("mask", 2, P)[:, d, :].unsqueeze(1).broadcast_to([P, HEADS, P]), ALU.mult)
                V.tensor_scalar(kd, kd, float(NOPE) ** -0.5, None, ALU.mult).then_inc(s_msk, 1)

            def masked_scores(l, t):
                if t == 0:
                    dve.wait_ge(s_msk, l + 1)
                if t >= 2:
                    W.wait(dve, l, f"ro.{t - 2}")
                job = f"rs.{t}"
                W.wait(dve, l, job)
                src = bank(W, job).rearrange("p (f n) -> p f n", f=2)[:, :, 0:GW]
                for d in range(2):
                    ins = V.tensor_tensor(sm[:, t % 2, d, :].rearrange("p (f n) -> p f n", f=2), src, masks[:, d], ALU.mult)
                W.take(ins, job)

            def states(l):
                for t in range(TS):
                    N.taken(dve, l, f"kv.{t}")
                s0 = par("s0", 2, NG, NOPE)
                for i in range(TS - 1):
                    for d in range(2):
                        t = i if d == 0 else TS - 1 - i
                        nt = t + 1 if d == 0 else t - 1
                        for c in range(NG):
                            old = s0[:, d, c, :] if i == 0 else sret[:, t, d, c, :]
                            ins = V.scalar_tensor_tensor(sret[:, nt, d, c, :], old, cdec[:, d, c:c + 1], kvs[:, t, d, c * NOPE:(c + 1) * NOPE], ALU.mult, ALU.add)
                    if i < TS - 2:
                        link(ins)
                ins.then_inc(s_sret, 1)

            def heads(t):
                return otok[:, t, :].rearrange("p (g e) -> p g e", g=8)

            def centre(l, t):
                W.taken(dve, l, f"ro.{t}")
                link(V.tensor_reduce(rsums[:, t, :], heads(t), AX.X, ALU.add, negate=True))
                V.scalar_tensor_tensor(heads(t), rsums[:, t, :].unsqueeze(2).broadcast_to([P, 8, NOPE]), 1.0 / NOPE, heads(t), ALU.mult, ALU.add).then_inc(s_ocen, 1)

            def variance(l, t):
                dve.wait_ge(s_osq, l * NT + t + 1)
                ins = V.tensor_reduce(rvar[:, t, :], osq[:, t, :].rearrange("p (g e) -> p g e", g=8), AX.X, ALU.add)
                if t == NT - 1:
                    ins.then_inc(s_ovar, 1)

            def retention(l):
                masked_scores(l, 0)
                states(l)
                for t in range(NT):
                    if t + 1 < NT:
                        masked_scores(l, t + 1)
                    centre(l, t)
                    if t:
                        variance(l, t - 1)
                variance(l, NT - 1)
                dve.wait_ge(s_ostd, l + 1)
                link(V.reciprocal(rrstd, rdev))
                marks = []
                for t in range(NT):
                    marks.append(mark(V.tensor_tensor(heads(t), heads(t), rrstd[:, t, :].unsqueeze(2).broadcast_to([P, 8, NOPE]), ALU.mult)))
                for t in range(NT):
                    chain.wait(marks[t])
                    for d in range(2):
                        o = otok[:, t, :].rearrange("p (f d c e) -> p f d c e", f=2, d=2, c=NG)[:, :, d]
                        g = gates[:, d, t, :].rearrange("p (c f e) -> p f c e", c=NG, f=2)
                        ins = V.tensor_tensor(o, o, g, ALU.mult)
                    marks[t] = mark(ins)
                for t in range(NT):
                    chain.wait(marks[t])
                    o = otok[:, t, :].rearrange("p (f d c e) -> p f d c e", f=2, d=2, c=NG)
                    ins = V.tensor_tensor(yct[:, t, :].rearrange("p (c f e) -> p f c e", c=NG, f=2), o[:, :, 0], o[:, :, 1], ALU.add)
                ins.then_inc(s_yc, 1)

            def residual(l):
                W.taken(dve, l, "g1.s")
                W.taken(dve, l, "g1.p")
                for u in range(4):
                    lo, hi = u * GW, (u + 1) * GW
                    for which, s_, tiles, n in (("s", 1, slice(0, TS), TS), ("p", 0, slice(CTX, NT), 1)):
                        job = f"o.{u}.{which}"
                        W.wait(dve, l, job)
                        tmp = (otmp[:, 0:n * GW] if s_ else otmp_p).rearrange("p (t n) -> p t n", t=n)
                        if u:
                            dve.wait_ge(s_res, 8 * l + 2 * u - s_)
                        W.take(V.tensor_tensor(tmp, bank(W, job)[:, 0:n * GW].rearrange("p (t n) -> p t n", t=n), g1b[:, s_, lo:hi].unsqueeze(1).broadcast_to([P, n, GW]), ALU.mult), job)
                        W.taken(dve, l, job)
                        V.tensor_tensor(x[:, tiles, lo:hi], x[:, tiles, lo:hi], tmp, ALU.add).then_inc(s_res, 1)

            def affinity(l):
                N.wait(dve, l, "logits")
                lgts = bank(N, "logits")[:, 0:NT * EXPERTS].rearrange("p (t e) -> p t e", t=NT)
                link(V.tensor_reduce(amax, lgts, AX.X, ALU.max))
                N.take(V.tensor_tensor(aff, lgts, amax.unsqueeze(2).broadcast_to([P, NT, EXPERTS]), ALU.subtract), "logits")
                dve.wait_ge(s_lexp, l + 1)
                link(V.tensor_reduce(asum, aff, AX.X, ALU.add))
                link(V.reciprocal(arec, asum))
                V.tensor_tensor(aff, aff, arec.unsqueeze(2).broadcast_to([P, NT, EXPERTS]), ALU.mult).then_inc(s_aff, 1)
                for dst, src in ((Afull, A2), (Bfull, modT[:, 3 * KD:4 * KD, :])):
                    V.tensor_copy(dst[:, :, 0:CAPS], src[:, :, 1:2].broadcast_to([P, KD, CAPS]))
                    V.tensor_copy(dst[:, :, CAPS:SLOTS], src[:, :, 0:1].broadcast_to([P, KD, CAPP])).then_inc(s_full, 1)

            def choose(l):
                for job, lo, hi, cap, first in (("afft.s", 0, SAMPLE, CAPS, 0.0), ("afft.p", SAMPLE, NTOK, CAPP, float(CAPS))):
                    w, c = work[:, lo:hi], cum[:, lo:hi]
                    T.wait(dve, l, job)
                    T.take(V.tensor_copy(w, bank(T, job, EXPERTS)[:, 0:hi - lo]), job)
                    T.taken(dve, l, job)
                    for _ in range(cap // 8):
                        settle(dve)
                        link(V.max(top8[0:EXPERTS, :], w))
                        settle(dve)
                        link(V.match_replace(w, top8[0:EXPERTS, :], w, -1.0))
                    link(V.tensor_scalar(w, w, 0.0, None, ALU.is_lt))
                    link(V.tensor_tensor_scan(c, w, w, first, ALU.add, ALU.max))
                    V.tensor_tensor(w, c, w, ALU.mult).then_inc(s_slotcode, 1)

            def select(l, e):
                V.tensor_copy(affc.unsqueeze(2), aff[:, :, bass.ds(e, 1)])
                V.tensor_tensor(S, con("iota").unsqueeze(1).broadcast_to([P, NT, SLOTS]), slotT[:, :, bass.ds(e, 1)].broadcast_to([P, NT, SLOTS]), ALU.is_equal).then_inc(s_S, 1)

            def gathered(e, at, n):
                for i in range(2):
                    T.wait(dve, l_[0], at + i, e)
                    o = bank(T, at + i)[:, 0:4 * SLOTS].rearrange("p (k c) -> p k c", k=4)
                    dst = xeT[:, 4 * i:4 * i + 4, :]
                    T.take(V.tensor_tensor(dst, o, Afull[:, 4 * i:4 * i + 4, :], ALU.mult), at + i)
                    T.taken(dve, l_[0], at + i, e)
                    V.tensor_tensor(dst, dst, Bfull[:, 4 * i:4 * i + 4, :], ALU.add).then_inc(s_xe, 1)

            def expert(e, n, last):
                if not last:
                    T.wait(dve, l_[0], 3, e)
                    settle(dve)
                    select(l_[0], e + 1)
                for i in range(2):
                    dve.wait_ge(s_silu, START + 2 * n + i + 1)
                    h = hm[0:SLOTS, i * 512:(i + 1) * 512]
                    V.tensor_tensor(h, h, psW[0:SLOTS, 1, i * 512:(i + 1) * 512], ALU.mult).then_inc(s_hm, 1)
                at = FRONT
                if not last:
                    gathered(e, at, n + 1)
                    at += 2
                at += 2
                T.taken(dve, l_[0], 3, e)
                dve.wait_ge(s_dn_used, 4 * n + 4)
                for i in range(2):
                    c = slice(i * 512, (i + 1) * 512)
                    V.scalar_tensor_tensor(ye[0:SLOTS, c], psN[0:SLOTS, i, :], gate[0:SLOTS, :], g2b[0:SLOTS, c], ALU.mult, ALU.mult).then_inc(s_ye, 1)
                for j in range(COMBINE):
                    half, t = divmod(j, NT)
                    xs = x[:, t, half * 512:(half + 1) * 512]
                    T.wait(dve, l_[0], at + j, e)
                    T.take(V.tensor_tensor(xs, xs, bank(T, at + j), ALU.add), at + j)

            l_ = [0]
            dve.wait_ge(s_consts, 16)
            dve.wait_ge(s_x, 32)
            with dve.Fori(0, DEPTH) as l:
                l_[0] = l
                chain.start_layer(l)
                normalised(l, 2 * l, True)
                dve.wait_ge(s_params, 16 * l + 16)
                decays(l)
                for s in STEPS:
                    kind, _, arg = s.partition(":")
                    if kind == "norm1":
                        N.taken(dve, l, "mod.6")
                        N.taken(dve, l, "mod.7")
                        scales(l, A1, modT[:, KD:2 * KD, :], par("n1g"))
                        norm_out(l, "norm1", A1, modT[:, 0:KD, :])
                    elif s == "in:mla":
                        latents(l)
                    elif s == "in:cg":
                        gate_conv(l)
                    elif kind == "mla_q":
                        rotate_queries(l)
                    elif kind == "mla_kv":
                        taps(l)
                    elif s == "in:vg":
                        spatial_norm(l)
                    elif kind == "conv_mean":
                        conv_centre(l)
                    elif kind == "conv_var":
                        conv_normalise(l)
                    elif kind == "mix":
                        mix_out(l)
                    elif kind == "ret_tables":
                        ret_masks(l)
                    elif kind == "att":
                        score_max(l, int(arg))
                        if int(arg):
                            probs_out(l, int(arg) - 1)
                    elif kind == "att_end":
                        probs_out(l, len(BLOCKS) - 1)
                    elif kind == "retention":
                        retention(l)
                    elif kind == "out_proj":
                        residual(l)
                    elif kind == "norm2":
                        N.taken(dve, l, "mod.18")
                        N.taken(dve, l, "mod.19")
                        scales(l, A2, modT[:, 4 * KD:5 * KD, :], par("n2g"))
                        normalised(l, 2 * l + 1, False)
                        norm_out(l, "norm2", A2, modT[:, 3 * KD:4 * KD, :])
                    elif kind == "router":
                        affinity(l)
                    elif kind == "rows_g2":
                        choose(l)
                dve.wait_ge(s_full, 2 * l + 2)
                chain.end_layer()
                T.taken(dve, l, "slots")
                dve.wait_ge(s_aff, l + 1)
                settle(dve)
                select(l, 0)
                gathered(0, 0, l * EXPERTS)
                W.taken(dve, l, "g2")
                settle(dve)
                with dve.Fori(0, EXPERTS - 1) as e:
                    expert(e, l * EXPERTS + e, False)
                expert(EXPERTS - 1, l * EXPERTS + EXPERTS - 1, True)
            dve.wait_ge(s_std, 2 * DEPTH + 1)
            V.reciprocal(rstd, std).then_inc(s_dve, 1)
            dve.wait_ge(s_dve, DEPTH * DVE_LINKS + 1)
            dve.wait_ge(s_fg, 16)
            for t in range(NT):
                V.scalar_tensor_tensor(xn[:, t, :], x[:, t, :], rstd[:, t:t + 1], stream_r[:, 0:D], ALU.mult, ALU.mult).then_inc(s_y, 1)

        @block.gpsimd
        def _(pool):
            Q = nc.gpsimd

            with pool.Fori(0, DEPTH) as l:
                W.wait(pool, l, "mla_a.s")
                settle(pool)
                for c in range(NG):
                    for lo, n in ((0, PAD), (PAD + SAMPLE, 2 * PAD), (CROW - PAD, PAD)):
                        ins = Q.memset(glu[:, c, lo:lo + n], 0.0)
                ins.then_inc(s_pads, 1)
                pool.wait_ge(s_tab, l + 1)
                W.wait(pool, l, "rgb.p")
                for d in range(2):
                    Q.tensor_tensor(qTd[:, d].rearrange("p c (t n) -> p c t n", t=TS), qT[:, :, 0:SAMPLE].rearrange("p c (t n) -> p c t n", t=TS),
                                    qdec[:, d].unsqueeze(2).broadcast_to([P, NG, TS, P]), ALU.mult).then_inc(s_qtd, 1)
                W.wait(pool, l, f"s.{len(BLOCKS) - 1}")
                pool.wait_ge(s_msk, l + 1)
                for j in ("ktok.1", "ktok.p"):
                    T.taken(pool, l, j)
                for d in range(2):
                    Q.tensor_tensor(kdk[:, d].rearrange("p t (h n) -> p t h n", h=HEADS), ktok.rearrange("p t (h n) -> p t h n", h=HEADS),
                                    kd[:, d * HEADS:(d + 1) * HEADS].unsqueeze(1).unsqueeze(3).broadcast_to([P, NT, HEADS, NOPE]), ALU.mult).then_inc(s_kdk, 1)


_OUT_SHAPES = (("y_prompt", (1, PROMPT, D)), ("y_sample", (1, SAMPLE, D)), ("new_ckv", (1, DEPTH, P, KL)),
               ("new_kpe", (1, DEPTH, P, ROPE)), ("new_state", (1, DEPTH, 2, HEADS, NOPE, NOPE)))
_BIG = ("x_prompt", "x_sample", "w_mod", "w_in", "w_out", "w_gate", "w_up", "w_down")


def _constants():
    c = np.zeros((P, NCONST), np.float32)

    def put(name, v):
        lo, hi = CAT[name]
        c[:, lo:hi] = np.asarray(v, np.float32).reshape(-1, hi - lo)

    j, i = np.arange(P)[:, None], np.arange(P)[None, :]
    put("ident", np.eye(P))
    put("mean", np.full((P, P), 1.0 / GW))
    put("expo", np.concatenate([np.maximum(i - j, 0), np.maximum(j - i, 0)], 1))
    put("mask", np.concatenate([i >= j, j >= i], 1) * float(NOPE) ** -0.5)
    put("qpos", np.concatenate([np.tile(i + 1, (P, 1)), np.tile(P - i, (P, 1))], 1))
    put("kpos", np.concatenate([P - 1 - j, j], 1))
    tok = np.arange(SAMPLE)
    inv = (np.float32(10000.0) ** (-np.arange(0, ROPE // 2, 2, dtype=np.float32) / np.float32(ROPE // 2))).astype(np.float32)
    ra, ca = ((v.astype(np.float32)[:, None] * inv) for v in (tok // 64, tok % 64))
    ang = np.concatenate([ra, ra, ca, ca], 1).reshape(TS, P, 1, ROPE).transpose(1, 0, 2, 3)
    sign = np.repeat(np.array([-1.0, 1.0, -1.0, 1.0], np.float32), ROPE // 4)
    put("cos", np.broadcast_to(np.cos(ang), (P, TS, HEADS, ROPE)))
    put("sin", np.broadcast_to(np.sin(ang) * sign, (P, TS, HEADS, ROPE)))
    put("iota", np.tile(np.arange(1, SLOTS + 1), (P, 1)))
    put("eps", np.full((P, 1), EPS))
    return c


def _params(a):
    out = np.zeros((DEPTH, P, NPARAM), np.float32)

    def put(name, v, rows=slice(0, P), cols=None):
        lo, hi = PAT[name]
        lo, hi = (lo, hi) if cols is None else (lo + cols[0], lo + cols[1])
        out[:, rows, lo:hi] = v.reshape(DEPTH, -1, hi - lo)

    def columns(v):
        return v.reshape(DEPTH, -1, P).transpose(0, 2, 1)

    def everywhere(v):
        return np.repeat(v.reshape(DEPTH, 1, -1), P, axis=1)

    for name, key in (("n1g", "norm1_g"), ("n2g", "norm2_g"), ("bmod", "b_mod"), ("sgg", "sg_norm_g"), ("convb", "conv_b"),
                      ("lng", "conv_ln_g"), ("lnb", "conv_ln_b"), ("gng", "ret_gn_g")):
        put(name, columns(a[key]))
    put("router", a["router"].reshape(DEPTH, KD, P, EXPERTS).transpose(0, 2, 1, 3))
    df, db = a["ret_decay_f"], a["ret_decay_b"]
    put("dec", everywhere(df), cols=(0, 4))
    put("dec", everywhere(db), cols=(4, 8))
    for half in range(2):
        rows = slice(64 * half, 64 * half + 64)
        put("dec", everywhere(df[:, half::2])[:, :64], rows, (8, 10))
        put("dec", everywhere(db[:, half::2])[:, :64], rows, (10, 12))
        put("sgb", everywhere(a["sg_b"][:, half::2])[:, :64], rows)
    put("convw", a["conv_w"].reshape(DEPTH, TAPS, NG, P).transpose(0, 3, 2, 1))
    put("sgw", a["sg_w"].transpose(0, 3, 1, 2))
    put("pw", a["conv_pw"].reshape(DEPTH, NG, P, GW).transpose(0, 2, 1, 3))
    put("qg", everywhere(a["q_norm_g"]))
    put("kvg", everywhere(a["kv_norm_g"]))
    put("wuq", a["w_uq"][:, 0:P], cols=(0, HEADS * QK))
    put("wuq", a["w_uq"][:, P:QL], slice(0, QL - P), (HEADS * QK, 2 * HEADS * QK))
    put("wukv", a["w_ukv"])
    put("cache", a["cache_mla_ckv"][0], cols=(0, KL))
    put("cache", a["cache_mla_kpe"][0], cols=(KL, KL + ROPE))
    put("s0", a["state_ret"][0].reshape(DEPTH, 2, NG, P, NOPE).transpose(0, 3, 1, 2, 4))
    return out


def kernel(**inputs):
    import concourse.bacc as bacc
    from concourse.bass_utils import run_bass_kernel_spmd

    a = {k: np.ascontiguousarray(v) for k, v in inputs.items()}
    arrays = {k: a[k] for k in _BIG}
    arrays["cond"] = np.ascontiguousarray(np.stack([a["c_ctx"], a["c"][0]]).reshape(2, KD, P).transpose(2, 1, 0).reshape(P, KD * 2))
    arrays["params"], arrays["consts"] = _params(a), _constants()
    arrays["final_g"] = a["final_norm_g"]
    nc = bacc.Bacc("TRN2", target_bir_lowering=False, num_devices=1)
    io = {k: nc.dram_tensor(k, v.shape, F32, kind="ExternalInput").ap() for k, v in arrays.items()}
    for name, shape in _OUT_SHAPES:
        io[name] = nc.dram_tensor(name, shape, F32, kind="ExternalOutput").ap()
    build(nc, io)
    r = run_bass_kernel_spmd(nc, [arrays], core_ids=[0])
    return tuple(r.results[0][name] for name, _ in _OUT_SHAPES)
```

```python
from contextlib import ExitStack

import concourse.bass as bass
from concourse import mybir
import numpy as np

F32 = mybir.dt.float32
ALU = mybir.AluOpType
ACT = mybir.ActivationFunctionType
AX = mybir.AxisListType

P = 128
D = 1024
KD = D // P
DEPTH = 2
TS, TP = 4, 1
NT = TS + TP
CTX = TS
NTOK = NT * P
NKEY = NTOK + P
SAMPLE, PROMPT = TS * P, TP * P
HEADS = 4
GW = 256
NG = GW // P
TAPS = 31
PAD = TAPS // 2
CROW = SAMPLE + PROMPT + 4 * PAD
CVAL = CROW - 2 * PAD
CPROMPT = SAMPLE + 2 * PAD
QL, KL, ROPE, NOPE, QK = 192, 128, 32, 64, 96
MLA_IN = QL + KL + ROPE
EXPERTS, FF = 16, 1024
KF = FF // P
CAPS, CAPP = 64, 16
PAIRS = EXPERTS // 2
HALFW = 512
QW = 256
STRIP = 32
EPS = 1e-6
ATT_SCALE = float(QK) ** -0.5

IN_AT = dict(u=0, vg=256, ca=512, cg=768, rq=1024, rk=1280, rv=1536, rgf=1792, rgb=2048, mla_a=2304, mla_b=2560)
MLA_B = QL + KL + ROPE - GW

UNITS = [("mod", i) for i in range(8)] + [("in", "mla_a"), ("in", "mla_b")]
for _n, _g in enumerate(["", "ca", "cg", "u", "vg", "rq", "rk", "rv"]):
    UNITS += ([("in", _g)] if _g else []) + [("mod", 8 + 2 * _n), ("mod", 9 + 2 * _n)]
UNITS += [("in", "rgf"), ("in", "rgb")] + [("out", i) for i in range(4)]
MOD_FIRST, MOD_UNITS = 8, 24
NSTREAM = 3
NUNIT = len(UNITS)
assert NUNIT % NSTREAM == 0

BLOCKS = [(h, t) for h in range(HEADS) for t in range(TS)] + [("ctx", CTX)]
BLOCKS_AFTER = {"rq": 3, "rk": 3, "rv": 3, "rgf": 3, "rgb": 5}

STEPS = ["mod:0-8", "norm1", "in:mla", "mod:8-10", "in:ca", "mod:10-12", "in:cg", "mod:12-14", "latents", "mla_q", "mla_kv",
         "in:u", "mod:14-16", "in:vg", "mod:16-18", "conv_mean"]
_b = 0
for _n, _g in enumerate(["rq", "rk", "rv", "rgf", "rgb"]):
    STEPS += [f"in:{_g}"] + ([f"mod:{18 + 2 * _n}-{20 + 2 * _n}"] if _n < 3 else [])
    STEPS += {"rq": ["conv_var", "mix"], "rk": ["conv_out"], "rv": ["ret_tables"]}.get(_g, [])
    STEPS += [f"att:{_i}" for _i in range(_b, _b + BLOCKS_AFTER[_g])]
    _b += BLOCKS_AFTER[_g]
STEPS += ["att_end", "rows_g1", "retention", "out_proj", "norm2", "router", "rows_g2"]



def mod_order(lo, hi):
    out = []
    for u in range(lo, hi):
        out.append(("mod", u))
        if u not in (0, MOD_FIRST):
            out.append(("modc", u - 1))
        if u in (MOD_FIRST - 1, MOD_UNITS - 1):
            out.append(("modc", u))
    return out


TOKEN_MAJOR = ("vg", "rv", "rgf", "rgb")
W_JOBS, T_JOBS, N_JOBS = [], [], []
for _s in STEPS:
    _k, _, _a = _s.partition(":")
    if _k == "mod":
        N_JOBS += [f"{_j}.{_i}" for _j, _i in mod_order(*map(int, _a.split("-")))]
    elif _k in ("norm1", "norm2"):
        T_JOBS += [f"{_k}.{i}" for i in range(KD + 2)]
    elif _k == "in":
        W_JOBS += ["mla_a.s", "mla_a.p", "mla_b"] if _a == "mla" else [f"{_a}.s", f"{_a}.p"] if _a in TOKEN_MAJOR else [f"{_a}.0", f"{_a}.1"]
        T_JOBS += ["ktok.0", "ktok.1", "ktok.p"] if _a == "rk" else []
    elif _k == "latents":
        T_JOBS += ["cq.0", "cq.1", "cq.p", "ckv.0", "ckv.1", "kpe.0", "kpe.1"]
    elif _k == "mla_q":
        W_JOBS += ["q.0", "q.1", "q.2"]
        T_JOBS += [f"qh.{h}" for h in range(HEADS)] + ["qh.p"]
    elif _k == "mla_kv":
        W_JOBS += [f"kh.{h}" for h in range(HEADS)] + ["v.0", "v.1"]
    elif _k == "mix":
        W_JOBS += ["mix.0", "mix.1"]
    elif _k == "conv_mean":
        W_JOBS += ["mean"]
    elif _k == "conv_var":
        N_JOBS += ["var"]
        W_JOBS += ["cstd"]
    elif _k == "conv_out":
        W_JOBS += ["pw.0", "pw.1"]
    elif _k == "att":
        W_JOBS += [f"s.{_a}"]
    elif _k == "rows_g1":
        W_JOBS += ["g1.s", "g1.p"]
    elif _k == "retention":
        N_JOBS += [f"kv.{t}" for t in range(NT)]
        for _t in range(NT):
            W_JOBS += [f"rs.{_t}"]
            if _t:
                W_JOBS += [f"ro.{_t - 1}"]
        W_JOBS += [f"ro.{NT - 1}"]
        T_JOBS += ["yc.0", "yc.1", "yc.p"]
    elif _k == "out_proj":
        W_JOBS += [f"o.{u}.{h}" for u in range(4) for h in "sp"]
    elif _k == "router":
        N_JOBS += ["logits"]
        T_JOBS += ["logits.t", "afft.s", "afft.p", "slots"]
    elif _k == "rows_g2":
        W_JOBS += ["g2.s", "g2.p"]
    if _k == "att" and int(_a) >= 1 or _k == "att_end":
        _i = int(_a) - 1 if _k == "att" else len(BLOCKS) - 1
        T_JOBS += [f"pt.{_i}", f"pt.{_i}b"] if _i < len(BLOCKS) - 1 else [f"pt.{_i}"]
        N_JOBS += [f"pv.{_i - 1}"] if _i else []
    if _k == "att_end":
        N_JOBS += [f"pv.{len(BLOCKS) - 1}"]
        T_JOBS += ["yd.0", "yd.1", "yd.p"]
for _jobs in (W_JOBS, T_JOBS, N_JOBS):
    if len(_jobs) % 2:
        _jobs.append("spare")

GATHERED = 3
FRONT = GATHERED
COMBINE = NT * 2
T_PAIR = 2 + 3 + GATHERED + 2 + COMBINE
T_MOE = FRONT + PAIRS * T_PAIR - GATHERED

LAST_JOB = {("in", g): (f"{g}.p" if g in TOKEN_MAJOR else f"{g}.1") for g in IN_AT}
LAST_JOB[("in", "mla_a")], LAST_JOB[("in", "mla_b")] = "mla_a.p", "mla_b"
LAST_JOB.update({("out", i): f"o.{i}.p" for i in range(4)})
LAST_JOB.update({("mod", i): f"mod.{i}" for i in range(24)})

PARAMS = dict(n1g=KD, n2g=KD, bmod=48, router=KD * STRIP, sgg=NG, convb=NG, lng=NG, lnb=NG, gng=NG, dec=12,
              convw=NG * TAPS, sgb=NG * P, sgw=HEADS * P, pw=NG * GW, qg=QL, kvg=KL, wuq=2 * HEADS * QK,
              wukv=HEADS * 2 * NOPE, cache=KL + ROPE, s0=2 * NG * NOPE)
CONSTS = dict(ident=P, mean=P, expo=2 * P, mask=2 * P, qpos=2 * P, kpos=2, cos=TS * ROPE,
              sin=TS * ROPE, iota=CAPS, eps=1, strips=2)


def spans(sizes):
    out, at = {}, 0
    for name, n in sizes.items():
        out[name] = (at, at + n)
        at += n
    return out, at


PAT, NPARAM = spans(PARAMS)
CAT, NCONST = spans(CONSTS)
NSMALL = 367
KEPT = PAT["router"][1]


START = 1


class Jobs:

    def __init__(self, jobs, moe, per_expert, done, out):
        self.at = {j: i for i, j in enumerate(jobs)}
        self.dense, self.layer, self.expert, self.done_sem, self.out_sem = len(jobs), len(jobs) + moe, per_expert, done, out
        assert len(self.at) == len(jobs) and self.layer % 2 == 0 and per_expert % 2 == 0

    def index(self, job):
        return self.at[job] if isinstance(job, str) else self.dense + job

    def buf(self, job):
        return self.index(job) % 2

    def full(self, l, job, e=0):
        return l * self.layer + e * self.expert + self.index(job)

    def half(self, l, job, e=0):
        return l * (self.layer // 2) + e * (self.expert // 2) + self.index(job) // 2

    def claim(self, pe, l, job, e=0):
        pe.wait_ge(self.out_sem[self.buf(job)], START + self.half(l, job, e))

    def finish(self, ins):
        ins.then_inc(self.done_sem, 1)

    def wait(self, eng, l, job, e=0):
        eng.wait_ge(self.done_sem, START + self.full(l, job, e) + 1)

    def take(self, ins, job):
        ins.then_inc(self.out_sem[self.buf(job)], 1)

    def taken(self, eng, l, job, e=0):
        eng.wait_ge(self.out_sem[self.buf(job)], START + self.half(l, job, e) + 1)

    def layers_taken(self, eng, l):
        for s in self.out_sem:
            eng.wait_ge(s, START + l * (self.layer // 2))

    def layers_done(self, eng, l):
        eng.wait_ge(self.done_sem, START + l * self.layer)

    def start(self, eng):
        for s in (self.done_sem, *self.out_sem):
            eng.sem_inc(s, START)


class Chain:

    def __init__(self, eng, sem, per_layer):
        self.eng, self.sem, self.per_layer = eng, sem, per_layer
        self.base, self.n = 0, 0

    def start_layer(self, l, before=0):
        self.base, self.n = l * self.per_layer + before, 0

    def mark(self, ins):
        ins.then_inc(self.sem, 1)
        self.n += 1
        return self.n

    def wait(self, n):
        self.eng.wait_ge(self.sem, self.base + n)

    def link(self, ins):
        self.wait(self.mark(ins))

    def end_layer(self):
        if self.n != self.per_layer:
            raise ValueError(f"the links of a layer are {self.n}, not {self.per_layer}")


DVE_LINKS = 158


def build(nc, io):
    ctx = ExitStack()
    with ctx:
        def sb(name, n):
            return ctx.enter_context(nc.sbuf_tensor(name, [P, n], F32))[:, :]

        def sem(name):
            return ctx.enter_context(nc.semaphore(name))

        def carve(region, at, *dims, parts=(0, P)):
            n = int(np.prod(dims))
            v = region[parts[0]:parts[1], at:at + n]
            names = " ".join(f"d{i}" for i in range(len(dims)))
            return v.rearrange(f"p ({names}) -> p {names}", **{f"d{i}": d for i, d in enumerate(dims)}) if len(dims) > 1 else v

        x = carve(sb("x", NT * D), 0, NT, D)
        xn_r = sb("xn_yt", NT * D)
        xn = carve(xn_r, 0, NT, D)
        yT = carve(xn_r, 0, KD, NTOK)
        h_r = sb("ht", KD * NTOK)
        hT = carve(h_r, 0, KD, NTOK)
        stream_r = sb("stream", NSTREAM * KD * GW)
        stream = carve(stream_r, 0, NSTREAM, KD, GW)
        RING = 12
        ring_r = sb("ring", RING * 2 * D)
        ring = carve(ring_r, 0, RING, 2, D)
        par_r = sb("param_cols", NPARAM)
        con_r = sb("const_cols", NCONST)

        def par(name, *dims, parts=(0, P)):
            return carve(par_r, PAT[name][0], *(dims or (PARAMS[name],)), parts=parts)

        def con(name, *dims, parts=(0, P)):
            return carve(con_r, CAT[name][0], *(dims or (CONSTS[name],)), parts=parts)

        ident, mean_w = con("ident"), con("mean")
        ctxt = carve(sb("ctx_tok", NT * (KL + ROPE)), 0, NT, KL + ROPE)
        sT = carve(sb("cond_cols", KD * STRIP), 0, KD, STRIP)
        mod_r = sb("mod_rows", 2 * GW)
        mod_rows = carve(mod_r, 0, 2, GW)
        lgT = mod_r[:, 0:2 * P]
        modT = carve(sb("mod_cols", 48 * 2), 0, 48, 2)
        A1 = carve(sb("scale1", KD * 2), 0, KD, 2)
        A2 = carve(sb("scale2", KD * 2), 0, KD, 2)
        small_r = sb("stats", NSMALL)
        _at = [0]

        def small(*dims):
            v = carve(small_r, _at[0], *dims)
            _at[0] += int(np.prod(dims))
            assert _at[0] <= NSMALL
            return v

        ss, std, rstd = small(NT), small(NT), small(NT)
        mss, mstd, mrstd = small(2, NT), small(2, NT), small(2, NT)
        vss, vstd, vrstd = small(NT), small(NT), small(NT)
        cstd, crstd = small(NT), small(NT)
        lgt = small(6, 12)
        kd, cdec = small(2 * HEADS), small(2, NG)
        nmax, rsum, rinv = small(2, HEADS), small(2, HEADS), small(2, HEADS)
        amax, asum, arec = small(NT), small(NT), small(NT)
        rsums, rvar, rdev, rrstd = small(NT, 8), small(NT, 8), small(NT, 8), small(NT, 8)
        top8, spare = small(8), small(3, 2)

        r_at = [0]

        def room(n):
            r_at[0] += n
            assert r_at[0] <= RING * 2 * D
            return r_at[0] - n

        MLA0 = room(NT * MLA_IN)
        mla = carve(ring_r, MLA0, NT, MLA_IN)
        ydt = carve(ring_r, MLA0, NT, GW)
        LAT0 = room(HEADS * NTOK + HEADS * NKEY + 6 * GW + NKEY)
        qhT = carve(ring_r, LAT0, HEADS, NTOK, parts=(0, QK))
        khT = carve(ring_r, LAT0 + HEADS * NTOK, HEADS, NKEY)
        vall = carve(ring_r, LAT0 + HEADS * (NTOK + NKEY), 6, GW)
        ckvT = carve(ring_r, LAT0 + HEADS * (NTOK + NKEY) + 6 * GW, NKEY)
        kdk = carve(ring_r, LAT0, 2, NT, GW)
        otok = carve(ring_r, LAT0 + 2 * NT * GW, NT, 2 * GW)
        osq = carve(ring_r, LAT0 + 4 * NT * GW, NT, 2 * GW)
        QT0 = room(NG * NTOK)
        cqT = carve(ring_r, QT0, NG, NTOK)
        qT = carve(ring_r, QT0, NG, NTOK)
        UV0 = room(2 * NG * NTOK)
        uT = carve(ring_r, UV0, NG, NTOK)
        vg = carve(ring_r, UV0 + NG * NTOK, NT, GW)
        prob = carve(ring_r, UV0, 2, NTOK)
        probT = carve(ring_r, UV0 + 2 * NTOK, 2, NTOK)
        sm = carve(ring_r, UV0, 2, 2, 2 * GW)
        GL0 = room(NG * CROW)
        glu = carve(ring_r, GL0, NG, CROW)
        csq = carve(ring_r, GL0, NG, NTOK)
        CA0 = room(NG * CVAL)
        cacc = carve(ring_r, CA0, NG, CVAL)
        zT = carve(ring_r, CA0, NG, NTOK)
        kvs = carve(ring_r, CA0, NT, 2, NG * NOPE)
        lat_sq = carve(ring_r, UV0, NT, QL + KL)
        rot_k = carve(ring_r, UV0 + NT * (QL + KL), TS, ROPE)
        rot_q = carve(ring_r, UV0, TS, HEADS, ROPE)
        CS0 = room(NG * NTOK)
        cscr = carve(ring_r, CS0, NG, NTOK)
        qdec = carve(ring_r, CS0, 2, NG, P)
        yct = carve(ring_r, CS0, NT, GW)
        KT0 = room(2 * NG * NTOK)
        kT = carve(ring_r, KT0, NG, NTOK)
        ktok = carve(ring_r, KT0 + NG * NTOK, NT, GW)
        qtok = carve(ring_r, KT0, NT, HEADS * QK)
        RV0 = room(3 * NT * GW)
        rv = carve(ring_r, RV0, NT, GW)
        gates = carve(ring_r, RV0 + NT * GW, 2, NT, GW)
        g1b = carve(h_r, 0, 2, D)
        qTd = carve(h_r, 2 * D, 2, NG, SAMPLE)
        otmp = carve(h_r, 2 * D, TS * GW)
        otmp_p = carve(h_r, 2 * D + TS * GW, GW)
        sret = carve(h_r, 2 * D + 2 * NG * SAMPLE, TS, 2, NG, NOPE)
        masks = carve(ring_r, GL0, 2, 2, NG * P)
        moe_at = {id(h_r): 0, id(par_r): KEPT}

        def moe(region, *dims, parts=(0, P)):
            at = moe_at[id(region)]
            moe_at[id(region)] += int(np.prod(dims))
            assert moe_at[id(region)] <= {id(h_r): KD * NTOK, id(par_r): NPARAM}[id(region)]
            return carve(region, at, *dims, parts=parts)

        g2b, g2q = moe(h_r, D), moe(h_r, QW)
        slotT, aff = moe(h_r, NT, EXPERTS), moe(h_r, NT, EXPERTS)
        ye = moe(h_r, 2, HALFW)
        zeroed = moe(h_r, HALFW + KD * 4 * CAPP)
        yep = zeroed[:, 0:HALFW]
        xpT = zeroed[:, HALFW:].rearrange("p (k s c) -> p k s c", k=KD, s=4)
        hm, hmp = moe(h_r, HALFW), moe(par_r, QW)
        hmT, hmpT = moe(h_r, HALFW // P, P), moe(h_r, QW // P, P)
        Sp = moe(h_r, 2, CAPP)
        Spw = moe(h_r, 4, 2, CAPP)
        Gp = moe(h_r, P)
        S = moe(par_r, TS, 2, CAPS)
        Sw = moe(par_r, TS, 2, CAPS)
        G = moe(par_r, 2, TS * P)
        xeT = moe(par_r, KD, 2, CAPS)
        work = carve(h_r, D + QW + 2 * NT * EXPERTS, NTOK, parts=(0, EXPERTS))
        cum = carve(par_r, KEPT + QW + 2 * TS * 2 * CAPS, NTOK, parts=(0, EXPERTS))

        psW = ctx.enter_context(nc.psum_tensor("wide", [P, 2, 1024], F32))[:, :, :]
        psT = ctx.enter_context(nc.psum_tensor("turned", [P, 2, 512], F32))[:, :, :]
        psN = ctx.enter_context(nc.psum_tensor("narrow", [P, 2, 512], F32))[:, :, :]

        W = Jobs(W_JOBS, 0, 0, sem("wide_done"), [sem("wide_out0"), sem("wide_out1")])
        T = Jobs(T_JOBS, T_MOE, T_PAIR, sem("turned_done"), [sem("turned_out0"), sem("turned_out1")])
        N = Jobs(N_JOBS, 0, 0, sem("narrow_done"), [sem("narrow_out0"), sem("narrow_out1")])
        s_consts, s_x, s_cond = sem("consts_landed"), sem("x_landed"), sem("cond_landed")
        s_params = sem("params_landed")
        s_unit = [sem(f"unit_landed{i}") for i in range(NSTREAM)]
        s_slot = [sem(f"slot_landed{i}") for i in range(RING)]
        s_gu_used, s_dn_used = sem("gateup_used"), sem("down_used")
        s_cond_ready, s_passed = sem("cond_ready"), sem("waits_passed")
        s_dve = sem("vector_step")
        s_mixed = sem("spatial_out")
        s_sq, s_std, s_xn, s_scale = sem("squares_ready"), sem("std_ready"), sem("xn_ready"), sem("scale_ready")
        s_mss, s_mstd, s_lat, s_qrot = sem("latent_squares"), sem("latent_std"), sem("latents_ready"), sem("queries_rotated")
        s_ctx_out = sem("ctx_stored")
        s_pads, s_sig, s_conv, s_csq = sem("pads_ready"), sem("conv_gate"), sem("conv_ready"), sem("conv_squares")
        s_cstd, s_crs, s_zin, s_z = sem("conv_std"), sem("conv_rstd"), sem("conv_normed"), sem("conv_silu")
        s_vss, s_vstd, s_vn = sem("spatial_squares"), sem("spatial_std"), sem("spatial_normed")
        s_nmax = sem("score_max")
        s_dec, s_dexp, s_dlog, s_lg = sem("decay_in"), sem("decay_exp"), sem("decay_log"), sem("log_decay")
        s_tab, s_msk = sem("decay_tables"), sem("masks_ready")
        s_kdk, s_qtd, s_sret = sem("k_decayed"), sem("q_decayed"), sem("states_ready")
        s_ocen, s_osq, s_ovar, s_ostd, s_yc = sem("ret_centred"), sem("ret_squares"), sem("ret_var"), sem("ret_std"), sem("ret_out")
        s_res, s_st_out = sem("residual_added"), sem("state_stored")
        s_lexp, s_aff = sem("logit_exp"), sem("affinity_ready")
        s_slotcode = sem("slotcode_ready")
        s_zeros, s_S, s_swap, s_weighed = sem("strips_zeroed"), sem("select_ready"), sem("selection_swapped"), sem("selection_weighed")
        s_silu, s_hm, s_ye, s_yep = sem("silu_ready"), sem("hidden_ready"), sem("latent_rows_out"), sem("context_rows_out")
        s_y, s_ystored, s_fg = sem("y_ready"), sem("y_stored"), sem("final_gain_landed")

        RINGS = ((W, W_JOBS), (T, T_JOBS), (N, N_JOBS))

        def bank(R, job, rows=P):
            return {id(W): psW, id(T): psT, id(N): psN}[id(R)][0:rows, R.buf(job), :]

        mod_h = io["w_mod"].rearrange("l (k p) n -> l p k n", p=P)
        in_h = io["w_in"].rearrange("l (k p) n -> l p k n", p=P)
        out_h = io["w_out"].rearrange("l (k p) n -> l p k n", p=P)
        down_h = io["w_down"].rearrange("l e (k p) n -> l e p k n", p=P)

        block = ctx.enter_context(nc.Block())

        def settle(eng):
            eng.sem_inc(s_passed, 1)

        @block.sync
        def _(sp):
            for R, _jobs in RINGS:
                R.start(sp)
            for s in (s_silu, s_hm):
                sp.sem_inc(s, START)
            sp.dma_start(sT.rearrange("p k s -> p (k s)"), io["cond"]).then_inc(s_cond, 16)
            sp.dma_start(con_r, io["consts"]).then_inc(s_consts, 16)
            sp.dma_start(x[:, 0:TS, :], io["x_sample"][0].rearrange("(t p) d -> p t d", p=P)).then_inc(s_x, 16)
            sp.dma_start(x[:, CTX, :], io["x_prompt"][0]).then_inc(s_x, 16)

            sp.wait_ge(s_consts, 16)

            def load_unit(l, n):
                kind, which = UNITS[n]
                if n < NSTREAM:
                    W.layers_done(sp, l)
                else:
                    before = UNITS[n - NSTREAM]
                    (N if before[0] == "mod" else W).wait(sp, l, LAST_JOB[before])
                settle(sp)
                lo = {"mod": lambda: which * GW, "out": lambda: which * GW, "in": lambda: IN_AT[which]}[kind]()
                w = MLA_B if which == "mla_b" else GW
                src = {"mod": mod_h, "in": in_h, "out": out_h}[kind][bass.ds(l, 1), :, :, lo:lo + w]
                sp.dma_start(stream[:, n % NSTREAM, :, 0:w], src.rearrange("l p k n -> (l p) k n")).then_inc(s_unit[n % NSTREAM], 16)

            def load_gateup(l, e, k):
                for i, w in enumerate(("w_gate", "w_up")):
                    src = io[w][bass.ds(l, 1), bass.ds(e, 1), k * P:(k + 1) * P, :]
                    sp.dma_start(ring[:, k, i, :], src.rearrange("l e p n -> (l e p) n")).then_inc(s_slot[k], 16)

            def load_down(l, e, j):
                src = down_h[bass.ds(l, 1), bass.ds(e, 1), :, 2 * j:2 * j + 2, :]
                sp.dma_start(ring[:, KD + j, :, :], src.rearrange("l e p k n -> (l e p) k n")).then_inc(s_slot[KD + j], 16)

            with sp.Fori(0, DEPTH) as l:
                for n in range(NSTREAM):
                    load_unit(l, n)
                T.layers_taken(sp, l)
                settle(sp)
                sp.dma_start(par_r, io["params"][bass.ds(l, 1)].rearrange("l p n -> (l p) n")).then_inc(s_params, 16)
                for n in range(NSTREAM, NUNIT):
                    load_unit(l, n)
                W.wait(sp, l, "o.0.s")
                sp.wait_ge(s_ctx_out, 32 * l + 32)
                sp.wait_ge(s_st_out, 32 * l + 32)
                settle(sp)
                for k in range(KD):
                    load_gateup(l, 0, k)
                for j in range(4):
                    load_down(l, 0, j)
                with sp.Fori(1, EXPERTS) as e:
                    for k in range(KD):
                        sp.wait_ge(s_gu_used, (l * EXPERTS + e) * KD + k - (KD - 1))
                        settle(sp)
                        load_gateup(l, e, k)
                    for j in range(4):
                        sp.wait_ge(s_dn_used, (l * EXPERTS + e) * 4 + j - 3)
                        settle(sp)
                        load_down(l, e, j)
            W.layers_done(sp, DEPTH)
            sp.dma_start(stream_r[:, 0:D], io["final_g"].partition_broadcast(P)).then_inc(s_fg, 16)
            sp.wait_ge(s_y, NT)
            sp.dma_start(io["y_sample"][0].rearrange("(t p) d -> p t d", p=P), xn[:, 0:TS, :]).then_inc(s_ystored, 16)
            sp.dma_start(io["y_prompt"][0], xn[:, CTX, :]).then_inc(s_ystored, 16)
            sp.wait_ge(s_ystored, 32)

        @block.tensor
        def _(pe):
            mm = nc.tensor.matmul
            unit_no = [0]

            def next_unit(l):
                n = unit_no[0]
                unit_no[0] += 1
                pe.wait_ge(s_unit[n % NSTREAM], (l * (NUNIT // NSTREAM) + n // NSTREAM + 1) * 16)
                return stream[:, n % NSTREAM, :, :]

            def mod_unit(l, u):
                job = f"mod.{u}"
                w = next_unit(l)
                N.claim(pe, l, job)
                for k in range(KD):
                    q = k % 4
                    ins = mm(psN[q * STRIP:(q + 1) * STRIP, N.buf(job), 0:GW], sT[:, k, :], w[:, k, :], start=(k < 4), stop=(k >= 4))
                N.finish(ins)

            def mod_columns(l, u):
                job = f"modc.{u}"
                N.taken(pe, l, f"mod.{u}")
                N.claim(pe, l, job)
                for c in range(NG):
                    ins = mm(bank(N, job)[:, 2 * c:2 * c + 2], mod_rows[:, u % 2, c * P:(c + 1) * P], con("strips"), start=True, stop=True)
                N.finish(ins)

            def transposes(l, job, outs_ins):
                T.claim(pe, l, job)
                settle(pe)
                for o, i in outs_ins:
                    ins = nc.tensor.transpose(o, i, ident[0:i.shape[0], 0:i.shape[0]])
                T.finish(ins)

            def norm(l, which):
                for k in range(KD):
                    job = f"{which}.{k}"
                    if k == 0:
                        pe.wait_ge(s_xn, l * 2 * NT + (NT if which == "norm2" else 0) + TS)
                    o = bank(T, job)
                    transposes(l, job, [(o[:, t * P:(t + 1) * P], xn[:, t, k * P:(k + 1) * P]) for t in range(TS)])
                for i in range(2):
                    job = f"{which}.{KD + i}"
                    if i == 0:
                        pe.wait_ge(s_xn, l * 2 * NT + (NT if which == "norm2" else 0) + NT)
                    o = bank(T, job)
                    transposes(l, job, [(o[:, j * P:(j + 1) * P], xn[:, CTX, (4 * i + j) * P:(4 * i + j + 1) * P]) for j in range(4)])

            def feature_major(l, g):
                w = next_unit(l)
                for c in range(NG):
                    job = f"{g}.{c}"
                    W.claim(pe, l, job)
                    o = bank(W, job)
                    for lo, hi in ((SAMPLE, NTOK), (0, SAMPLE)):
                        for k in range(KD):
                            ins = mm(o[:, lo:hi], w[:, k, c * P:(c + 1) * P], hT[:, k, lo:hi], start=(k == 0), stop=(k == KD - 1))
                    W.finish(ins)

            def token_major(l, g, width=GW, src=hT, jobs=None):
                w = next_unit(l)
                for job, tiles in (jobs or ((f"{g}.s", range(TS)), (f"{g}.p", [CTX]))):
                    W.claim(pe, l, job)
                    o = bank(W, job)
                    for n, t in enumerate(tiles):
                        for k in range(KD):
                            ins = mm(o[:, n * width:(n + 1) * width], src[:, k, t * P:(t + 1) * P], w[:, k, 0:width], start=(k == 0), stop=(k == KD - 1))
                    W.finish(ins)

            def latents(l):
                pe.wait_ge(s_lat, l + 1)
                for c, n in ((0, P), (1, QL - P)):
                    o = bank(T, f"cq.{c}", n)
                    transposes(l, f"cq.{c}", [(o[:, t * P:(t + 1) * P], mla[:, t, c * P:c * P + n]) for t in range(TS)])
                o = bank(T, "cq.p")
                transposes(l, "cq.p", [(o[0:n, c * P:(c + 1) * P], mla[:, CTX, c * P:c * P + n]) for c, n in ((0, P), (1, QL - P))])
                cache = par("cache")
                rows = [ctxt[:, t, :] for t in range(TS)] + [cache, ctxt[:, CTX, :]]
                for name, lo, m in (("ckv", 0, KL), ("kpe", KL + ROPE - QK, QK)):
                    o = bank(T, f"{name}.0", m)
                    transposes(l, f"{name}.0", [(o[:, t * P:(t + 1) * P], rows[t][:, lo:lo + m]) for t in range(TS)])
                    o = bank(T, f"{name}.1", m)
                    transposes(l, f"{name}.1", [(o[:, t * P:(t + 1) * P], rows[TS + t][:, lo:lo + m]) for t in range(2)])

            def mla_q(l):
                wuq = par("wuq", 2, HEADS * QK)
                T.taken(pe, l, "cq.p")
                T.taken(pe, l, "cq.1")
                for j, tiles in enumerate(((0, 1), (2, 3), (4,))):
                    W.claim(pe, l, f"q.{j}")
                    o = bank(W, f"q.{j}")
                    for n, t in enumerate(tiles):
                        mm(o[:, n * 512:n * 512 + HEADS * QK], cqT[:, 0, t * P:(t + 1) * P], wuq[:, 0, :], start=True, stop=False)
                        ins = mm(o[:, n * 512:n * 512 + HEADS * QK], cqT[0:QL - P, 1, t * P:(t + 1) * P], wuq[0:QL - P, 1, :], start=False, stop=True)
                    W.finish(ins)

            def turn_q(l):
                pe.wait_ge(s_qrot, l + 1)
                W.taken(pe, l, "q.2")
                for h in range(HEADS):
                    o = bank(T, f"qh.{h}", QK)
                    transposes(l, f"qh.{h}", [(o[:, t * P:(t + 1) * P], qtok[:, t, h * QK:(h + 1) * QK]) for t in range(TS)])
                o = bank(T, "qh.p", QK)
                transposes(l, "qh.p", [(o[:, h * P:(h + 1) * P], qtok[:, CTX, h * QK:(h + 1) * QK]) for h in range(HEADS)])

            def mla_kv(l):
                wukv = par("wukv", HEADS, 2, NOPE)
                T.taken(pe, l, "ckv.0")
                T.taken(pe, l, "ckv.1")
                for h in range(HEADS):
                    W.claim(pe, l, f"kh.{h}")
                    o = bank(W, f"kh.{h}", NOPE)
                    mm(o[:, 0:512], wukv[:, h, 0, :], ckvT[:, 0:512], start=True, stop=True)
                    W.finish(mm(o[:, 512:NKEY], wukv[:, h, 0, :], ckvT[:, 512:NKEY], start=True, stop=True))
                for j, tiles in enumerate(((0, 1, 2, 3), (4, 5))):
                    W.claim(pe, l, f"v.{j}")
                    o = bank(W, f"v.{j}")
                    for n, t in enumerate(tiles):
                        ins = mm(o[:, n * GW:(n + 1) * GW].rearrange("p (h d) -> p h d", h=HEADS), ckvT[:, t * P:(t + 1) * P], wukv[:, :, 1, :], start=True, stop=True)
                    W.finish(ins)

            def mix(l):
                sgw = par("sgw", HEADS, P)
                pe.wait_ge(s_vn, l + 1)
                for c in range(NG):
                    W.claim(pe, l, f"mix.{c}")
                    o = bank(W, f"mix.{c}")
                    for t in range(NT):
                        for half in range(2):
                            h = 2 * c + half
                            ins = mm(o[half * 64:half * 64 + 64, t * P:(t + 1) * P], vg[:, t, h * 64:(h + 1) * 64], sgw[:, h, :], start=True, stop=True)
                    W.finish(ins)

            def conv_mean(l):
                pe.wait_ge(s_conv, l + 1)
                W.claim(pe, l, "mean")
                o = bank(W, "mean")
                for dst, lo, n in ((0, 0, SAMPLE), (SAMPLE, CPROMPT, PROMPT)):
                    for c in range(NG):
                        ins = mm(o[:, dst:dst + n], mean_w, cacc[:, c, lo:lo + n], start=(c == 0), stop=(c == NG - 1))
                W.finish(ins)

            def conv_var(l):
                pe.wait_ge(s_csq, l + 1)
                N.claim(pe, l, "var")
                o = bank(N, "var")
                for t in range(NT):
                    for c in range(NG):
                        ins = mm(o[:, t:t + 1], csq[:, c, t * P:(t + 1) * P], mean_w[:, 0:1], start=(c == 0), stop=(c == NG - 1))
                N.finish(ins)
                pe.wait_ge(s_crs, l + 1)
                W.claim(pe, l, "cstd")
                o = bank(W, "cstd")
                for t in range(NT):
                    ins = mm(o[:, t * P:(t + 1) * P], crstd[:, t:t + 1].broadcast_to([P, P]), ident, start=True, stop=True)
                W.finish(ins)

            def conv_out(l):
                pw = par("pw", NG, GW)
                pe.wait_ge(s_z, 2 * l + 2)
                for c in range(NG):
                    W.claim(pe, l, f"pw.{c}")
                    o = bank(W, f"pw.{c}")
                    for lo, hi in ((0, SAMPLE), (SAMPLE, NTOK)):
                        for k in range(NG):
                            ins = mm(o[:, lo:hi], pw[:, k, c * P:(c + 1) * P], zT[:, k, lo:hi], start=(k == 0), stop=(k == NG - 1))
                    W.finish(ins)

            def scores(l, i):
                h, t = BLOCKS[i]
                job = f"s.{i}"
                if i == 0:
                    for j in ("qh.3", "qh.p"):
                        T.taken(pe, l, j)
                    for j in ("v.0", "v.1"):
                        W.taken(pe, l, j)
                W.claim(pe, l, job)
                o = bank(W, job)
                if h == "ctx":
                    for h in range(HEADS):
                        ins = mm(o[:, h * P:(h + 1) * P], qhT[:, h, CTX * P:NTOK], khT[0:QK, h, NKEY - P:NKEY], start=True, stop=True)
                else:
                    mm(o[:, 0:512], qhT[:, h, t * P:(t + 1) * P], khT[0:QK, h, 0:512], start=True, stop=True)
                    ins = mm(o[:, 512:640], qhT[:, h, t * P:(t + 1) * P], khT[0:QK, h, 512:640], start=True, stop=True)
                W.finish(ins)

            def turn_probs(l, i):
                pr = prob[:, i % 2, :]
                W.taken(pe, l, f"s.{i}")
                o = bank(T, f"pt.{i}")
                transposes(l, f"pt.{i}", [(o[:, j * P:(j + 1) * P], pr[:, j * P:(j + 1) * P]) for j in range(4)])
                if BLOCKS[i][0] != "ctx":
                    o = bank(T, f"pt.{i}b")
                    transposes(l, f"pt.{i}b", [(o[:, 0:P], pr[:, 4 * P:5 * P])])

            def weigh_values(l, i):
                h, t = BLOCKS[i]
                job = f"pv.{i}"
                T.taken(pe, l, f"pt.{i}")
                if h != "ctx":
                    T.taken(pe, l, f"pt.{i}b")
                N.claim(pe, l, job)
                o = bank(N, job)
                pt = probT[:, i % 2, :]
                if h == "ctx":
                    for h in range(HEADS):
                        ins = mm(o[:, h * 64:(h + 1) * 64], pt[:, h * P:(h + 1) * P], vall[:, 5, h * 64:(h + 1) * 64], start=True, stop=True)
                else:
                    for j in range(5):
                        ins = mm(o[:, 0:64], pt[:, j * P:(j + 1) * P], vall[:, j, h * 64:(h + 1) * 64], start=(j == 0), stop=(j == 4))
                N.finish(ins)

            def turn_rows(l, name, rows):
                for c in range(NG):
                    o = bank(T, f"{name}.{c}")
                    transposes(l, f"{name}.{c}", [(o[:, t * P:(t + 1) * P], rows[:, t, c * P:(c + 1) * P]) for t in range(TS)])
                o = bank(T, f"{name}.p")
                transposes(l, f"{name}.p", [(o[:, c * P:(c + 1) * P], rows[:, CTX, c * P:(c + 1) * P]) for c in range(NG)])

            def turn_k(l):
                W.taken(pe, l, "rk.0")
                W.taken(pe, l, "rk.1")
                for i in range(2):
                    o = bank(T, f"ktok.{i}")
                    transposes(l, f"ktok.{i}", [(o[:, (2 * n + c) * P:(2 * n + c + 1) * P], kT[:, c, (2 * i + n) * P:(2 * i + n + 1) * P])
                                                 for n in range(2) for c in range(NG)])
                o = bank(T, "ktok.p")
                transposes(l, "ktok.p", [(o[:, c * P:(c + 1) * P], kT[:, c, SAMPLE:NTOK]) for c in range(NG)])

            def rows_g1(l):
                N.taken(pe, l, "modc.10")
                N.taken(pe, l, "modc.11")
                for s, job in ((1, "g1.s"), (0, "g1.p")):
                    W.claim(pe, l, job)
                    o = bank(W, job)
                    for k in range(KD):
                        ins = mm(o[:, k * P:(k + 1) * P], modT[:, 2 * KD + k, s:s + 1].broadcast_to([P, P]), ident, start=True, stop=True)
                    W.finish(ins)

            def retention(l):
                pe.wait_ge(s_kdk, 2 * l + 2)
                W.taken(pe, l, "rv.s")
                W.taken(pe, l, "rv.p")
                for t in range(NT):
                    N.claim(pe, l, f"kv.{t}")
                    o = bank(N, f"kv.{t}")
                    dirs = [d for d in range(2) if t == CTX or (t < TS - 1 if d == 0 else t > 0)]
                    for d in dirs:
                        for c in range(NG):
                            for half in range(2):
                                h = 2 * c + half
                                at = (d * NG + c) * 64
                                ins = mm(o[half * 64:half * 64 + 64, at:at + 64], kdk[:, d, t, h * 64:(h + 1) * 64], rv[:, t, h * 64:(h + 1) * 64], start=True, stop=True)
                    N.finish(ins)

                def ret_scores(t):
                    W.claim(pe, l, f"rs.{t}")
                    o = bank(W, f"rs.{t}")
                    for half in range(2):
                        for c in range(NG):
                            p = slice(half * 64, half * 64 + 64)
                            ins = mm(o[:, half * 512 + c * P:half * 512 + (c + 1) * P], kT[p, c, t * P:(t + 1) * P], qT[p, c, t * P:(t + 1) * P], start=True, stop=True)
                    W.finish(ins)

                def ret_out(t):
                    W.taken(pe, l, f"rs.{t}")
                    if t == 0:
                        pe.wait_ge(s_qtd, 2 * l + 2)
                        pe.wait_ge(s_sret, l + 1)
                    W.claim(pe, l, f"ro.{t}")
                    o = bank(W, f"ro.{t}")
                    for half in range(2):
                        for d in range(2):
                            for c in range(NG):
                                h = 2 * c + half
                                p = slice(half * 64, half * 64 + 64)
                                out = o[:, half * 512 + (d * NG + c) * 64:half * 512 + (d * NG + c + 1) * 64]
                                ins = mm(out, sm[:, t % 2, d, half * GW + c * P:half * GW + (c + 1) * P], rv[:, t, h * 64:(h + 1) * 64], start=True, stop=(t == CTX))
                                if t != CTX:
                                    first = t == (0 if d == 0 else TS - 1)
                                    st = par("s0", 2, NG, NOPE)[p, d, c, :] if first else sret[p, t, d, c, :]
                                    ins = mm(out, qTd[p, d, c, t * P:(t + 1) * P], st, start=False, stop=True)
                    W.finish(ins)

                for t in range(NT):
                    ret_scores(t)
                    if t:
                        ret_out(t - 1)
                ret_out(NT - 1)
                pe.wait_ge(s_yc, l + 1)
                turn_rows(l, "yc", yct)

            def out_proj(l):
                for j in ("yc.1", "yc.p"):
                    T.taken(pe, l, j)
                pe.wait_ge(s_mixed, 2 * l + 2)
                for u in range(4):
                    token_major(l, None, src=yT, jobs=((f"o.{u}.s", range(TS)), (f"o.{u}.p", [CTX])))

            def router(l):
                rt = par("router", KD, STRIP)
                T.taken(pe, l, f"norm2.{KD}")
                T.taken(pe, l, f"norm2.{KD + 1}")
                N.claim(pe, l, "logits")
                o = bank(N, "logits")
                for k in range(KD):
                    for t in range(TS):
                        mm(o[t * STRIP:(t + 1) * STRIP, 0:P], rt[:, k, :], hT[:, k, t * P:(t + 1) * P], start=(k == 0), stop=(k == KD - 1))
                for k in range(KD):
                    ins = mm(o[0:STRIP, P:2 * P], rt[:, k, :], hT[:, k, SAMPLE:NTOK], start=(k == 0), stop=(k == KD - 1))
                N.finish(ins)
                N.taken(pe, l, "logits")
                o = bank(T, "logits.t")
                transposes(l, "logits.t", [(o[:, 0:P], lgT[:, 0:P]), (o[:, P:P + STRIP], lgT[0:STRIP, P:2 * P])])

            def choose(l):
                pe.wait_ge(s_aff, l + 1)
                o = bank(T, "afft.s", EXPERTS)
                transposes(l, "afft.s", [(o[:, t * P:(t + 1) * P], aff[:, t, :]) for t in range(TS)])
                o = bank(T, "afft.p", EXPERTS)
                transposes(l, "afft.p", [(o[:, 0:P], aff[:, CTX, :])])

            def turn_slots(l):
                pe.wait_ge(s_slotcode, 2 * l + 2)
                o = bank(T, "slots")
                transposes(l, "slots", [(o[:, t * EXPERTS:(t + 1) * EXPERTS], work[:, t * P:(t + 1) * P]) for t in range(NT)])

            def rows_g2(l):
                W.claim(pe, l, "g2.s")
                o = bank(W, "g2.s")
                for k in range(KD):
                    ins = mm(o[:, k * P:(k + 1) * P], modT[:, 5 * KD + k, 1:2].broadcast_to([P, P]), ident, start=True, stop=True)
                W.finish(ins)
                W.claim(pe, l, "g2.p")
                o = bank(W, "g2.p")
                for j in range(QW // P):
                    for q in range(4):
                        col = modT[:, 5 * KD + q * (QW // P) + j, 0:1].broadcast_to([P, STRIP])
                        ins = mm(o[q * STRIP:(q + 1) * STRIP, j * P:(j + 1) * P], col, ident, start=True, stop=True)
                W.finish(ins)

            def gather(l, e, at, parts):
                for job, i in zip(at, parts):
                    T.claim(pe, l, job, e)
                    o = bank(T, job)
                    if i < 2:
                        for k in range(4):
                            for t in range(TS):
                                ins = mm(o[:, k * P:(k + 1) * P], xn[:, t, (4 * i + k) * P:(4 * i + k + 1) * P], S[:, t].rearrange("p x c -> p (x c)"), start=(t == 0), stop=(t == TS - 1))
                    else:
                        for k in range(KD):
                            ins = mm(o[:, k * STRIP:(k + 1) * STRIP], xn[:, CTX, k * P:(k + 1) * P], Sp.rearrange("p x c -> p (x c)"), start=True, stop=True)
                    T.finish(ins)

            def turn_selection(l, e, n):
                pe.wait_ge(s_weighed, n + 1)
                for job, src in ((FRONT + 2, S), (FRONT + 3, Sw)):
                    T.claim(pe, l, job, e)
                    o = bank(T, job)
                    for t in range(TS):
                        ins = nc.tensor.transpose(o[:, t * P:(t + 1) * P], src[:, t].rearrange("p x c -> p (x c)"), ident)
                    T.finish(ins)
                T.claim(pe, l, FRONT + 4, e)
                T.finish(nc.tensor.transpose(bank(T, FRONT + 4)[:, 0:P], Spw.rearrange("p q x c -> p (q x c)"), ident))

            def gate_up(l, m, i):
                for k in range(KD):
                    pe.wait_ge(s_slot[k], (m + 1) * 32)

                    def lat():
                        for w in range(2):
                            for h in range(2):
                                ins = mm(psW[h * 64:(h + 1) * 64, 0, w * HALFW:(w + 1) * HALFW], xeT[:, k, i, :], ring[:, k, w, h * HALFW:(h + 1) * HALFW], start=(k == 0), stop=(k == KD - 1))
                        return ins

                    def con_():
                        for w in range(2):
                            for q in range(4):
                                ins = mm(psW[q * STRIP:(q + 1) * STRIP, 1, w * QW:(w + 1) * QW], xpT[:, k, 2 * i:2 * i + 2, :].rearrange("p x c -> p (x c)"),
                                         ring[:, k, w, q * QW:(q + 1) * QW], start=(k == 0 and w == 0), stop=(k == KD - 1 and w == 1))
                        return ins

                    for part in ((lat, con_) if k % 2 == 0 else (con_, lat)):
                        ins = part()
                    ins.then_inc(s_gu_used, 1)

            def turn_hidden(l, e, m, at):
                for job, src, n in ((at, hm, HALFW // P), (at + 1, hmp, QW // P)):
                    pe.wait_ge(s_hm, START + 2 * m + 1 + job - at)
                    T.claim(pe, l, job, e)
                    o = bank(T, job)
                    for j in range(n):
                        ins = nc.tensor.transpose(o[:, j * P:(j + 1) * P], src[:, j * P:(j + 1) * P], ident)
                    T.finish(ins)

            def down(l, e, m, i, at):
                for job in (at, at + 1):
                    T.taken(pe, l, job, e)
                for k in range(KF):
                    if k % 2 == 0:
                        pe.wait_ge(s_slot[KD + k // 2], (m + 1) * 16)

                    def lat():
                        h_, j = divmod(k, HALFW // P)
                        for c in range(2):
                            h = c ^ i
                            ins = mm(psN[c * 64:(c + 1) * 64, h, :], hmT[:, j, h_ * 64:(h_ + 1) * 64], ring[:, KD + k // 2, k % 2, h * HALFW:(h + 1) * HALFW], start=(k == 0), stop=(k == KF - 1))
                        return ins

                    def con_():
                        q_, j = divmod(k, QW // P)
                        for q in range(4):
                            ins = mm(psW[q * STRIP:(q + 1) * STRIP, 1, HALFW:HALFW + QW], hmpT[:, j, q_ * STRIP:(q_ + 1) * STRIP], ring[:, KD + k // 2, k % 2, q * QW:(q + 1) * QW],
                                     start=(k == 0 and i == 0), stop=(k == KF - 1 and i == 1))
                        return ins

                    for part in ((lat, con_) if k % 2 == 0 else (con_, lat)):
                        ins = part()
                    if k % 2:
                        ins.then_inc(s_dn_used, 1)

            def combine(l, e, n, turned, at):
                for job in (turned - 1, turned):
                    T.taken(pe, l, job, e)
                for j in range(COMBINE):
                    half, t = divmod(j, NT)
                    if j == 0:
                        pe.wait_ge(s_ye, 4 * n + 4)
                    if j == CTX:
                        pe.wait_ge(s_yep, n + 1)
                    T.claim(pe, l, at + j, e)
                    if t == CTX:
                        p = slice(half * 64, half * 64 + 64)
                        ins = mm(bank(T, at + j), Gp[p, :], yep[p, :], start=True, stop=True)
                    else:
                        ins = mm(bank(T, at + j), G[:, half, t * P:(t + 1) * P], ye[:, half, :], start=True, stop=True)
                    T.finish(ins)

            def pair(l, e, n, first, last):
                for job in ((1, 2) if first else (FRONT + 6, FRONT + 9)):
                    T.taken(pe, l, job if first else job - T_PAIR, e)
                if not first:
                    pe.wait_ge(s_hm, START + 4 * n)
                gate_up(l, 2 * n, 0)
                if not first:
                    combine(l, e, n - 1, FRONT + 4 - T_PAIR, FRONT + 10 - T_PAIR)
                turn_hidden(l, e, 2 * n, FRONT)
                turn_selection(l, e, n)
                down(l, e, 2 * n, 0, FRONT)
                pe.wait_ge(s_hm, START + 4 * n + 2)
                gate_up(l, 2 * n + 1, 1)
                at = FRONT + 5
                if not last:
                    pe.wait_ge(s_S, n + 2)
                    gather(l, e, (at, at + 1), (0, 1))
                    at += 2
                turn_hidden(l, e, 2 * n + 1, at)
                if not last:
                    gather(l, e, (at + 2,), (2,))
                down(l, e, 2 * n + 1, 1, at)
                if last:
                    combine(l, e, n, FRONT + 4, at + 2)

            pe.wait_ge(s_consts, 16)
            pe.wait_ge(s_cond_ready, 1)
            with pe.Fori(0, DEPTH) as l:
                unit_no[0] = 0
                for s in STEPS:
                    kind, _, arg = s.partition(":")
                    if kind == "mod":
                        for which, u in mod_order(*map(int, arg.split("-"))):
                            (mod_unit if which == "mod" else mod_columns)(l, u)
                            if u == MOD_FIRST:
                                pe.wait_ge(s_params, 16 * l + 16)
                    elif kind in ("norm1", "norm2"):
                        norm(l, kind)
                    elif kind == "in":
                        if arg == "mla":
                            for k in range(KD + 2):
                                T.taken(pe, l, f"norm1.{k}") if k >= KD else None
                            token_major(l, None, jobs=(("mla_a.s", range(TS)), ("mla_a.p", [CTX])))
                            token_major(l, None, width=MLA_B, jobs=(("mla_b", range(NT)),))
                        elif arg in TOKEN_MAJOR:
                            token_major(l, arg)
                        else:
                            feature_major(l, arg)
                        if arg == "rk":
                            turn_k(l)
                    elif kind == "latents":
                        latents(l)
                    elif kind == "mla_q":
                        mla_q(l)
                    elif kind == "mla_kv":
                        mla_kv(l)
                        turn_q(l)
                    elif kind == "mix":
                        mix(l)
                    elif kind == "conv_mean":
                        conv_mean(l)
                    elif kind == "conv_var":
                        conv_var(l)
                    elif kind == "conv_out":
                        conv_out(l)
                    elif kind == "att":
                        i = int(arg)
                        scores(l, i)
                        if i > 1:
                            weigh_values(l, i - 2)
                        if i:
                            turn_probs(l, i - 1)
                    elif kind == "att_end":
                        weigh_values(l, len(BLOCKS) - 2)
                        turn_probs(l, len(BLOCKS) - 1)
                        weigh_values(l, len(BLOCKS) - 1)
                        N.taken(pe, l, f"pv.{len(BLOCKS) - 1}")
                        N.taken(pe, l, f"pv.{len(BLOCKS) - 2}")
                        turn_rows(l, "yd", ydt)
                    elif kind == "rows_g1":
                        rows_g1(l)
                    elif kind == "retention":
                        retention(l)
                    elif kind == "out_proj":
                        out_proj(l)
                    elif kind == "router":
                        router(l)
                    elif kind == "rows_g2":
                        rows_g2(l)
                        choose(l)
                        turn_slots(l)
                for R, jobs in RINGS:
                    if "spare" in R.at:
                        R.claim(pe, l, "spare")
                        R.finish(mm(bank(R, "spare")[:, 0:2], ident, ident[:, 0:2], start=True, stop=True))
                n0 = l * PAIRS
                pe.wait_ge(s_S, n0 + 1)
                gather(l, 0, range(GATHERED), range(GATHERED))
                for j in ("g2.s", "g2.p"):
                    W.taken(pe, l, j)
                pair(l, 0, n0, True, False)
                with pe.Fori(1, PAIRS - 1) as e:
                    pair(l, e, n0 + e, False, False)
                pair(l, PAIRS - 1, n0 + PAIRS - 1, False, True)

        @block.scalar
        def _(act):
            A = nc.scalar.activation
            def out(R, l, job, dst, src, func=ACT.Identity, **kw):
                R.wait(act, l, job)
                R.take(A(dst, src, func, **kw), job)

            def norm_squares(n):
                for t in range(NT):
                    ins = A(xn[:, t, :], x[:, t, :], ACT.Square, accum_out=ss[:, t:t + 1])
                ins.then_inc(s_sq, 1)
                act.wait_ge(s_sq, n + 1)
                A(std, ss, ACT.Sqrt, scale=1.0 / D, bias=con("eps")).then_inc(s_std, 1)

            def norm_out(l, which, scale, shift):
                act.wait_ge(s_scale, 2 * l + (2 if which == "norm2" else 1))
                for k in range(0, KD, 2):
                    out(T, l, f"{which}.{k}", hT[:, k, 0:SAMPLE], bank(T, f"{which}.{k}"), scale=scale[:, k, 1:2], bias=shift[:, k, 1:2])
                job = f"{which}.{KD}"
                T.wait(act, l, job)
                for k in range(4):
                    ins = A(hT[:, k, SAMPLE:NTOK], bank(T, job)[:, k * P:(k + 1) * P], ACT.Identity, scale=scale[:, k, 0:1], bias=shift[:, k, 0:1])
                T.take(ins, job)

            def mod_rows_out(l, u):
                out(N, l, f"mod.{u}", mod_rows[:, u % 2, :], bank(N, f"mod.{u}")[:, 0:GW])

            def mod_out(l, u):
                job = f"modc.{u}"
                N.wait(act, l, job)
                for c in range(NG):
                    j = NG * u + c
                    ins = A(modT[:, j, :], bank(N, job)[:, 2 * c:2 * c + 2], ACT.Identity, bias=par("bmod")[:, j:j + 1])
                N.take(ins, job)

            def rows_out(l, g, dst, func=ACT.Identity):
                out(W, l, f"{g}.s", dst[:, 0:TS, :], bank(W, f"{g}.s").rearrange("p (t n) -> p t n", t=TS), func)
                out(W, l, f"{g}.p", dst[:, CTX, :], bank(W, f"{g}.p")[:, 0:GW], func)

            def turned_rows_out(l, name, chunk, gain=None):
                for c in range(NG):
                    kw = {} if gain is None else dict(scale=gain[:, c:c + 1])
                    out(T, l, f"{name}.{c}", yT[:, chunk + c, 0:SAMPLE], bank(T, f"{name}.{c}"), **kw)
                T.wait(act, l, f"{name}.p")
                for c in range(NG):
                    kw = {} if gain is None else dict(scale=gain[:, c:c + 1])
                    ins = A(yT[:, chunk + c, SAMPLE:NTOK], bank(T, f"{name}.p")[:, c * P:(c + 1) * P], ACT.Identity, **kw)
                T.take(ins, f"{name}.p")

            def decays(l):
                A(lgt[:, 0, :], par("dec"), ACT.Exp, scale=float(np.log(2.0))).then_inc(s_dexp, 1)
                act.wait_ge(s_dec, l + 1)
                A(lgt[:, 4, :], lgt[:, 1, :], ACT.Ln).then_inc(s_dlog, 1)

            def ret_tables(l):
                act.wait_ge(s_lg, l + 1)
                lg = lgt[:, 5, :]
                A(kd, kd, ACT.Exp)
                A(cdec.rearrange("p a b -> p (a b)"), lg[:, 8:12], ACT.Exp, scale=float(P))
                for d in range(2):
                    for c in range(NG):
                        for half in range(2):
                            h = 2 * c + half
                            A(masks[:, d, half, c * P:(c + 1) * P], con("expo", 2, P)[:, d, :], ACT.Exp, scale=lg[:, d * HEADS + h:d * HEADS + h + 1])
                        ins = A(qdec[:, d, c, :], con("qpos", 2, P)[:, d, :], ACT.Exp, scale=lg[:, 8 + NG * d + c:9 + NG * d + c])
                ins.then_inc(s_tab, 1)

            def softmax_exp(l, i):
                h, t = BLOCKS[i]
                job = f"s.{i}"
                act.wait_ge(s_nmax, l * len(BLOCKS) + i + 1)
                if i >= 2:
                    T.wait(act, l, f"pt.{i - 2}b")
                o = bank(W, job)
                if h == "ctx":
                    for h in range(HEADS):
                        ins = A(prob[:, i % 2, h * P:(h + 1) * P], o[:, h * P:(h + 1) * P], ACT.Exp, scale=ATT_SCALE, bias=nmax[:, i % 2, h:h + 1], accum_out=rsum[:, i % 2, h:h + 1])
                else:
                    ins = A(prob[:, i % 2, :], o[:, 0:NTOK], ACT.Exp, scale=ATT_SCALE, bias=nmax[:, i % 2, 0:1], accum_out=rsum[:, i % 2, 0:1])
                W.take(ins, job)

            def last_prob_out(l, i):
                if BLOCKS[i][0] == "ctx":
                    return
                if i >= 2:
                    N.wait(act, l, f"pv.{i - 2}")
                out(T, l, f"pt.{i}b", probT[:, i % 2, 4 * P:5 * P], bank(T, f"pt.{i}b")[:, 0:P])

            act.wait_ge(s_cond, 16)
            A(sT.rearrange("p k s -> p (k s)"), sT.rearrange("p k s -> p (k s)"), ACT.Silu).then_inc(s_cond_ready, 1)
            act.wait_ge(s_consts, 16)
            act.wait_ge(s_x, 32)
            with act.Fori(0, DEPTH) as l:
                T.layers_taken(act, l)
                norm_squares(2 * l)
                act.wait_ge(s_params, 16 * l + 16)
                decays(l)
                for s in STEPS:
                    kind, _, arg = s.partition(":")
                    if kind == "mod":
                        for which, u in mod_order(*map(int, arg.split("-"))):
                            (mod_rows_out if which == "mod" else mod_out)(l, u)
                    elif kind == "norm1":
                        norm_out(l, "norm1", A1, modT[:, 0:KD, :])
                    elif kind == "in":
                        if arg == "mla":
                            out(W, l, "mla_a.s", mla[:, 0:TS, 0:GW], bank(W, "mla_a.s").rearrange("p (t n) -> p t n", t=TS))
                            out(W, l, "mla_a.p", mla[:, CTX, 0:GW], bank(W, "mla_a.p")[:, 0:GW])
                            out(W, l, "mla_b", mla[:, :, GW:MLA_IN], bank(W, "mla_b")[:, 0:NT * MLA_B].rearrange("p (t n) -> p t n", t=NT))
                        elif arg == "ca":
                            for c in range(NG):
                                job = f"ca.{c}"
                                W.wait(act, l, job)
                                A(glu[:, c, PAD:PAD + SAMPLE], bank(W, job)[:, 0:SAMPLE], ACT.Identity)
                                W.take(A(glu[:, c, CPROMPT + PAD:CPROMPT + PAD + PROMPT], bank(W, job)[:, SAMPLE:NTOK], ACT.Identity), job)
                        elif arg == "cg":
                            for c in range(NG):
                                out(W, l, f"cg.{c}", cscr[:, c, :], bank(W, f"cg.{c}")[:, 0:NTOK], ACT.Sigmoid)
                        elif arg in ("u", "rq", "rk"):
                            dst = dict(u=uT, rq=qT, rk=kT)[arg]
                            for c in range(NG):
                                out(W, l, f"{arg}.{c}", dst[:, c, :], bank(W, f"{arg}.{c}")[:, 0:NTOK])
                            if arg == "rk":
                                for i in range(2):
                                    out(T, l, f"ktok.{i}", ktok[:, 2 * i:2 * i + 2, :], bank(T, f"ktok.{i}").rearrange("p (t n) -> p t n", t=2))
                                out(T, l, "ktok.p", ktok[:, CTX, :], bank(T, "ktok.p")[:, 0:GW])
                        elif arg == "vg":
                            rows_out(l, "vg", vg)
                            act.wait_ge(s_vss, l + 1)
                            A(vstd, vss, ACT.Sqrt, scale=1.0 / GW, bias=con("eps")).then_inc(s_vstd, 1)
                        elif arg == "rv":
                            rows_out(l, "rv", rv)
                        elif arg in ("rgf", "rgb"):
                            rows_out(l, arg, gates[:, int(arg == "rgb")], ACT.Silu)
                        if arg == "mla":
                            act.wait_ge(s_mss, l + 1)
                            A(mstd[:, 0, :], mss[:, 0, :], ACT.Sqrt, scale=1.0 / QL, bias=con("eps"))
                            A(mstd[:, 1, :], mss[:, 1, :], ACT.Sqrt, scale=1.0 / KL, bias=con("eps")).then_inc(s_mstd, 1)
                    elif kind == "latents":
                        act.wait_ge(s_lat, l + 1)
                        act.dma_start(io["new_ckv"][0, bass.ds(l, 1)].rearrange("l p n -> (l p) n"), ctxt[:, CTX, 0:KL]).then_inc(s_ctx_out, 16)
                        act.dma_start(io["new_kpe"][0, bass.ds(l, 1)].rearrange("l p n -> (l p) n"), ctxt[:, CTX, KL:KL + ROPE]).then_inc(s_ctx_out, 16)
                        out(T, l, "cq.0", cqT[:, 0, 0:SAMPLE], bank(T, "cq.0"))
                        out(T, l, "cq.1", cqT[0:QL - P, 1, 0:SAMPLE], bank(T, "cq.1", QL - P))
                        T.wait(act, l, "cq.p")
                        A(cqT[:, 0, SAMPLE:NTOK], bank(T, "cq.p")[:, 0:P], ACT.Identity)
                        T.take(A(cqT[0:QL - P, 1, SAMPLE:NTOK], bank(T, "cq.p", QL - P)[:, P:2 * P], ACT.Identity), "cq.p")
                        out(T, l, "ckv.0", ckvT[:, 0:512], bank(T, "ckv.0"))
                        out(T, l, "ckv.1", ckvT[:, 512:NKEY], bank(T, "ckv.1")[:, 0:NKEY - 512])
                        for i, (lo, hi) in enumerate(((0, 512), (512, NKEY))):
                            src = bank(T, f"kpe.{i}")[NOPE:QK, 0:hi - lo].unsqueeze(1).broadcast_to([ROPE, HEADS, hi - lo])
                            out(T, l, f"kpe.{i}", khT[NOPE:QK, :, lo:hi], src)
                    elif kind == "mla_q":
                        for j, n in enumerate((2, 2, 1)):
                            src = bank(W, f"q.{j}").rearrange("p (t n) -> p t n", t=2)[:, 0:n, 0:HEADS * QK]
                            out(W, l, f"q.{j}", qtok[:, 2 * j:2 * j + n, :], src)
                    elif kind == "mla_kv":
                        for h in range(HEADS):
                            out(W, l, f"kh.{h}", khT[0:NOPE, h, :], bank(W, f"kh.{h}", NOPE)[:, 0:NKEY])
                        for j, n in enumerate((4, 2)):
                            out(W, l, f"v.{j}", vall[:, 4 * j:4 * j + n, :], bank(W, f"v.{j}")[:, 0:n * GW].rearrange("p (t n) -> p t n", t=n))
                        for h in range(HEADS):
                            out(T, l, f"qh.{h}", qhT[:, h, 0:SAMPLE], bank(T, f"qh.{h}", QK))
                        out(T, l, "qh.p", qhT[:, :, SAMPLE:NTOK], bank(T, "qh.p", QK).rearrange("p (h n) -> p h n", h=HEADS))
                    elif kind == "conv_mean":
                        W.taken(act, l, "mean")
                        A(csq, cscr, ACT.Square).then_inc(s_csq, 1)
                    elif kind == "conv_var":
                        out(N, l, "var", cstd, bank(N, "var")[:, 0:NT], ACT.Sqrt, bias=con("eps"))
                        W.taken(act, l, "cstd")
                        for c in range(NG):
                            A(zT[:, c, :], cscr[:, c, :], ACT.Silu, scale=par("lng")[:, c:c + 1], bias=par("lnb")[:, c:c + 1]).then_inc(s_z, 1)
                    elif kind == "conv_out":
                        for c in range(NG):
                            out(W, l, f"pw.{c}", yT[:, NG + c, :], bank(W, f"pw.{c}")[:, 0:NTOK])
                    elif kind == "ret_tables":
                        ret_tables(l)
                    elif kind == "att":
                        i = int(arg)
                        softmax_exp(l, i)
                        if i:
                            last_prob_out(l, i - 1)
                    elif kind == "att_end":
                        turned_rows_out(l, "yd", 3 * NG)
                    elif kind == "rows_g1":
                        for s_, job in ((1, "g1.s"), (0, "g1.p")):
                            out(W, l, job, g1b[:, s_, :], bank(W, job))
                    elif kind == "retention":
                        for t in range(NT):
                            out(N, l, f"kv.{t}", kvs[:, t], bank(N, f"kv.{t}")[:, 0:2 * NG * NOPE].rearrange("p (d n) -> p d n", d=2)) if t == CTX else None
                            if t != CTX:
                                N.wait(act, l, f"kv.{t}")
                                ds_ = [d for d in range(2) if (t < TS - 1 if d == 0 else t > 0)]
                                lo, hi = ds_[0] * NG * NOPE, (ds_[-1] + 1) * NG * NOPE
                                N.take(A(kvs[:, t].rearrange("p d n -> p (d n)")[:, lo:hi], bank(N, f"kv.{t}")[:, lo:hi], ACT.Identity), f"kv.{t}")
                        N.taken(act, l, f"kv.{CTX}")
                        for d in range(2):
                            dst = io["new_state"][0, bass.ds(l, 1), d].rearrange("l (c f) k e -> (l f k) c e", f=2)
                            act.dma_start(dst, kvs[:, CTX, d].rearrange("p (c e) -> p c e", c=NG)).then_inc(s_st_out, 16)
                        for t in range(NT):
                            out(W, l, f"ro.{t}", otok[:, t, :].rearrange("p (f n) -> p f n", f=2), bank(W, f"ro.{t}").rearrange("p (f n) -> p f n", f=2)[:, :, 0:2 * NG * NOPE])
                            act.wait_ge(s_ocen, l * NT + t + 1)
                            A(osq[:, t, :], otok[:, t, :], ACT.Square).then_inc(s_osq, 1)
                        act.wait_ge(s_ovar, l + 1)
                        A(rdev, rvar, ACT.Sqrt, scale=1.0 / NOPE, bias=con("eps")).then_inc(s_ostd, 1)
                        turned_rows_out(l, "yc", 2 * NG, par("gng"))
                    elif kind == "norm2":
                        act.wait_ge(s_res, 8 * l + 8)
                        norm_squares(2 * l + 1)
                        norm_out(l, "norm2", A2, modT[:, 3 * KD:4 * KD, :])
                    elif kind == "router":
                        N.wait(act, l, "logits")
                        A(lgT[:, 0:P], bank(N, "logits")[:, 0:P], ACT.Identity)
                        N.take(A(lgT[0:STRIP, P:2 * P], bank(N, "logits", STRIP)[:, P:2 * P], ACT.Identity), "logits")
                        T.taken(act, l, "logits.t")
                        A(aff, aff, ACT.Exp).then_inc(s_lexp, 1)
                    elif kind == "rows_g2":
                        out(W, l, "g2.s", g2b, bank(W, "g2.s"))
                        out(W, l, "g2.p", g2q, bank(W, "g2.p")[:, 0:QW])
                        out(T, l, "slots", slotT, bank(T, "slots")[:, 0:NT * EXPERTS].rearrange("p (t e) -> p t e", t=NT))
                for i, (R, jobs) in enumerate(RINGS):
                    if "spare" in R.at:
                        out(R, l, "spare", spare[:, i], bank(R, "spare")[:, 0:2])

                def take_all(e, job, dst, src):
                    T.wait(act, l, job, e)
                    T.take(A(dst, src, ACT.Identity), job)

                def gathered(e, at, parts):
                    scale, shift = A2, modT[:, 3 * KD:4 * KD, :]
                    for job, i in zip(at, parts):
                        T.wait(act, l, job, e)
                        o = bank(T, job)
                        for k in (range(4 * i, 4 * i + 4) if i < 2 else range(KD)):
                            if i < 2:
                                dst, src, s_ = xeT[:, k].rearrange("p x c -> p (x c)"), o[:, (k % 4) * P:(k % 4 + 1) * P], 1
                            else:
                                dst, src, s_ = xpT[:, k, 0:4:3, :], o[:, k * STRIP:(k + 1) * STRIP].rearrange("p (x c) -> p x c", x=2), 0
                            ins = A(dst, src, ACT.Identity, scale=scale[:, k, s_:s_ + 1], bias=shift[:, k, s_:s_ + 1])
                        T.take(ins, job)

                def silu(m):
                    act.wait_ge(s_gu_used, (m + 1) * KD)
                    A(hm, psW[:, 0, 0:HALFW], ACT.Silu).then_inc(s_silu, 1)
                    A(hmp, psW[:, 1, 0:QW], ACT.Silu).then_inc(s_silu, 1)

                def hidden_out(e, at):
                    take_all(e, at, hmT.rearrange("p j c -> p (j c)"), bank(T, at))
                    take_all(e, at + 1, hmpT.rearrange("p j c -> p (j c)"), bank(T, at + 1)[:, 0:QW])

                def pair(e, n, last):
                    silu(2 * n)
                    hidden_out(e, FRONT)
                    for d in range(2):
                        take_all(e, FRONT + 2 + d, G[:, d, :], bank(T, FRONT + 2 + d))
                    take_all(e, FRONT + 4, Gp, bank(T, FRONT + 4)[:, 0:P])
                    silu(2 * n + 1)
                    at = FRONT + 5
                    if not last:
                        gathered(e, (at, at + 1), (0, 1))
                        at += 2
                    hidden_out(e, at)
                    if not last:
                        gathered(e, (at + 2,), (2,))

                act.wait_ge(s_zeros, l + 1)
                gathered(0, range(GATHERED), range(GATHERED))
                with act.Fori(0, PAIRS - 1) as e:
                    pair(e, l * PAIRS + e, False)
                pair(PAIRS - 1, l * PAIRS + PAIRS - 1, True)
            T.layers_taken(act, DEPTH)
            norm_squares(2 * DEPTH)

        @block.vector
        def _(dve):
            V = nc.vector
            chain = Chain(dve, s_dve, DVE_LINKS)
            link, mark = chain.link, chain.mark

            def normalised(l, n, first):
                dve.wait_ge(s_std, n + 1)
                link(V.reciprocal(rstd, std))
                for t in range(NT):
                    V.tensor_scalar(xn[:, t, :], x[:, t, :], rstd[:, t:t + 1], None, ALU.mult).then_inc(s_xn, 1)

            def scales(l, dst, sc, gain):
                V.scalar_tensor_tensor(dst, sc, 1.0, gain.unsqueeze(2).broadcast_to([P, KD, 2]), ALU.add, ALU.mult).then_inc(s_scale, 1)

            def norm_out(l, which, scale, shift):
                dve.wait_ge(s_scale, 2 * l + (2 if which == "norm2" else 1))
                for k in range(1, KD, 2):
                    job = f"{which}.{k}"
                    T.wait(dve, l, job)
                    T.take(V.tensor_scalar(hT[:, k, 0:SAMPLE], bank(T, job), scale[:, k, 1:2], shift[:, k, 1:2], ALU.mult, ALU.add), job)
                job = f"{which}.{KD + 1}"
                T.wait(dve, l, job)
                for k in range(4):
                    ins = V.tensor_scalar(hT[:, 4 + k, SAMPLE:NTOK], bank(T, job)[:, k * P:(k + 1) * P], scale[:, 4 + k, 0:1], shift[:, 4 + k, 0:1], ALU.mult, ALU.add)
                T.take(ins, job)

            def decays(l):
                dve.wait_ge(s_dexp, l + 1)
                y, u, d, z, ln, lg = (lgt[:, i, :] for i in range(6))
                V.tensor_scalar(u, y, -1.0, 1.0, ALU.mult, ALU.add).then_inc(s_dec, 1)
                dve.wait_ge(s_dec, l + 1)
                link(V.tensor_scalar(d, u, -1.0, None, ALU.add))
                link(V.tensor_scalar(z, d, 0.0, None, ALU.is_equal))
                link(V.tensor_tensor(d, d, z, ALU.subtract))
                link(V.reciprocal(d, d))
                dve.wait_ge(s_dlog, l + 1)
                link(V.tensor_tensor(d, d, ln, ALU.mult))
                link(V.tensor_tensor(d, d, z, ALU.add))
                link(V.scalar_tensor_tensor(lg, y, -1.0, d, ALU.mult, ALU.mult))
                V.tensor_scalar(kd[:, 0:HEADS], lg[:, 0:HEADS], con("kpos")[:, 0:1], None, ALU.mult)
                V.tensor_scalar(kd[:, HEADS:2 * HEADS], lg[:, HEADS:2 * HEADS], con("kpos")[:, 1:2], None, ALU.mult).then_inc(s_lg, 1)

            def latents(l):
                W.taken(dve, l, "mla_a.p")
                W.taken(dve, l, "mla_b")
                link(V.tensor_tensor(lat_sq, mla[:, :, 0:QL + KL], mla[:, :, 0:QL + KL], ALU.mult))
                V.tensor_reduce(mss[:, 0, :], lat_sq[:, :, 0:QL], AX.X, ALU.add)
                V.tensor_reduce(mss[:, 1, :], lat_sq[:, :, QL:QL + KL], AX.X, ALU.add).then_inc(s_mss, 1)
                kp = mla[:, 0:TS, QL + KL:MLA_IN]
                kpv = kp.rearrange("p t (a b e) -> p t a b e", a=2, b=2)
                sinv = con("sin", TS, ROPE).rearrange("p t (a b e) -> p t a b e", a=2, b=2)
                rot = rot_k.rearrange("p t (a b e) -> p t a b e", a=2, b=2)
                for b in range(2):
                    V.tensor_tensor(rot[:, :, :, b, :], kpv[:, :, :, 1 - b, :], sinv[:, :, :, b, :], ALU.mult)
                link(V.tensor_tensor(ctxt[:, 0:TS, KL:KL + ROPE], kp, con("cos", TS, ROPE), ALU.mult))
                V.tensor_tensor(ctxt[:, 0:TS, KL:KL + ROPE], ctxt[:, 0:TS, KL:KL + ROPE], rot_k, ALU.add)
                V.tensor_copy(ctxt[:, CTX, KL:KL + ROPE], mla[:, CTX, QL + KL:MLA_IN])
                dve.wait_ge(s_mstd, l + 1)
                link(V.reciprocal(mrstd, mstd))
                V.tensor_tensor(mla[:, :, 0:QL], mla[:, :, 0:QL], mrstd[:, 0, :].unsqueeze(2).broadcast_to([P, NT, QL]), ALU.mult)
                link(V.tensor_tensor(ctxt[:, :, 0:KL], mla[:, :, QL:QL + KL], mrstd[:, 1, :].unsqueeze(2).broadcast_to([P, NT, KL]), ALU.mult))
                V.tensor_tensor(mla[:, :, 0:QL], mla[:, :, 0:QL], par("qg").unsqueeze(1).broadcast_to([P, NT, QL]), ALU.mult)
                V.tensor_tensor(ctxt[:, :, 0:KL], ctxt[:, :, 0:KL], par("kvg").unsqueeze(1).broadcast_to([P, NT, KL]), ALU.mult).then_inc(s_lat, 1)

            def rotate_queries(l):
                W.taken(dve, l, "q.0")
                W.taken(dve, l, "q.1")
                q = carve(ring_r, KT0, TS, HEADS, QK)[:, :, :, NOPE:QK]
                shape = [P, TS, HEADS, ROPE // 4]
                for i in range(4):
                    lo, other = i * (ROPE // 4), (i ^ 1) * (ROPE // 4)
                    sin = con("sin", TS, ROPE)[:, :, lo:lo + ROPE // 4].unsqueeze(2).broadcast_to(shape)
                    ins = V.tensor_tensor(rot_q[:, :, :, lo:lo + ROPE // 4], q[:, :, :, other:other + ROPE // 4], sin, ALU.mult)
                link(ins)
                link(V.tensor_tensor(q, q, con("cos", TS, ROPE).unsqueeze(2).broadcast_to([P, TS, HEADS, ROPE]), ALU.mult))
                V.tensor_tensor(q, q, rot_q, ALU.add).then_inc(s_qrot, 1)

            def gate_conv(l):
                for c in range(NG):
                    W.taken(dve, l, f"cg.{c}")
                    for lo, n, at in ((PAD, SAMPLE, 0), (CPROMPT + PAD, PROMPT, SAMPLE)):
                        ins = V.tensor_tensor(glu[:, c, lo:lo + n], glu[:, c, lo:lo + n], cscr[:, c, at:at + n], ALU.mult)
                link(ins)

            def taps(l):
                dve.wait_ge(s_pads, l + 1)
                w = par("convw", NG, TAPS)
                last = [0, 0]
                for k in range(TAPS):
                    for c in range(NG):
                        src = glu[:, c, k:k + CVAL]
                        if k == 0:
                            last[c] = mark(V.tensor_scalar(cacc[:, c, :], src, w[:, c, 0:1], par("convb")[:, c:c + 1], ALU.mult, ALU.add))
                            continue
                        chain.wait(last[c])
                        ins = V.scalar_tensor_tensor(cacc[:, c, :], src, w[:, c, k:k + 1], cacc[:, c, :], ALU.mult, ALU.add)
                        if k == TAPS - 1 and c == NG - 1:
                            ins.then_inc(s_conv, 1)
                        else:
                            last[c] = mark(ins)

            def spatial_norm(l):
                W.taken(dve, l, "vg.s")
                W.taken(dve, l, "vg.p")
                sq = carve(ring_r, KT0 + NG * NTOK, NT, GW)
                T.wait(dve, l, "qh.p")
                link(V.tensor_tensor(sq, vg, vg, ALU.mult))
                V.tensor_reduce(vss, sq, AX.X, ALU.add).then_inc(s_vss, 1)
                dve.wait_ge(s_vstd, l + 1)
                link(V.reciprocal(vrstd, vstd))
                V.tensor_tensor(vg, vg, vrstd.unsqueeze(2).broadcast_to([P, NT, GW]), ALU.mult).then_inc(s_vn, 1)

            def conv_centre(l):
                W.wait(dve, l, "mean")
                o = bank(W, "mean")
                V.tensor_tensor(cscr[:, :, 0:SAMPLE], cacc[:, :, 0:SAMPLE], o[:, 0:SAMPLE].unsqueeze(1).broadcast_to([P, NG, SAMPLE]), ALU.subtract)
                W.take(V.tensor_tensor(cscr[:, :, SAMPLE:NTOK], cacc[:, :, CPROMPT:CPROMPT + PROMPT], o[:, SAMPLE:NTOK].unsqueeze(1).broadcast_to([P, NG, PROMPT]), ALU.subtract), "mean")

            def conv_normalise(l):
                N.taken(dve, l, "var")
                V.reciprocal(crstd, cstd).then_inc(s_crs, 1)
                W.wait(dve, l, "cstd")
                W.take(V.tensor_tensor(cscr, cscr, bank(W, "cstd")[:, 0:NTOK].unsqueeze(1).broadcast_to([P, NG, NTOK]), ALU.mult), "cstd")

            def mix_out(l):
                sgb = par("sgb", NG, P)
                W.taken(dve, l, "u.0")
                W.taken(dve, l, "u.1")
                for c in range(NG):
                    job = f"mix.{c}"
                    W.wait(dve, l, job)
                    src = bank(W, job)[:, 0:NTOK].rearrange("p (t n) -> p t n", t=NT)
                    dst = yT[:, c, :].rearrange("p (t n) -> p t n", t=NT)
                    W.take(V.scalar_tensor_tensor(dst, src, par("sgg")[:, c:c + 1], sgb[:, c, :].unsqueeze(1).broadcast_to([P, NT, P]), ALU.mult, ALU.add), job)
                for c in range(NG):
                    W.taken(dve, l, f"mix.{c}")
                    V.tensor_tensor(yT[:, c, :], yT[:, c, :], uT[:, c, :], ALU.mult).then_inc(s_mixed, 1)

            def score_max(l, i):
                h, t = BLOCKS[i]
                W.wait(dve, l, f"s.{i}")
                o = bank(W, f"s.{i}")
                nh = HEADS if h == "ctx" else 1
                src = o[:, 0:HEADS * P].rearrange("p (h n) -> p h n", h=HEADS) if h == "ctx" else o[:, 0:NTOK]
                link(V.tensor_reduce(nmax[:, i % 2, 0:nh], src, AX.X, ALU.max, negate=True))
                V.tensor_scalar(nmax[:, i % 2, 0:nh], nmax[:, i % 2, 0:nh], ATT_SCALE, None, ALU.mult).then_inc(s_nmax, 1)

            inv_at = {}

            def probs_out(l, i):
                h, t = BLOCKS[i]
                nh = HEADS if h == "ctx" else 1
                W.taken(dve, l, f"s.{i}")
                inv_at[i] = mark(V.reciprocal(rinv[:, i % 2, 0:nh], rsum[:, i % 2, 0:nh]))
                T.wait(dve, l, f"pt.{i}")
                if i >= 2:
                    N.wait(dve, l, f"pv.{i - 2}")
                T.take(V.tensor_copy(probT[:, i % 2, 0:4 * P], bank(T, f"pt.{i}")), f"pt.{i}")

            def values_out(l, i):
                h, t = BLOCKS[i]
                N.wait(dve, l, f"pv.{i}")
                chain.wait(inv_at[i])
                if h == "ctx":
                    src = bank(N, f"pv.{i}")[:, 0:GW].rearrange("p (h n) -> p h n", h=HEADS)
                    ins = V.tensor_tensor(ydt[:, CTX, :].rearrange("p (h n) -> p h n", h=HEADS), src, rinv[:, i % 2, :].unsqueeze(2).broadcast_to([P, HEADS, NOPE]), ALU.mult)
                else:
                    ins = V.tensor_scalar(ydt[:, t, h * NOPE:(h + 1) * NOPE], bank(N, f"pv.{i}")[:, 0:NOPE], rinv[:, i % 2, 0:1], None, ALU.mult)
                N.take(ins, f"pv.{i}")

            def ret_masks(l):
                dve.wait_ge(s_tab, l + 1)
                for d in range(2):
                    v = masks[:, d].rearrange("p f (c n) -> p (f c) n", c=NG)
                    V.tensor_tensor(v, v, con("mask", 2, P)[:, d, :].unsqueeze(1).broadcast_to([P, HEADS, P]), ALU.mult)
                V.tensor_scalar(kd, kd, float(NOPE) ** -0.5, None, ALU.mult).then_inc(s_msk, 1)

            def masked_scores(l, t):
                if t == 0:
                    dve.wait_ge(s_msk, l + 1)
                if t >= 2:
                    W.wait(dve, l, f"ro.{t - 2}")
                job = f"rs.{t}"
                W.wait(dve, l, job)
                src = bank(W, job).rearrange("p (f n) -> p f n", f=2)[:, :, 0:GW]
                for d in range(2):
                    ins = V.tensor_tensor(sm[:, t % 2, d, :].rearrange("p (f n) -> p f n", f=2), src, masks[:, d], ALU.mult)
                W.take(ins, job)

            def states(l):
                for t in range(TS):
                    N.taken(dve, l, f"kv.{t}")
                s0 = par("s0", 2, NG, NOPE)
                for i in range(TS - 1):
                    for d in range(2):
                        t = i if d == 0 else TS - 1 - i
                        nt = t + 1 if d == 0 else t - 1
                        for c in range(NG):
                            old = s0[:, d, c, :] if i == 0 else sret[:, t, d, c, :]
                            ins = V.scalar_tensor_tensor(sret[:, nt, d, c, :], old, cdec[:, d, c:c + 1], kvs[:, t, d, c * NOPE:(c + 1) * NOPE], ALU.mult, ALU.add)
                    if i < TS - 2:
                        link(ins)
                ins.then_inc(s_sret, 1)

            def heads(t):
                return otok[:, t, :].rearrange("p (g e) -> p g e", g=8)

            def centre(l, t):
                W.taken(dve, l, f"ro.{t}")
                link(V.tensor_reduce(rsums[:, t, :], heads(t), AX.X, ALU.add, negate=True))
                V.scalar_tensor_tensor(heads(t), rsums[:, t, :].unsqueeze(2).broadcast_to([P, 8, NOPE]), 1.0 / NOPE, heads(t), ALU.mult, ALU.add).then_inc(s_ocen, 1)

            def variance(l, t):
                dve.wait_ge(s_osq, l * NT + t + 1)
                ins = V.tensor_reduce(rvar[:, t, :], osq[:, t, :].rearrange("p (g e) -> p g e", g=8), AX.X, ALU.add)
                if t == NT - 1:
                    ins.then_inc(s_ovar, 1)

            def retention(l):
                masked_scores(l, 0)
                states(l)
                for t in range(NT):
                    if t + 1 < NT:
                        masked_scores(l, t + 1)
                    centre(l, t)
                    if t:
                        variance(l, t - 1)
                variance(l, NT - 1)
                dve.wait_ge(s_ostd, l + 1)
                link(V.reciprocal(rrstd, rdev))
                marks = []
                for t in range(NT):
                    marks.append(mark(V.tensor_tensor(heads(t), heads(t), rrstd[:, t, :].unsqueeze(2).broadcast_to([P, 8, NOPE]), ALU.mult)))
                for t in range(NT):
                    chain.wait(marks[t])
                    for d in range(2):
                        o = otok[:, t, :].rearrange("p (f d c e) -> p f d c e", f=2, d=2, c=NG)[:, :, d]
                        g = gates[:, d, t, :].rearrange("p (c f e) -> p f c e", c=NG, f=2)
                        ins = V.tensor_tensor(o, o, g, ALU.mult)
                    marks[t] = mark(ins)
                for t in range(NT):
                    chain.wait(marks[t])
                    o = otok[:, t, :].rearrange("p (f d c e) -> p f d c e", f=2, d=2, c=NG)
                    ins = V.tensor_tensor(yct[:, t, :].rearrange("p (c f e) -> p f c e", c=NG, f=2), o[:, :, 0], o[:, :, 1], ALU.add)
                ins.then_inc(s_yc, 1)

            def residual(l):
                W.taken(dve, l, "g1.s")
                W.taken(dve, l, "g1.p")
                for u in range(4):
                    lo, hi = u * GW, (u + 1) * GW
                    for which, s_, tiles, n in (("s", 1, slice(0, TS), TS), ("p", 0, slice(CTX, NT), 1)):
                        job = f"o.{u}.{which}"
                        W.wait(dve, l, job)
                        tmp = (otmp[:, 0:n * GW] if s_ else otmp_p).rearrange("p (t n) -> p t n", t=n)
                        if u:
                            dve.wait_ge(s_res, 8 * l + 2 * u - s_)
                        W.take(V.tensor_tensor(tmp, bank(W, job)[:, 0:n * GW].rearrange("p (t n) -> p t n", t=n), g1b[:, s_, lo:hi].unsqueeze(1).broadcast_to([P, n, GW]), ALU.mult), job)
                        W.taken(dve, l, job)
                        V.tensor_tensor(x[:, tiles, lo:hi], x[:, tiles, lo:hi], tmp, ALU.add).then_inc(s_res, 1)

            def affinity(l):
                T.wait(dve, l, "logits.t")
                lgts = bank(T, "logits.t")[:, 0:NT * STRIP].rearrange("p (t e) -> p t e", t=NT)[:, :, 0:EXPERTS]
                link(V.tensor_reduce(amax, lgts, AX.X, ALU.max))
                T.take(V.tensor_tensor(aff, lgts, amax.unsqueeze(2).broadcast_to([P, NT, EXPERTS]), ALU.subtract), "logits.t")
                dve.wait_ge(s_lexp, l + 1)
                link(V.tensor_reduce(asum, aff, AX.X, ALU.add))
                link(V.reciprocal(arec, asum))
                V.tensor_tensor(aff, aff, arec.unsqueeze(2).broadcast_to([P, NT, EXPERTS]), ALU.mult).then_inc(s_aff, 1)
            def choose(l):
                for job, lo, hi, cap in (("afft.s", 0, SAMPLE, CAPS), ("afft.p", SAMPLE, NTOK, CAPP)):
                    w, c = work[:, lo:hi], cum[:, lo:hi]
                    T.wait(dve, l, job)
                    T.take(V.tensor_copy(w, bank(T, job, EXPERTS)[:, 0:hi - lo]), job)
                    T.taken(dve, l, job)
                    for _ in range(cap // 8):
                        settle(dve)
                        link(V.max(top8[0:EXPERTS, :], w))
                        settle(dve)
                        link(V.match_replace(w, top8[0:EXPERTS, :], w, -1.0))
                    link(V.tensor_scalar(w, w, 0.0, None, ALU.is_lt))
                    link(V.tensor_tensor_scan(c, w, w, 0.0, ALU.add, ALU.max))
                    V.tensor_tensor(w, c, w, ALU.mult).then_inc(s_slotcode, 1)

            def select(l, e):
                code = slotT[:, :, bass.ds(e * 2, 2)]
                V.tensor_tensor(S, con("iota").unsqueeze(1).unsqueeze(1).broadcast_to([P, TS, 2, CAPS]), code[:, 0:TS].unsqueeze(3).broadcast_to([P, TS, 2, CAPS]), ALU.is_equal)
                V.tensor_tensor(Sp, con("iota")[:, 0:CAPP].unsqueeze(1).broadcast_to([P, 2, CAPP]), code[:, CTX].unsqueeze(2).broadcast_to([P, 2, CAPP]), ALU.is_equal).then_inc(s_S, 1)

            def weigh(l, e, n):
                gates_ = aff[:, :, bass.ds(e * 2, 2)]
                for x_ in range(2):
                    V.tensor_tensor(Sw[:, :, x_, :], S[:, :, 1 - x_, :], gates_[:, 0:TS, 1 - x_:2 - x_].broadcast_to([P, TS, CAPS]), ALU.mult).then_inc(s_swap, 1)
                dve.wait_ge(s_swap, 2 * n + 2)
                V.tensor_tensor(S, S, gates_[:, 0:TS].unsqueeze(3).broadcast_to([P, TS, 2, CAPS]), ALU.mult)
                V.tensor_tensor(Spw, Sp.unsqueeze(1).broadcast_to([P, 4, 2, CAPP]), gates_[:, CTX].unsqueeze(1).unsqueeze(3).broadcast_to([P, 4, 2, CAPP]), ALU.mult).then_inc(s_weighed, 1)

            def hidden(m):
                for i, (h, up) in enumerate(((hm, psW[:, 0, HALFW:2 * HALFW]), (hmp, psW[:, 1, QW:2 * QW]))):
                    dve.wait_ge(s_silu, START + 2 * m + i + 1)
                    V.tensor_tensor(h, h, up, ALU.mult).then_inc(s_hm, 1)

            def rows_out(m, i):
                dve.wait_ge(s_dn_used, 4 * m + 4)
                for c in range(2):
                    h = c ^ i
                    p = slice(c * 64, c * 64 + 64)
                    V.tensor_tensor(ye[p, h, :], psN[p, h, :], g2b[p, h * HALFW:(h + 1) * HALFW], ALU.mult).then_inc(s_ye, 1)
                if i:
                    for q in range(4):
                        p = slice(q * STRIP, (q + 1) * STRIP)
                        ins = V.tensor_tensor(yep[p, (q % 2) * QW:(q % 2 + 1) * QW], psW[p, 1, HALFW:HALFW + QW], g2q[p, :], ALU.mult)
                    ins.then_inc(s_yep, 1)

            def combined(l, e, at):
                for j in range(COMBINE):
                    half, t = divmod(j, NT)
                    xs = x[:, t, half * HALFW:(half + 1) * HALFW]
                    T.wait(dve, l, at + j, e)
                    T.take(V.tensor_tensor(xs, xs, bank(T, at + j), ALU.add), at + j)

            def pair(l, e, n, first, last):
                hidden(2 * n)
                if not first:
                    combined(l, e, FRONT + 10 - T_PAIR)
                if not last:
                    T.wait(dve, l, FRONT + 4, e)
                    settle(dve)
                    select(l, e + 1)
                rows_out(2 * n, 0)
                hidden(2 * n + 1)
                if not last:
                    T.wait(dve, l, FRONT + 9, e)
                    settle(dve)
                    weigh(l, e + 1, n + 1)
                rows_out(2 * n + 1, 1)
                if last:
                    combined(l, e, FRONT + 7)

            l_ = [0]
            dve.wait_ge(s_consts, 16)
            dve.wait_ge(s_x, 32)
            with dve.Fori(0, DEPTH) as l:
                l_[0] = l
                chain.start_layer(l)
                normalised(l, 2 * l, True)
                dve.wait_ge(s_params, 16 * l + 16)
                decays(l)
                for s in STEPS:
                    kind, _, arg = s.partition(":")
                    if kind == "norm1":
                        N.taken(dve, l, "modc.6")
                        N.taken(dve, l, "modc.7")
                        scales(l, A1, modT[:, KD:2 * KD, :], par("n1g"))
                        norm_out(l, "norm1", A1, modT[:, 0:KD, :])
                    elif s == "in:mla":
                        latents(l)
                    elif s == "in:cg":
                        gate_conv(l)
                    elif kind == "mla_q":
                        rotate_queries(l)
                    elif kind == "mla_kv":
                        taps(l)
                    elif s == "in:vg":
                        spatial_norm(l)
                    elif kind == "conv_mean":
                        conv_centre(l)
                    elif kind == "conv_var":
                        conv_normalise(l)
                    elif kind == "mix":
                        mix_out(l)
                    elif kind == "ret_tables":
                        ret_masks(l)
                    elif kind == "att":
                        score_max(l, int(arg))
                        if int(arg) > 1:
                            values_out(l, int(arg) - 2)
                        if int(arg):
                            probs_out(l, int(arg) - 1)
                    elif kind == "att_end":
                        values_out(l, len(BLOCKS) - 2)
                        probs_out(l, len(BLOCKS) - 1)
                        values_out(l, len(BLOCKS) - 1)
                    elif kind == "retention":
                        retention(l)
                    elif kind == "out_proj":
                        residual(l)
                    elif kind == "norm2":
                        N.taken(dve, l, "modc.18")
                        N.taken(dve, l, "modc.19")
                        scales(l, A2, modT[:, 4 * KD:5 * KD, :], par("n2g"))
                        normalised(l, 2 * l + 1, False)
                        norm_out(l, "norm2", A2, modT[:, 3 * KD:4 * KD, :])
                    elif kind == "router":
                        affinity(l)
                    elif kind == "rows_g2":
                        choose(l)
                chain.end_layer()
                T.taken(dve, l, "slots")
                dve.wait_ge(s_aff, l + 1)
                settle(dve)
                select(l, 0)
                T.wait(dve, l, GATHERED - 1)
                dve.wait_ge(s_S, l * PAIRS + 1)
                settle(dve)
                weigh(l, 0, l * PAIRS)
                for j in ("g2.s", "g2.p"):
                    W.taken(dve, l, j)
                dve.wait_ge(s_zeros, l + 1)
                settle(dve)
                pair(l, 0, l * PAIRS, True, False)
                with dve.Fori(1, PAIRS - 1) as e:
                    pair(l, e, l * PAIRS + e, False, False)
                pair(l, PAIRS - 1, l * PAIRS + PAIRS - 1, False, True)
            dve.wait_ge(s_std, 2 * DEPTH + 1)
            V.reciprocal(rstd, std).then_inc(s_dve, 1)
            dve.wait_ge(s_dve, DEPTH * DVE_LINKS + 1)
            dve.wait_ge(s_fg, 16)
            for t in range(NT):
                V.scalar_tensor_tensor(xn[:, t, :], x[:, t, :], rstd[:, t:t + 1], stream_r[:, 0:D], ALU.mult, ALU.mult).then_inc(s_y, 1)

        @block.gpsimd
        def _(pool):
            Q = nc.gpsimd

            with pool.Fori(0, DEPTH) as l:
                W.wait(pool, l, "mla_a.s")
                settle(pool)
                for c in range(NG):
                    for lo, n in ((0, PAD), (PAD + SAMPLE, 2 * PAD), (CROW - PAD, PAD)):
                        ins = Q.memset(glu[:, c, lo:lo + n], 0.0)
                ins.then_inc(s_pads, 1)
                pool.wait_ge(s_tab, l + 1)
                W.wait(pool, l, "rgb.p")
                for d in range(2):
                    Q.tensor_tensor(qTd[:, d].rearrange("p c (t n) -> p c t n", t=TS), qT[:, :, 0:SAMPLE].rearrange("p c (t n) -> p c t n", t=TS),
                                    qdec[:, d].unsqueeze(2).broadcast_to([P, NG, TS, P]), ALU.mult).then_inc(s_qtd, 1)
                W.wait(pool, l, f"s.{len(BLOCKS) - 1}")
                pool.wait_ge(s_msk, l + 1)
                for j in ("ktok.1", "ktok.p"):
                    T.taken(pool, l, j)
                for d in range(2):
                    Q.tensor_tensor(kdk[:, d].rearrange("p t (h n) -> p t h n", h=HEADS), ktok.rearrange("p t (h n) -> p t h n", h=HEADS),
                                    kd[:, d * HEADS:(d + 1) * HEADS].unsqueeze(1).unsqueeze(3).broadcast_to([P, NT, HEADS, NOPE]), ALU.mult).then_inc(s_kdk, 1)
                T.wait(pool, l, "slots")
                settle(pool)
                Q.memset(zeroed, 0.0).then_inc(s_zeros, 1)


_OUT_SHAPES = (("y_prompt", (1, PROMPT, D)), ("y_sample", (1, SAMPLE, D)), ("new_ckv", (1, DEPTH, P, KL)),
               ("new_kpe", (1, DEPTH, P, ROPE)), ("new_state", (1, DEPTH, 2, HEADS, NOPE, NOPE)))
_BIG = ("x_prompt", "x_sample", "w_mod", "w_in", "w_out", "w_gate", "w_up", "w_down")


def _constants():
    c = np.zeros((P, NCONST), np.float32)

    def put(name, v):
        lo, hi = CAT[name]
        c[:, lo:hi] = np.asarray(v, np.float32).reshape(-1, hi - lo)

    j, i = np.arange(P)[:, None], np.arange(P)[None, :]
    put("ident", np.eye(P))
    put("mean", np.full((P, P), 1.0 / GW))
    put("expo", np.concatenate([np.maximum(i - j, 0), np.maximum(j - i, 0)], 1))
    put("mask", np.concatenate([i >= j, j >= i], 1) * float(NOPE) ** -0.5)
    put("qpos", np.concatenate([np.tile(i + 1, (P, 1)), np.tile(P - i, (P, 1))], 1))
    put("kpos", np.concatenate([P - 1 - j, j], 1))
    tok = np.arange(SAMPLE)
    inv = (np.float32(10000.0) ** (-np.arange(0, ROPE // 2, 2, dtype=np.float32) / np.float32(ROPE // 2))).astype(np.float32)
    ra, ca = ((v.astype(np.float32)[:, None] * inv) for v in (tok // 64, tok % 64))
    ang = np.concatenate([ra, ra, ca, ca], 1).reshape(TS, P, ROPE).transpose(1, 0, 2)
    sign = np.repeat(np.array([-1.0, 1.0, -1.0, 1.0], np.float32), ROPE // 4)
    put("cos", np.cos(ang))
    put("sin", np.sin(ang) * sign)
    put("iota", np.tile(np.arange(1, CAPS + 1), (P, 1)))
    put("strips", np.tile(np.eye(STRIP)[:, 0:2], (P // STRIP, 1)))
    put("eps", np.full((P, 1), EPS))
    return c


def _params(a):
    out = np.zeros((DEPTH, P, NPARAM), np.float32)

    def put(name, v, rows=slice(0, P), cols=None):
        lo, hi = PAT[name]
        lo, hi = (lo, hi) if cols is None else (lo + cols[0], lo + cols[1])
        out[:, rows, lo:hi] = v.reshape(DEPTH, -1, hi - lo)

    def columns(v):
        return v.reshape(DEPTH, -1, P).transpose(0, 2, 1)

    def everywhere(v):
        return np.repeat(v.reshape(DEPTH, 1, -1), P, axis=1)

    for name, key in (("n1g", "norm1_g"), ("n2g", "norm2_g"), ("bmod", "b_mod"), ("sgg", "sg_norm_g"), ("convb", "conv_b"),
                      ("lng", "conv_ln_g"), ("lnb", "conv_ln_b"), ("gng", "ret_gn_g")):
        put(name, columns(a[key]))
    rt = np.zeros((DEPTH, P, KD, STRIP), np.float32)
    rt[..., 0:EXPERTS] = a["router"].reshape(DEPTH, KD, P, EXPERTS).transpose(0, 2, 1, 3)
    put("router", rt)
    df, db = a["ret_decay_f"], a["ret_decay_b"]
    put("dec", everywhere(df), cols=(0, 4))
    put("dec", everywhere(db), cols=(4, 8))
    for half in range(2):
        rows = slice(64 * half, 64 * half + 64)
        put("dec", everywhere(df[:, half::2])[:, :64], rows, (8, 10))
        put("dec", everywhere(db[:, half::2])[:, :64], rows, (10, 12))
        put("sgb", everywhere(a["sg_b"][:, half::2])[:, :64], rows)
    put("convw", a["conv_w"].reshape(DEPTH, TAPS, NG, P).transpose(0, 3, 2, 1))
    put("sgw", a["sg_w"].transpose(0, 3, 1, 2))
    put("pw", a["conv_pw"].reshape(DEPTH, NG, P, GW).transpose(0, 2, 1, 3))
    put("qg", everywhere(a["q_norm_g"]))
    put("kvg", everywhere(a["kv_norm_g"]))
    put("wuq", a["w_uq"][:, 0:P], cols=(0, HEADS * QK))
    put("wuq", a["w_uq"][:, P:QL], slice(0, QL - P), (HEADS * QK, 2 * HEADS * QK))
    put("wukv", a["w_ukv"])
    put("cache", a["cache_mla_ckv"][0], cols=(0, KL))
    put("cache", a["cache_mla_kpe"][0], cols=(KL, KL + ROPE))
    put("s0", a["state_ret"][0].reshape(DEPTH, 2, NG, P, NOPE).transpose(0, 3, 1, 2, 4))
    return out


def kernel(**inputs):
    import concourse.bacc as bacc
    from concourse.bass_utils import run_bass_kernel_spmd

    a = {k: np.ascontiguousarray(v) for k, v in inputs.items()}
    arrays = {k: a[k] for k in _BIG}
    cond = np.zeros((P, KD, STRIP), np.float32)
    cond[:, :, 0:2] = np.stack([a["c_ctx"], a["c"][0]]).reshape(2, KD, P).transpose(2, 1, 0)
    arrays["cond"] = cond.reshape(P, KD * STRIP)
    arrays["params"], arrays["consts"] = _params(a), _constants()
    arrays["final_g"] = a["final_norm_g"]
    nc = bacc.Bacc("TRN2", target_bir_lowering=False, num_devices=1)
    io = {k: nc.dram_tensor(k, v.shape, F32, kind="ExternalInput").ap() for k, v in arrays.items()}
    for name, shape in _OUT_SHAPES:
        io[name] = nc.dram_tensor(name, shape, F32, kind="ExternalOutput").ap()
    build(nc, io)
    r = run_bass_kernel_spmd(nc, [arrays], core_ids=[0])
    return tuple(r.results[0][name] for name, _ in _OUT_SHAPES)
```

```python
from contextlib import ExitStack

import concourse.bass as bass
from concourse import mybir
import numpy as np

F32 = mybir.dt.float32
ALU = mybir.AluOpType
ACT = mybir.ActivationFunctionType
AX = mybir.AxisListType

P = 128
D = 1024
KD = D // P
DEPTH = 2
TS, TP = 4, 1
NT = TS + TP
CTX = TS
NTOK = NT * P
NKEY = NTOK + P
SAMPLE, PROMPT = TS * P, TP * P
HEADS = 4
GW = 256
NG = GW // P
TAPS = 31
PAD = TAPS // 2
CROW = SAMPLE + PROMPT + 4 * PAD
CVAL = CROW - 2 * PAD
CPROMPT = SAMPLE + 2 * PAD
QL, KL, ROPE, NOPE, QK = 192, 128, 32, 64, 96
MLA_IN = QL + KL + ROPE
EXPERTS, FF = 16, 1024
KF = FF // P
CAPS, CAPP = 64, 16
PAIRS = EXPERTS // 2
HALFW = 512
QW = 256
STRIP = 32
ACT_TILES = 2
EPS = 1e-6
ATT_SCALE = float(QK) ** -0.5

IN_AT = dict(u=0, vg=256, ca=512, cg=768, rq=1024, rk=1280, rv=1536, rgf=1792, rgb=2048, mla_a=2304, mla_b=2560)
MLA_B = QL + KL + ROPE - GW

MOD_FIRST, MOD_UNITS = 8, 24

BLOCKS = [(h, t) for h in range(HEADS) for t in range(TS)] + [("ctx", CTX)]
BLOCKS_AFTER = {"rq": 3, "rk": 3, "rv": 3, "rgf": 3, "rgb": 5}

STEPS = ["norm1", "in:mla", "mod:8-9", "in:ca", "mod:9-10", "in:cg", "mod:10-11", "latents", "mla_q", "mla_kv",
         "in:u", "mod:11-12", "in:vg", "mod:12-13"]
_b = 0
for _n, _g in enumerate(["rq", "rk", "rv", "rgf", "rgb"]):
    STEPS += [f"in:{_g}", f"mod:{13 + _n}-{14 + _n}"]
    STEPS += {"rq": ["conv_mean", "mix"], "rk": ["conv_var"], "rv": ["conv_out"]}.get(_g, [])
    STEPS += [f"att:{_i}" for _i in range(_b, _b + BLOCKS_AFTER[_g])] + (["ret_tables"] if _g == "rv" else [])
    _b += BLOCKS_AFTER[_g]
STEPS += ["att_end", "rows_g1", "retention", "out:0", "mod:18-19", "out:1", "mod:19-20", "out:2", "out:3", "mod:20-24", "norm2", "router", "rows_g2", f"mod:0-{MOD_FIRST}"]

UNITS = []
for _s in STEPS:
    _k, _, _a = _s.partition(":")
    if _k == "mod":
        UNITS += [("mod", _i) for _i in range(*map(int, _a.split("-")))]
    elif _k == "in":
        UNITS += [("in", _g) for _g in (["mla_a", "mla_b"] if _a == "mla" else [_a])]
    elif _k == "out":
        UNITS += [("out", int(_a))]
NSTREAM = 3
NUNIT = len(UNITS)
NLAYER = NUNIT - MOD_FIRST
assert NUNIT % NSTREAM == 0 and UNITS[NLAYER:] == [("mod", u) for u in range(MOD_FIRST)]

def mod_order(lo, hi):
    out = []
    for u in range(lo, hi):
        out.append(("mod", u))
        if u not in (0, MOD_FIRST):
            out.append(("modc", u - 1))
        if u in (MOD_FIRST - 1, MOD_UNITS - 1):
            out.append(("modc", u))
    return out


TOKEN_MAJOR = ("vg", "rv", "rgf", "rgb")
W_JOBS, T_JOBS, N_JOBS = [], [], []
for _s in STEPS:
    _k, _, _a = _s.partition(":")
    if _k == "mod":
        N_JOBS += [f"{_j}.{_i}" for _j, _i in mod_order(*map(int, _a.split("-")))]
    elif _k in ("norm1", "norm2"):
        T_JOBS += [f"{_k}.{i}" for i in range(KD + 2)]
    elif _k == "in":
        W_JOBS += ["mla_a.s", "mla_a.p", "mla_b"] if _a == "mla" else [f"{_a}.s", f"{_a}.p"] if _a in TOKEN_MAJOR else [f"{_a}.0", f"{_a}.1"]
        T_JOBS += ["ktok.0", "ktok.1", "ktok.p"] if _a == "rk" else []
    elif _k == "latents":
        T_JOBS += ["cq.0", "cq.1", "cq.p", "ckv.0", "ckv.1", "kpe.0", "kpe.1"]
    elif _k == "mla_q":
        W_JOBS += ["q.0", "q.1", "q.2"]
        T_JOBS += [f"qh.{h}" for h in range(HEADS)] + ["qh.p"]
    elif _k == "mla_kv":
        W_JOBS += [f"kh.{h}" for h in range(HEADS)] + ["v.0", "v.1"]
    elif _k == "mix":
        W_JOBS += ["mix.0", "mix.1"]
    elif _k == "conv_mean":
        W_JOBS += ["mean"]
    elif _k == "conv_var":
        N_JOBS += ["var"]
        W_JOBS += ["cstd"]
    elif _k == "conv_out":
        W_JOBS += ["pw.0", "pw.1"]
    elif _k == "att":
        W_JOBS += [f"s.{_a}"]
    elif _k == "rows_g1":
        W_JOBS += ["g1.s", "g1.p"]
    elif _k == "retention":
        N_JOBS += [f"kv.{t}" for t in range(NT)]
        N_JOBS += [f"rs.{_t}.{_h}" for _t in range(NT) for _h in range(2)]
        T_JOBS += [f"ro.{_t}.{_h}" for _t in range(NT) for _h in range(2)]
        T_JOBS += ["yc.0", "yc.1", "yc.p"]
    elif _k == "out":
        W_JOBS += [f"o.{_a}.{h}" for h in "sp"]
    elif _k == "router":
        N_JOBS += ["logits"]
        T_JOBS += ["logits.t", "afft.s", "afft.p", "slots"]
    elif _k == "rows_g2":
        W_JOBS += ["g2.s", "g2.p"]
    if _k == "att" and int(_a) >= 1 or _k == "att_end":
        _i = int(_a) - 1 if _k == "att" else len(BLOCKS) - 1
        T_JOBS += [f"pt.{_i}", f"pt.{_i}b"] if _i < len(BLOCKS) - 1 else [f"pt.{_i}"]
        N_JOBS += [f"pv.{_i - 1}"] if _i else []
    if _k == "att_end":
        N_JOBS += [f"pv.{len(BLOCKS) - 1}"]
        T_JOBS += ["yd.0", "yd.1", "yd.p"]
for _jobs in (W_JOBS, T_JOBS, N_JOBS):
    if len(_jobs) % 2:
        _jobs.append("spare")

GATHERED = 3
FRONT = GATHERED
COMBINE = NT * 2
SELECT, NEXT = FRONT, FRONT + 3
COMBINED = NEXT + GATHERED
T_PAIR = COMBINED + COMBINE - FRONT
T_MOE = FRONT + PAIRS * T_PAIR - GATHERED

LAST_JOB = {("in", g): (f"{g}.p" if g in TOKEN_MAJOR else f"{g}.1") for g in IN_AT}
LAST_JOB[("in", "mla_a")], LAST_JOB[("in", "mla_b")] = "mla_a.p", "mla_b"
LAST_JOB.update({("out", i): f"o.{i}.p" for i in range(4)})
LAST_JOB.update({("mod", i): f"mod.{i}" for i in range(24)})

PARAMS = dict(n1g=KD, n2g=KD, bmod=48, router=KD * STRIP, sgg=NG, convb=NG, lng=NG, lnb=NG, gng=NG, dec=12,
              convw=NG * TAPS, sgb=NG * P, sgw=HEADS * P, pw=NG * GW, qg=QL, kvg=KL, wuq=2 * HEADS * QK,
              wukv=HEADS * 2 * NOPE, cache=KL + ROPE, s0=2 * NG * NOPE)
CONSTS = dict(ident=P, mean=P, expo=2 * P, mask=2 * P, qpos=2 * P, kpos=2, cos=TS * ROPE,
              sin=TS * ROPE, iota=CAPS, eps=1, strips=2)


def spans(sizes):
    out, at = {}, 0
    for name, n in sizes.items():
        out[name] = (at, at + n)
        at += n
    return out, at


PAT, NPARAM = spans(PARAMS)
CAT, NCONST = spans(CONSTS)
NSMALL = 367
KEPT = PAT["router"][1]


START = 1


class Jobs:

    def __init__(self, jobs, moe, per_expert, done, out, ahead=0):
        self.at = {j: i for i, j in enumerate(jobs)}
        self.dense, self.layer, self.expert, self.done_sem, self.out_sem = len(jobs), len(jobs) + moe, per_expert, done, out
        self.ahead = ahead
        assert len(self.at) == len(jobs) and self.layer % 2 == 0 and per_expert % 2 == 0 and ahead % 2 == 0

    def index(self, job):
        return self.at[job] if isinstance(job, str) else self.dense + job

    def buf(self, job):
        return self.index(job) % 2

    def full(self, l, job, e=0):
        return l * self.layer + e * self.expert + self.index(job) + self.ahead

    def half(self, l, job, e=0):
        return l * (self.layer // 2) + e * (self.expert // 2) + self.index(job) // 2 + self.ahead // 2

    def claim(self, pe, l, job, e=0):
        pe.wait_ge(self.out_sem[self.buf(job)], START + self.half(l, job, e))

    def finish(self, ins):
        ins.then_inc(self.done_sem, 1)

    def wait(self, eng, l, job, e=0):
        eng.wait_ge(self.done_sem, START + self.full(l, job, e) + 1)

    def take(self, ins, job):
        ins.then_inc(self.out_sem[self.buf(job)], 1)

    def taken(self, eng, l, job, e=0):
        eng.wait_ge(self.out_sem[self.buf(job)], START + self.half(l, job, e) + 1)

    def layers_taken(self, eng, l):
        for s in self.out_sem:
            eng.wait_ge(s, START + l * (self.layer // 2) + self.ahead // 2)

    def layers_done(self, eng, l):
        eng.wait_ge(self.done_sem, START + l * self.layer + self.ahead)

    def start(self, eng):
        for s in (self.done_sem, *self.out_sem):
            eng.sem_inc(s, START)


class Chain:

    def __init__(self, eng, sem, per_layer):
        self.eng, self.sem, self.per_layer = eng, sem, per_layer
        self.base, self.n = 0, 0

    def start_layer(self, l, before=0):
        self.base, self.n = l * self.per_layer + before, 0

    def mark(self, ins):
        ins.then_inc(self.sem, 1)
        self.n += 1
        return self.n

    def wait(self, n):
        self.eng.wait_ge(self.sem, self.base + n)

    def link(self, ins):
        self.wait(self.mark(ins))

    def end_layer(self):
        if self.n != self.per_layer:
            raise ValueError(f"the links of a layer are {self.n}, not {self.per_layer}")


DVE_LINKS = 161


def build(nc, io):
    ctx = ExitStack()
    with ctx:
        def sb(name, n):
            return ctx.enter_context(nc.sbuf_tensor(name, [P, n], F32))[:, :]

        def sem(name):
            return ctx.enter_context(nc.semaphore(name))

        def carve(region, at, *dims, parts=(0, P)):
            n = int(np.prod(dims))
            v = region[parts[0]:parts[1], at:at + n]
            names = " ".join(f"d{i}" for i in range(len(dims)))
            return v.rearrange(f"p ({names}) -> p {names}", **{f"d{i}": d for i, d in enumerate(dims)}) if len(dims) > 1 else v

        x = carve(sb("x", NT * D), 0, NT, D)
        xn_r = sb("xn_yt", NT * D)
        xn = carve(xn_r, 0, NT, D)
        yT = carve(xn_r, 0, KD, NTOK)
        h_r = sb("ht", KD * NTOK)
        hT = carve(h_r, 0, KD, NTOK)
        stream_r = sb("stream", NSTREAM * KD * GW)
        stream = carve(stream_r, 0, NSTREAM, KD, GW)
        RING = 12
        ring_r = sb("ring", RING * 2 * D)
        ring = carve(ring_r, 0, RING, 2, D)
        par_r = sb("param_cols", NPARAM)
        con_r = sb("const_cols", NCONST)

        def par(name, *dims, parts=(0, P)):
            return carve(par_r, PAT[name][0], *(dims or (PARAMS[name],)), parts=parts)

        def con(name, *dims, parts=(0, P)):
            return carve(con_r, CAT[name][0], *(dims or (CONSTS[name],)), parts=parts)

        ident, mean_w = con("ident"), con("mean")
        ctxt = carve(sb("ctx_tok", NT * (KL + ROPE)), 0, NT, KL + ROPE)
        sT = carve(sb("cond_cols", KD * STRIP), 0, KD, STRIP)
        mod_r = sb("mod_rows", 2 * GW)
        mod_rows = carve(mod_r, 0, 2, GW)
        lgT = mod_r[:, 0:2 * P]
        modT = carve(sb("mod_cols", 48 * 2), 0, 48, 2)
        A1 = carve(sb("scale1", KD * 2), 0, KD, 2)
        A2 = carve(sb("scale2", KD * 2), 0, KD, 2)
        small_r = sb("stats", NSMALL)
        _at = [0]

        def small(*dims):
            v = carve(small_r, _at[0], *dims)
            _at[0] += int(np.prod(dims))
            assert _at[0] <= NSMALL
            return v

        ss, std, rstd = small(NT), small(NT), small(NT)
        mss, mstd, mrstd = small(2, NT), small(2, NT), small(2, NT)
        vss, vstd, vrstd = small(NT), small(NT), small(NT)
        cstd, crstd = small(NT), small(NT)
        lgt = small(6, 12)
        ss_unit = lgt[:, 0:2, :].rearrange("p a b -> p (a b)")[:, 0:NT * 4].rearrange("p (t u) -> p t u", t=NT)
        kd, cdec = small(2 * HEADS), small(2, NG)
        nmax, rsum, rinv = small(2, HEADS), small(2, HEADS), small(2, HEADS)
        amax, asum, arec = small(NT), small(NT), small(NT)
        rsums, rvar, rdev, rrstd = small(NT, 8), small(NT, 8), small(NT, 8), small(NT, 8)
        top8, spare = small(8), small(3, 2)

        r_at = [0]

        def room(n):
            r_at[0] += n
            assert r_at[0] <= RING * 2 * D
            return r_at[0] - n

        MLA0 = room(NT * MLA_IN)
        mla = carve(ring_r, MLA0, NT, MLA_IN)
        ydt = carve(ring_r, MLA0, NT, GW)
        LAT0 = room(HEADS * NTOK + HEADS * NKEY + 6 * GW + NKEY)
        qhT = carve(ring_r, LAT0, HEADS, NTOK, parts=(0, QK))
        khT = carve(ring_r, LAT0 + HEADS * NTOK, HEADS, NKEY)
        vall = carve(ring_r, LAT0 + HEADS * (NTOK + NKEY), 6, GW)
        ckvT = carve(ring_r, LAT0 + HEADS * (NTOK + NKEY) + 6 * GW, NKEY)
        kdk = carve(ring_r, LAT0, 2, NT, GW)
        otok = carve(ring_r, LAT0 + 2 * NT * GW, NT, 2 * GW)
        osq = carve(ring_r, LAT0 + 4 * NT * GW, NT, 2 * GW)
        QT0 = room(NG * NTOK)
        cqT = carve(ring_r, QT0, NG, NTOK)
        qT = carve(ring_r, QT0, NG, NTOK)
        UV0 = room(2 * NG * NTOK)
        uT = carve(ring_r, UV0, NG, NTOK)
        vg = carve(ring_r, UV0 + NG * NTOK, NT, GW)
        prob = carve(ring_r, UV0, 2, NTOK)
        probT = carve(ring_r, UV0 + 2 * NTOK, 2, NTOK)
        sm = carve(ring_r, UV0, 2, 2, 2 * GW)
        GL0 = room(NG * CROW)
        glu = carve(ring_r, GL0, NG, CROW)
        csq = carve(ring_r, GL0, NG, NTOK)
        CA0 = room(NG * CVAL)
        cacc = carve(ring_r, CA0, NG, CVAL)
        zT = carve(ring_r, CA0, NG, NTOK)
        kvs = carve(ring_r, CA0, NT, 2, NG * NOPE)
        lat_sq = carve(ring_r, UV0, NT, QL + KL)
        rot_k = carve(ring_r, UV0 + NT * (QL + KL), TS, ROPE)
        rot_q = carve(ring_r, UV0, TS, HEADS, ROPE)
        CS0 = room(NG * NTOK)
        cscr = carve(ring_r, CS0, NG, NTOK)
        qdec = carve(ring_r, CS0, 2, NG, P)
        yct = carve(ring_r, CS0, NT, GW)
        KT0 = room(2 * NG * NTOK)
        kT = carve(ring_r, KT0, NG, NTOK)
        ktok = carve(ring_r, KT0 + NG * NTOK, NT, GW)
        qtok = carve(ring_r, KT0, NT, HEADS * QK)
        RV0 = room(3 * NT * GW)
        rv = carve(ring_r, RV0, NT, GW)
        gates = carve(ring_r, RV0 + NT * GW, 2, NT, GW)
        g1b = carve(h_r, 0, 2, D)
        qTd = carve(h_r, 2 * D, 2, NG, SAMPLE)
        otmp = carve(h_r, 2 * D, TS * GW)
        otmp_p = carve(h_r, 2 * D + TS * GW, GW)
        squares = carve(h_r, 2 * D + NT * GW, NT, GW)
        sret = carve(h_r, 2 * D + 2 * NG * SAMPLE, TS, 2, NG, NOPE)
        masks = carve(ring_r, GL0, 2, 2, NG * P)
        moe_at = {id(h_r): 0, id(par_r): KEPT}

        def moe(region, *dims, parts=(0, P)):
            at = moe_at[id(region)]
            moe_at[id(region)] += int(np.prod(dims))
            assert moe_at[id(region)] <= {id(h_r): KD * NTOK, id(par_r): NPARAM}[id(region)]
            return carve(region, at, *dims, parts=parts)

        g2b, g2q = moe(h_r, D), moe(h_r, QW)
        slotT, aff = moe(h_r, NT, EXPERTS), moe(h_r, NT, EXPERTS)
        ye = moe(h_r, 2, HALFW)
        zeroed = moe(h_r, HALFW + KD * 4 * CAPP)
        yep = zeroed[:, 0:HALFW]
        xpT = zeroed[:, HALFW:].rearrange("p (k s c) -> p k s c", k=KD, s=4)
        hm, hmp = moe(h_r, HALFW), moe(par_r, QW)
        hmT, hmpT = moe(h_r, HALFW // P, P), moe(h_r, QW // P, P)
        Sp = moe(h_r, 2, CAPP)
        Spw = moe(h_r, 4, 2, CAPP)
        Gp = moe(h_r, P)
        S = moe(par_r, TS, 2, CAPS)
        Sw = moe(par_r, TS, 2, CAPS)
        G = moe(par_r, 2, TS * P)
        xeT = moe(par_r, KD, 2, CAPS)
        work = carve(h_r, D + QW + 2 * NT * EXPERTS, NTOK, parts=(0, EXPERTS))
        cum = carve(par_r, KEPT + QW + 2 * TS * 2 * CAPS, NTOK, parts=(0, EXPERTS))

        psW = ctx.enter_context(nc.psum_tensor("wide", [P, 2, 1024], F32))[:, :, :]
        psT = ctx.enter_context(nc.psum_tensor("turned", [P, 2, 512], F32))[:, :, :]
        psN = ctx.enter_context(nc.psum_tensor("narrow", [P, 2, 512], F32))[:, :, :]

        W = Jobs(W_JOBS, 0, 0, sem("wide_done"), [sem("wide_out0"), sem("wide_out1")])
        T = Jobs(T_JOBS, T_MOE, T_PAIR, sem("turned_done"), [sem("turned_out0"), sem("turned_out1")])
        N = Jobs(N_JOBS, 0, 0, sem("narrow_done"), [sem("narrow_out0"), sem("narrow_out1")], 2 * MOD_FIRST)
        assert N_JOBS[-1] == f"modc.{MOD_FIRST - 1}"
        s_consts, s_x, s_cond = sem("consts_landed"), sem("x_landed"), sem("cond_landed")
        s_params = sem("params_landed")
        s_unit = [sem(f"unit_landed{i}") for i in range(NSTREAM)]
        s_slot = [sem(f"slot_landed{i}") for i in range(RING)]
        s_gu_used, s_dn_used = sem("gateup_used"), sem("down_used")
        s_cond_ready, s_passed = sem("cond_ready"), sem("waits_passed")
        s_dve = sem("vector_step")
        s_mixed = sem("spatial_out")
        s_unit_sq, s_ss, s_rstd, s_xn_act = sem("unit_squares"), sem("squares_added"), sem("rstd_ready"), sem("xn_by_scalar")
        s_std, s_xn, s_scale = sem("std_ready"), sem("xn_ready"), sem("scale_ready")
        s_mss, s_mstd, s_lat, s_qrot = sem("latent_squares"), sem("latent_std"), sem("latents_ready"), sem("queries_rotated")
        s_ctx_out = sem("ctx_stored")
        s_pads, s_conv, s_csq = sem("pads_ready"), sem("conv_ready"), sem("conv_squares")
        s_crs, s_z = sem("conv_rstd"), sem("conv_silu")
        s_vss, s_vstd, s_vn = sem("spatial_squares"), sem("spatial_std"), sem("spatial_normed")
        s_nmax = sem("score_max")
        s_dec, s_dexp, s_dlog, s_lg = sem("decay_in"), sem("decay_exp"), sem("decay_log"), sem("log_decay")
        s_tab, s_msk = sem("decay_tables"), sem("masks_ready")
        s_kdk, s_qtd, s_sret = sem("k_decayed"), sem("q_decayed"), sem("states_ready")
        s_ocen, s_osq, s_ovar, s_ostd, s_yc = sem("ret_centred"), sem("ret_squares"), sem("ret_var"), sem("ret_std"), sem("ret_out")
        s_res, s_st_out = sem("residual_added"), sem("state_stored")
        s_lexp, s_aff = sem("logit_exp"), sem("affinity_ready")
        s_slotcode = sem("slotcode_ready")
        s_zeros, s_S, s_swap, s_weighed = sem("strips_zeroed"), sem("select_ready"), sem("selection_swapped"), sem("selection_weighed")
        s_turned, s_hT = sem("hidden_turned"), sem("hidden_turned_out")
        s_half_sq = sem("half_squares")
        s_silu, s_hm, s_ye, s_yep = sem("silu_ready"), sem("hidden_ready"), sem("latent_rows_out"), sem("context_rows_out")
        s_y, s_ystored, s_fg = sem("y_ready"), sem("y_stored"), sem("final_gain_landed")

        RINGS = ((W, W_JOBS), (T, T_JOBS), (N, N_JOBS))

        def bank(R, job, rows=P):
            return {id(W): psW, id(T): psT, id(N): psN}[id(R)][0:rows, R.buf(job), :]

        mod_h = io["w_mod"].rearrange("l (k p) n -> l p k n", p=P)
        in_h = io["w_in"].rearrange("l (k p) n -> l p k n", p=P)
        out_h = io["w_out"].rearrange("l (k p) n -> l p k n", p=P)
        down_h = io["w_down"].rearrange("l e (k p) n -> l e p k n", p=P)

        block = ctx.enter_context(nc.Block())

        def before(R, job):
            return R.at[job] - R.layer - R.dense

        def settle(eng):
            eng.sem_inc(s_passed, 1)

        @block.sync
        def _(sp):
            for R, _jobs in RINGS:
                R.start(sp)
            for s in (s_silu, s_hm):
                sp.sem_inc(s, START)
            sp.dma_start(sT.rearrange("p k s -> p (k s)"), io["cond"]).then_inc(s_cond, 16)
            sp.dma_start(con_r, io["consts"]).then_inc(s_consts, 16)
            sp.dma_start(x[:, 0:TS, :], io["x_sample"][0].rearrange("(t p) d -> p t d", p=P)).then_inc(s_x, 16)
            sp.dma_start(x[:, CTX, :], io["x_prompt"][0]).then_inc(s_x, 16)

            sp.wait_ge(s_consts, 16)

            def load_unit(l, n):
                kind, which = UNITS[n]
                ahead = isinstance(l, int)
                if ahead and n - NSTREAM < NLAYER:
                    pass
                elif n < NSTREAM:
                    N.wait(sp, l, before(N, f"mod.{MOD_FIRST - NSTREAM + n}"))
                    settle(sp)
                else:
                    last = UNITS[n - NSTREAM]
                    (N if last[0] == "mod" else W).wait(sp, l, LAST_JOB[last])
                    settle(sp)
                lo = IN_AT[which] if kind == "in" else which * GW
                w = MLA_B if which == "mla_b" else GW
                at = l if n < NLAYER else 0 if ahead else (l + 1) % DEPTH
                src = {"mod": mod_h, "in": in_h, "out": out_h}[kind][bass.ds(at, 1), :, :, lo:lo + w]
                sp.dma_start(stream[:, n % NSTREAM, :, 0:w], src.rearrange("l p k n -> (l p) k n")).then_inc(s_unit[n % NSTREAM], 16)

            def load_gateup(l, e, k):
                for i, w in enumerate(("w_gate", "w_up")):
                    src = io[w][bass.ds(l, 1), bass.ds(e, 1), k * P:(k + 1) * P, :]
                    sp.dma_start(ring[:, k, i, :], src.rearrange("l e p n -> (l e p) n")).then_inc(s_slot[k], 16)

            def load_down(l, e, j):
                src = down_h[bass.ds(l, 1), bass.ds(e, 1), :, 2 * j:2 * j + 2, :]
                sp.dma_start(ring[:, KD + j, :, :], src.rearrange("l e p k n -> (l e p) k n")).then_inc(s_slot[KD + j], 16)

            for n in range(NLAYER, NUNIT):
                load_unit(-1, n)
            with sp.Fori(0, DEPTH) as l:
                for n in range(NUNIT):
                    load_unit(l, n)
                    if n == 0:
                        T.layers_taken(sp, l)
                        settle(sp)
                        sp.dma_start(par_r, io["params"][bass.ds(l, 1)].rearrange("l p n -> (l p) n")).then_inc(s_params, 16)
                    if n == UNITS.index(("out", 2)):
                        W.wait(sp, l, "o.0.s")
                        sp.wait_ge(s_ctx_out, 32 * l + 32)
                        sp.wait_ge(s_st_out, 32 * l + 32)
                        settle(sp)
                    at = 3 * (n - UNITS.index(("out", 2)))
                    for slot in range(max(at, 0), min(at + 3, RING)):
                        if slot < KD:
                            load_gateup(l, 0, slot)
                        else:
                            load_down(l, 0, slot - KD)
                with sp.Fori(1, EXPERTS) as e:
                    for k in range(KD):
                        sp.wait_ge(s_gu_used, (l * EXPERTS + e) * KD + k - (KD - 1))
                        settle(sp)
                        load_gateup(l, e, k)
                    for j in range(4):
                        sp.wait_ge(s_dn_used, (l * EXPERTS + e) * 4 + j - 3)
                        settle(sp)
                        load_down(l, e, j)
            N.layers_done(sp, DEPTH)
            sp.dma_start(stream_r[:, 0:D], io["final_g"].partition_broadcast(P)).then_inc(s_fg, 16)
            for t in range(NT):
                sp.wait_ge(s_y, t + 1)
                dst = io["y_prompt"][0] if t == CTX else io["y_sample"][0, t * P:(t + 1) * P]
                sp.dma_start(dst, xn[:, t, :]).then_inc(s_ystored, 16)
            sp.wait_ge(s_ystored, NT * 16)

        @block.tensor
        def _(pe):
            mm = nc.tensor.matmul
            unit_no = [NLAYER]

            def units_ahead(n):
                return sum(m % NSTREAM == n % NSTREAM for m in range(NLAYER, NUNIT))

            def next_unit(l):
                n = unit_no[0]
                unit_no[0] += 1
                pe.wait_ge(s_unit[n % NSTREAM], (l * (NUNIT // NSTREAM) + n // NSTREAM + 1 + units_ahead(n)) * 16)
                return stream[:, n % NSTREAM, :, :]

            def mod_unit(l, u):
                job = f"mod.{u}"
                w = next_unit(l)
                N.claim(pe, l, job)
                for k in range(KD):
                    q = k % 4
                    ins = mm(psN[q * STRIP:(q + 1) * STRIP, N.buf(job), 0:GW], sT[:, k, :], w[:, k, :], start=(k < 4), stop=(k >= 4))
                N.finish(ins)

            def mod_columns(l, u):
                job = f"modc.{u}"
                N.taken(pe, l, f"mod.{u}")
                N.claim(pe, l, job)
                for c in range(NG):
                    ins = mm(bank(N, job)[:, 2 * c:2 * c + 2], mod_rows[:, u % 2, c * P:(c + 1) * P], con("strips"), start=True, stop=True)
                N.finish(ins)

            def modulation(l, lo, hi):
                for which, u in mod_order(lo, hi):
                    (mod_unit if which == "mod" else mod_columns)(l, u)

            def transposes(l, job, outs_ins):
                T.claim(pe, l, job)
                settle(pe)
                for o, i in outs_ins:
                    ins = nc.tensor.transpose(o, i, ident[0:i.shape[0], 0:i.shape[0]])
                T.finish(ins)

            def norm(l, which):
                for k in range(KD):
                    job = f"{which}.{k}"
                    if k == 0:
                        pe.wait_ge(s_xn_act, (2 * l + (which == "norm2") + 1) * ACT_TILES)
                        pe.wait_ge(s_xn, (2 * l + (which == "norm2")) * (NT - ACT_TILES) + TS - ACT_TILES)
                    o = bank(T, job)
                    transposes(l, job, [(o[:, t * P:(t + 1) * P], xn[:, t, k * P:(k + 1) * P]) for t in range(TS)])
                for i in range(2):
                    job = f"{which}.{KD + i}"
                    if i == 0:
                        pe.wait_ge(s_xn, (2 * l + (which == "norm2") + 1) * (NT - ACT_TILES))
                    o = bank(T, job)
                    transposes(l, job, [(o[:, j * P:(j + 1) * P], xn[:, CTX, (4 * i + j) * P:(4 * i + j + 1) * P]) for j in range(4)])

            def feature_major(l, g):
                w = next_unit(l)
                for c in range(NG):
                    job = f"{g}.{c}"
                    W.claim(pe, l, job)
                    o = bank(W, job)
                    for lo, hi in ((SAMPLE, NTOK), (0, SAMPLE)):
                        for k in range(KD):
                            ins = mm(o[:, lo:hi], w[:, k, c * P:(c + 1) * P], hT[:, k, lo:hi], start=(k == 0), stop=(k == KD - 1))
                    W.finish(ins)

            def token_major(l, g, width=GW, src=hT, jobs=None):
                w = next_unit(l)
                for job, tiles in (jobs or ((f"{g}.s", range(TS)), (f"{g}.p", [CTX]))):
                    W.claim(pe, l, job)
                    o = bank(W, job)
                    for n, t in enumerate(tiles):
                        for k in range(KD):
                            ins = mm(o[:, n * width:(n + 1) * width], src[:, k, t * P:(t + 1) * P], w[:, k, 0:width], start=(k == 0), stop=(k == KD - 1))
                    W.finish(ins)

            def latents(l):
                pe.wait_ge(s_lat, l + 1)
                for c, n in ((0, P), (1, QL - P)):
                    o = bank(T, f"cq.{c}", n)
                    transposes(l, f"cq.{c}", [(o[:, t * P:(t + 1) * P], mla[:, t, c * P:c * P + n]) for t in range(TS)])
                o = bank(T, "cq.p")
                transposes(l, "cq.p", [(o[0:n, c * P:(c + 1) * P], mla[:, CTX, c * P:c * P + n]) for c, n in ((0, P), (1, QL - P))])
                cache = par("cache")
                rows = [ctxt[:, t, :] for t in range(TS)] + [cache, ctxt[:, CTX, :]]
                for name, lo, m in (("ckv", 0, KL), ("kpe", KL + ROPE - QK, QK)):
                    o = bank(T, f"{name}.0", m)
                    transposes(l, f"{name}.0", [(o[:, t * P:(t + 1) * P], rows[t][:, lo:lo + m]) for t in range(TS)])
                    o = bank(T, f"{name}.1", m)
                    transposes(l, f"{name}.1", [(o[:, t * P:(t + 1) * P], rows[TS + t][:, lo:lo + m]) for t in range(2)])

            def mla_q(l):
                wuq = par("wuq", 2, HEADS * QK)
                T.taken(pe, l, "cq.p")
                T.taken(pe, l, "cq.1")
                for j, tiles in enumerate(((0, 1), (2, 3), (4,))):
                    W.claim(pe, l, f"q.{j}")
                    o = bank(W, f"q.{j}")
                    for n, t in enumerate(tiles):
                        mm(o[:, n * 512:n * 512 + HEADS * QK], cqT[:, 0, t * P:(t + 1) * P], wuq[:, 0, :], start=True, stop=False)
                        ins = mm(o[:, n * 512:n * 512 + HEADS * QK], cqT[0:QL - P, 1, t * P:(t + 1) * P], wuq[0:QL - P, 1, :], start=False, stop=True)
                    W.finish(ins)

            def turn_q(l):
                pe.wait_ge(s_qrot, l + 1)
                W.taken(pe, l, "q.2")
                for h in range(HEADS):
                    o = bank(T, f"qh.{h}", QK)
                    transposes(l, f"qh.{h}", [(o[:, t * P:(t + 1) * P], qtok[:, t, h * QK:(h + 1) * QK]) for t in range(TS)])
                o = bank(T, "qh.p", QK)
                transposes(l, "qh.p", [(o[:, h * P:(h + 1) * P], qtok[:, CTX, h * QK:(h + 1) * QK]) for h in range(HEADS)])

            def mla_kv(l):
                wukv = par("wukv", HEADS, 2, NOPE)
                T.taken(pe, l, "ckv.0")
                T.taken(pe, l, "ckv.1")
                for h in range(HEADS):
                    W.claim(pe, l, f"kh.{h}")
                    o = bank(W, f"kh.{h}", NOPE)
                    mm(o[:, 0:512], wukv[:, h, 0, :], ckvT[:, 0:512], start=True, stop=True)
                    W.finish(mm(o[:, 512:NKEY], wukv[:, h, 0, :], ckvT[:, 512:NKEY], start=True, stop=True))
                for j, tiles in enumerate(((0, 1, 2, 3), (4, 5))):
                    W.claim(pe, l, f"v.{j}")
                    o = bank(W, f"v.{j}")
                    for n, t in enumerate(tiles):
                        ins = mm(o[:, n * GW:(n + 1) * GW].rearrange("p (h d) -> p h d", h=HEADS), ckvT[:, t * P:(t + 1) * P], wukv[:, :, 1, :], start=True, stop=True)
                    W.finish(ins)

            def mix(l):
                sgw = par("sgw", HEADS, P)
                pe.wait_ge(s_vn, l + 1)
                for c in range(NG):
                    W.claim(pe, l, f"mix.{c}")
                    o = bank(W, f"mix.{c}")
                    for t in range(NT):
                        for half in range(2):
                            h = 2 * c + half
                            ins = mm(o[half * 64:half * 64 + 64, t * P:(t + 1) * P], vg[:, t, h * 64:(h + 1) * 64], sgw[:, h, :], start=True, stop=True)
                    W.finish(ins)

            def conv_mean(l):
                pe.wait_ge(s_conv, l + 1)
                W.claim(pe, l, "mean")
                o = bank(W, "mean")
                for dst, lo, n in ((0, 0, SAMPLE), (SAMPLE, CPROMPT, PROMPT)):
                    for c in range(NG):
                        ins = mm(o[:, dst:dst + n], mean_w, cacc[:, c, lo:lo + n], start=(c == 0), stop=(c == NG - 1))
                W.finish(ins)

            def conv_var(l):
                pe.wait_ge(s_csq, l + 1)
                N.claim(pe, l, "var")
                o = bank(N, "var")
                for t in range(NT):
                    for c in range(NG):
                        ins = mm(o[:, t:t + 1], csq[:, c, t * P:(t + 1) * P], mean_w[:, 0:1], start=(c == 0), stop=(c == NG - 1))
                N.finish(ins)
                pe.wait_ge(s_crs, l + 1)
                W.claim(pe, l, "cstd")
                o = bank(W, "cstd")
                for t in range(NT):
                    ins = mm(o[:, t * P:(t + 1) * P], crstd[:, t:t + 1].broadcast_to([P, P]), ident, start=True, stop=True)
                W.finish(ins)

            def conv_out(l):
                pw = par("pw", NG, GW)
                pe.wait_ge(s_z, 2 * l + 2)
                for c in range(NG):
                    W.claim(pe, l, f"pw.{c}")
                    o = bank(W, f"pw.{c}")
                    for lo, hi in ((0, SAMPLE), (SAMPLE, NTOK)):
                        for k in range(NG):
                            ins = mm(o[:, lo:hi], pw[:, k, c * P:(c + 1) * P], zT[:, k, lo:hi], start=(k == 0), stop=(k == NG - 1))
                    W.finish(ins)

            def scores(l, i):
                h, t = BLOCKS[i]
                job = f"s.{i}"
                if i == 0:
                    for j in ("qh.3", "qh.p"):
                        T.taken(pe, l, j)
                    for j in ("v.0", "v.1"):
                        W.taken(pe, l, j)
                W.claim(pe, l, job)
                o = bank(W, job)
                if h == "ctx":
                    for h in range(HEADS):
                        ins = mm(o[:, h * P:(h + 1) * P], qhT[:, h, CTX * P:NTOK], khT[0:QK, h, NKEY - P:NKEY], start=True, stop=True)
                else:
                    mm(o[:, 0:512], qhT[:, h, t * P:(t + 1) * P], khT[0:QK, h, 0:512], start=True, stop=True)
                    ins = mm(o[:, 512:640], qhT[:, h, t * P:(t + 1) * P], khT[0:QK, h, 512:640], start=True, stop=True)
                W.finish(ins)

            def turn_probs(l, i):
                pr = prob[:, i % 2, :]
                W.taken(pe, l, f"s.{i}")
                o = bank(T, f"pt.{i}")
                transposes(l, f"pt.{i}", [(o[:, j * P:(j + 1) * P], pr[:, j * P:(j + 1) * P]) for j in range(4)])
                if BLOCKS[i][0] != "ctx":
                    o = bank(T, f"pt.{i}b")
                    transposes(l, f"pt.{i}b", [(o[:, 0:P], pr[:, 4 * P:5 * P])])

            def weigh_values(l, i):
                h, t = BLOCKS[i]
                job = f"pv.{i}"
                T.taken(pe, l, f"pt.{i}")
                if h != "ctx":
                    T.taken(pe, l, f"pt.{i}b")
                N.claim(pe, l, job)
                o = bank(N, job)
                pt = probT[:, i % 2, :]
                if h == "ctx":
                    for h in range(HEADS):
                        ins = mm(o[:, h * 64:(h + 1) * 64], pt[:, h * P:(h + 1) * P], vall[:, 5, h * 64:(h + 1) * 64], start=True, stop=True)
                else:
                    for j in range(5):
                        ins = mm(o[:, 0:64], pt[:, j * P:(j + 1) * P], vall[:, j, h * 64:(h + 1) * 64], start=(j == 0), stop=(j == 4))
                N.finish(ins)

            def turn_rows(l, name, rows):
                for c in range(NG):
                    o = bank(T, f"{name}.{c}")
                    transposes(l, f"{name}.{c}", [(o[:, t * P:(t + 1) * P], rows[:, t, c * P:(c + 1) * P]) for t in range(TS)])
                o = bank(T, f"{name}.p")
                transposes(l, f"{name}.p", [(o[:, c * P:(c + 1) * P], rows[:, CTX, c * P:(c + 1) * P]) for c in range(NG)])

            def turn_k(l):
                W.taken(pe, l, "rk.0")
                W.taken(pe, l, "rk.1")
                for i in range(2):
                    o = bank(T, f"ktok.{i}")
                    transposes(l, f"ktok.{i}", [(o[:, (2 * n + c) * P:(2 * n + c + 1) * P], kT[:, c, (2 * i + n) * P:(2 * i + n + 1) * P])
                                                 for n in range(2) for c in range(NG)])
                o = bank(T, "ktok.p")
                transposes(l, "ktok.p", [(o[:, c * P:(c + 1) * P], kT[:, c, SAMPLE:NTOK]) for c in range(NG)])

            def rows_g1(l):
                N.taken(pe, l, "modc.10")
                N.taken(pe, l, "modc.11")
                for s, job in ((1, "g1.s"), (0, "g1.p")):
                    W.claim(pe, l, job)
                    o = bank(W, job)
                    for k in range(KD):
                        ins = mm(o[:, k * P:(k + 1) * P], modT[:, 2 * KD + k, s:s + 1].broadcast_to([P, P]), ident, start=True, stop=True)
                    W.finish(ins)

            def retention(l):
                pe.wait_ge(s_kdk, 2 * l + 2)
                W.taken(pe, l, "rv.s")
                W.taken(pe, l, "rv.p")
                for t in range(NT):
                    N.claim(pe, l, f"kv.{t}")
                    o = bank(N, f"kv.{t}")
                    dirs = [d for d in range(2) if t == CTX or (t < TS - 1 if d == 0 else t > 0)]
                    for d in dirs:
                        for c in range(NG):
                            for half in range(2):
                                h = 2 * c + half
                                at = (d * NG + c) * 64
                                ins = mm(o[half * 64:half * 64 + 64, at:at + 64], kdk[:, d, t, h * 64:(h + 1) * 64], rv[:, t, h * 64:(h + 1) * 64], start=True, stop=True)
                    N.finish(ins)

                def ret_scores(t):
                    for half in range(2):
                        N.claim(pe, l, f"rs.{t}.{half}")
                        p = slice(half * 64, half * 64 + 64)
                        for c in range(NG):
                            ins = mm(bank(N, f"rs.{t}.{half}")[:, c * P:(c + 1) * P], kT[p, c, t * P:(t + 1) * P], qT[p, c, t * P:(t + 1) * P], start=True, stop=True)
                        N.finish(ins)

                def ret_out(t):
                    for half in range(2):
                        N.taken(pe, l, f"rs.{t}.{half}")
                    if t == 0:
                        pe.wait_ge(s_qtd, 2 * l + 2)
                        pe.wait_ge(s_sret, l + 1)
                    for half in range(2):
                        T.claim(pe, l, f"ro.{t}.{half}")
                        p = slice(half * 64, half * 64 + 64)
                        for d in range(2):
                            for c in range(NG):
                                h = 2 * c + half
                                out = bank(T, f"ro.{t}.{half}")[:, (d * NG + c) * 64:(d * NG + c + 1) * 64]
                                ins = mm(out, sm[:, t % 2, d, half * GW + c * P:half * GW + (c + 1) * P], rv[:, t, h * 64:(h + 1) * 64], start=True, stop=(t == CTX))
                                if t != CTX:
                                    first = t == (0 if d == 0 else TS - 1)
                                    st = par("s0", 2, NG, NOPE)[p, d, c, :] if first else sret[p, t, d, c, :]
                                    ins = mm(out, qTd[p, d, c, t * P:(t + 1) * P], st, start=False, stop=True)
                        T.finish(ins)

                others = [k for k in range(KD) if k not in RET_CHUNKS]
                for t in range(NT):
                    ret_scores(t)
                    if t == 0:
                        for j in ("pw.0", "pw.1"):
                            W.taken(pe, l, j)
                        for j in ("yd.1", "yd.p"):
                            T.taken(pe, l, j)
                        pe.wait_ge(s_mixed, 2 * l + 2)
                        settle(pe)
                        out_weights[0] = next_unit(l)
                    if t < TS - 1:
                        out_first(l, t, others, True)
                    if t:
                        ret_out(t - 1)
                ret_out(NT - 1)
                for t in (TS - 1, CTX):
                    out_first(l, t, others, True)
                pe.wait_ge(s_yc, (l + 1) * NT)
                turn_rows(l, "yc", yct)

            RET_CHUNKS = (2 * NG, 2 * NG + 1)
            out_weights = [None]

            def out_first(l, t, chunks, first):
                job = "o.0.s" if t < TS else "o.0.p"
                if first and t in (0, CTX):
                    W.claim(pe, l, job)
                at = (t if t < TS else 0) * GW
                for k in chunks:
                    ins = mm(bank(W, job)[:, at:at + GW], yT[:, k, t * P:(t + 1) * P], out_weights[0][:, k, :],
                             start=(first and t % 2 == 0 and k == chunks[0]), stop=(not first and (t % 2 == 1 or t == CTX) and k == chunks[-1]))
                if not first and t in (TS - 1, CTX):
                    W.finish(ins)

            def out_proj(l, u):
                if u:
                    token_major(l, None, src=yT, jobs=((f"o.{u}.s", range(TS)), (f"o.{u}.p", [CTX])))
                    return
                for j in ("yc.1", "yc.p"):
                    T.taken(pe, l, j)
                for t in range(NT):
                    out_first(l, t, RET_CHUNKS, False)

            def router(l):
                rt = par("router", KD, STRIP)
                T.taken(pe, l, f"norm2.{KD}")
                T.taken(pe, l, f"norm2.{KD + 1}")
                N.claim(pe, l, "logits")
                o = bank(N, "logits")
                for k in range(KD):
                    for t in range(TS):
                        mm(o[t * STRIP:(t + 1) * STRIP, 0:P], rt[:, k, :], hT[:, k, t * P:(t + 1) * P], start=(k == 0), stop=(k == KD - 1))
                for k in range(KD):
                    ins = mm(o[0:STRIP, P:2 * P], rt[:, k, :], hT[:, k, SAMPLE:NTOK], start=(k == 0), stop=(k == KD - 1))
                N.finish(ins)
                N.taken(pe, l, "logits")
                o = bank(T, "logits.t")
                transposes(l, "logits.t", [(o[:, 0:P], lgT[:, 0:P]), (o[:, P:P + STRIP], lgT[0:STRIP, P:2 * P])])

            def choose(l):
                pe.wait_ge(s_aff, l + 1)
                o = bank(T, "afft.s", EXPERTS)
                transposes(l, "afft.s", [(o[:, t * P:(t + 1) * P], aff[:, t, :]) for t in range(TS)])
                o = bank(T, "afft.p", EXPERTS)
                transposes(l, "afft.p", [(o[:, 0:P], aff[:, CTX, :])])

            def turn_slots(l):
                pe.wait_ge(s_slotcode, 2 * l + 2)
                o = bank(T, "slots")
                transposes(l, "slots", [(o[:, t * EXPERTS:(t + 1) * EXPERTS], work[:, t * P:(t + 1) * P]) for t in range(NT)])

            def rows_g2(l):
                W.claim(pe, l, "g2.s")
                o = bank(W, "g2.s")
                for k in range(KD):
                    ins = mm(o[:, k * P:(k + 1) * P], modT[:, 5 * KD + k, 1:2].broadcast_to([P, P]), ident, start=True, stop=True)
                W.finish(ins)
                W.claim(pe, l, "g2.p")
                o = bank(W, "g2.p")
                for j in range(QW // P):
                    for q in range(4):
                        col = modT[:, 5 * KD + q * (QW // P) + j, 0:1].broadcast_to([P, STRIP])
                        ins = mm(o[q * STRIP:(q + 1) * STRIP, j * P:(j + 1) * P], col, ident, start=True, stop=True)
                W.finish(ins)

            def gather(l, e, at, parts):
                for job, i in zip(at, parts):
                    T.claim(pe, l, job, e)
                    o = bank(T, job)
                    if i < 2:
                        for k in range(4):
                            for t in range(TS):
                                ins = mm(o[:, k * P:(k + 1) * P], xn[:, t, (4 * i + k) * P:(4 * i + k + 1) * P], S[:, t].rearrange("p x c -> p (x c)"), start=(t == 0), stop=(t == TS - 1))
                    else:
                        for k in range(KD):
                            ins = mm(o[:, k * STRIP:(k + 1) * STRIP], xn[:, CTX, k * P:(k + 1) * P], Sp.rearrange("p x c -> p (x c)"), start=True, stop=True)
                    T.finish(ins)

            def turn_selection(l, e, n):
                pe.wait_ge(s_weighed, n + 1)
                for job, src in ((SELECT, S), (SELECT + 1, Sw)):
                    T.claim(pe, l, job, e)
                    o = bank(T, job)
                    for t in range(TS):
                        ins = nc.tensor.transpose(o[:, t * P:(t + 1) * P], src[:, t].rearrange("p x c -> p (x c)"), ident)
                    T.finish(ins)
                T.claim(pe, l, SELECT + 2, e)
                T.finish(nc.tensor.transpose(bank(T, SELECT + 2)[:, 0:P], Spw.rearrange("p q x c -> p (q x c)"), ident))

            def gate_up(l, m, i):
                for k in range(KD):
                    pe.wait_ge(s_slot[k], (m + 1) * 32)

                    def lat():
                        for w in range(2):
                            for h in range(2):
                                ins = mm(psW[h * 64:(h + 1) * 64, 0, w * HALFW:(w + 1) * HALFW], xeT[:, k, i, :], ring[:, k, w, h * HALFW:(h + 1) * HALFW], start=(k == 0), stop=(k == KD - 1))
                        return ins

                    def con_():
                        for w in range(2):
                            for q in range(4):
                                ins = mm(psW[q * STRIP:(q + 1) * STRIP, 1, w * QW:(w + 1) * QW], xpT[:, k, 2 * i:2 * i + 2, :].rearrange("p x c -> p (x c)"),
                                         ring[:, k, w, q * QW:(q + 1) * QW], start=(k == 0 and w == 0), stop=(k == KD - 1 and w == 1))
                        return ins

                    for part in ((lat, con_) if k % 2 == 0 else (con_, lat)):
                        ins = part()
                    ins.then_inc(s_gu_used, 1)

            def turn_hidden(m):
                for i, (src, dst, n) in enumerate(((hm, psW[:, 0, 0:HALFW], HALFW // P), (hmp, psW[:, 1, 0:QW], QW // P))):
                    pe.wait_ge(s_hm, START + 2 * m + 1 + i)
                    for j in range(n):
                        ins = nc.tensor.transpose(dst[:, j * P:(j + 1) * P], src[:, j * P:(j + 1) * P], ident)
                    ins.then_inc(s_turned, 1)

            def down(m, i):
                pe.wait_ge(s_hT, 2 * m + 1)
                for k in range(KF):
                    if k % 2 == 0:
                        pe.wait_ge(s_slot[KD + k // 2], (m + 1) * 16)

                    def lat():
                        h_, j = divmod(k, HALFW // P)
                        for c in range(2):
                            h = c ^ i
                            ins = mm(psN[c * 64:(c + 1) * 64, h, :], hmT[:, j, h_ * 64:(h_ + 1) * 64], ring[:, KD + k // 2, k % 2, h * HALFW:(h + 1) * HALFW], start=(k == 0), stop=(k == KF - 1))
                        return ins

                    def con_():
                        if k == 0:
                            pe.wait_ge(s_hT, 2 * m + 2)
                        q_, j = divmod(k, QW // P)
                        for q in range(4):
                            ins = mm(psW[q * STRIP:(q + 1) * STRIP, 1, HALFW:HALFW + QW], hmpT[:, j, q_ * STRIP:(q_ + 1) * STRIP], ring[:, KD + k // 2, k % 2, q * QW:(q + 1) * QW],
                                     start=(k == 0 and i == 0), stop=(k == KF - 1 and i == 1))
                        return ins

                    for part in ((lat, con_) if k % 2 == 0 else (con_, lat)):
                        ins = part()
                    if k % 2:
                        ins.then_inc(s_dn_used, 1)

            def combine(l, e, n, select, at, jobs):
                if 0 in jobs:
                    for job in (select + 1, select + 2):
                        T.taken(pe, l, job, e)
                    pe.wait_ge(s_ye, 4 * n + 4)
                for j in jobs:
                    half, t = divmod(j, NT)
                    if j == CTX:
                        pe.wait_ge(s_yep, n + 1)
                    T.claim(pe, l, at + j, e)
                    if t == CTX:
                        p = slice(half * 64, half * 64 + 64)
                        ins = mm(bank(T, at + j), Gp[p, :], yep[p, :], start=True, stop=True)
                    else:
                        ins = mm(bank(T, at + j), G[:, half, t * P:(t + 1) * P], ye[:, half, :], start=True, stop=True)
                    T.finish(ins)

            def pair(l, e, n, first, last):
                for job in ((1, 2) if first else (NEXT + 1 - T_PAIR, NEXT + 2 - T_PAIR)):
                    T.taken(pe, l, job, e)
                if not first:
                    pe.wait_ge(s_hm, START + 4 * n)
                gate_up(l, 2 * n, 0)
                for part in range(2):
                    if not first:
                        combine(l, e, n - 1, SELECT - T_PAIR, COMBINED - T_PAIR, range(part * NT, part * NT + NT))
                    if part == 0:
                        turn_hidden(2 * n)
                turn_selection(l, e, n)
                down(2 * n, 0)
                gate_up(l, 2 * n + 1, 1)
                if not last:
                    pe.wait_ge(s_S, n + 2)
                    gather(l, e, (NEXT,), (0,))
                turn_hidden(2 * n + 1)
                if not last:
                    gather(l, e, (NEXT + 1, NEXT + 2), (1, 2))
                down(2 * n + 1, 1)
                if last:
                    combine(l, e, n, SELECT, COMBINED - GATHERED, range(COMBINE))

            pe.wait_ge(s_consts, 16)
            pe.wait_ge(s_cond_ready, 1)
            modulation(-1, 0, MOD_FIRST)
            with pe.Fori(0, DEPTH) as l:
                unit_no[0] = 0
                for s in STEPS:
                    kind, _, arg = s.partition(":")
                    if s == STEPS[1]:
                        pe.wait_ge(s_params, 16 * l + 16)
                    if kind == "mod":
                        modulation(l, *map(int, arg.split("-")))
                    elif kind in ("norm1", "norm2"):
                        norm(l, kind)
                    elif kind == "in":
                        if arg == "mla":
                            for k in (KD, KD + 1):
                                T.taken(pe, l, f"norm1.{k}")
                            token_major(l, None, jobs=(("mla_a.s", range(TS)), ("mla_a.p", [CTX])))
                            token_major(l, None, width=MLA_B, jobs=(("mla_b", range(NT)),))
                        elif arg in TOKEN_MAJOR:
                            token_major(l, arg)
                        else:
                            feature_major(l, arg)
                        if arg == "rk":
                            turn_k(l)
                    elif kind == "latents":
                        latents(l)
                    elif kind == "mla_q":
                        mla_q(l)
                    elif kind == "mla_kv":
                        mla_kv(l)
                        turn_q(l)
                    elif kind == "mix":
                        mix(l)
                    elif kind == "conv_mean":
                        conv_mean(l)
                    elif kind == "conv_var":
                        conv_var(l)
                    elif kind == "conv_out":
                        conv_out(l)
                    elif kind == "att":
                        i = int(arg)
                        scores(l, i)
                        if i > 1:
                            weigh_values(l, i - 2)
                        if i:
                            turn_probs(l, i - 1)
                    elif kind == "att_end":
                        weigh_values(l, len(BLOCKS) - 2)
                        turn_probs(l, len(BLOCKS) - 1)
                        weigh_values(l, len(BLOCKS) - 1)
                        N.taken(pe, l, f"pv.{len(BLOCKS) - 1}")
                        N.taken(pe, l, f"pv.{len(BLOCKS) - 2}")
                        turn_rows(l, "yd", ydt)
                    elif kind == "rows_g1":
                        rows_g1(l)
                    elif kind == "retention":
                        retention(l)
                    elif kind == "out":
                        out_proj(l, int(arg))
                    elif kind == "router":
                        router(l)
                    elif kind == "rows_g2":
                        rows_g2(l)
                        choose(l)
                turn_slots(l)
                for R, jobs in RINGS:
                    if "spare" in R.at:
                        R.claim(pe, l, "spare")
                        R.finish(mm(bank(R, "spare")[:, 0:2], ident, ident[:, 0:2], start=True, stop=True))
                n0 = l * PAIRS
                pe.wait_ge(s_S, n0 + 1)
                gather(l, 0, range(GATHERED), range(GATHERED))
                for j in ("g2.s", "g2.p"):
                    W.taken(pe, l, j)
                pair(l, 0, n0, True, False)
                with pe.Fori(1, PAIRS - 1) as e:
                    pair(l, e, n0 + e, False, False)
                pair(l, PAIRS - 1, n0 + PAIRS - 1, False, True)

        @block.scalar
        def _(act):
            A = nc.scalar.activation
            def out(R, l, job, dst, src, func=ACT.Identity, **kw):
                R.wait(act, l, job)
                R.take(A(dst, src, func, **kw), job)

            def half_squares(j):
                half, t = divmod(j, NT)
                c = slice(half * HALFW, (half + 1) * HALFW)
                ins = A(xn[:, t, c], x[:, t, c], ACT.Square, accum_out=ss_unit[:, t, half:half + 1])
                if j == COMBINE - 1:
                    ins.then_inc(s_half_sq, 1)

            def norm_std(n):
                act.wait_ge(s_ss, n + 1)
                A(std, ss, ACT.Sqrt, scale=1.0 / D, bias=con("eps")).then_inc(s_std, 1)

            def normalised(n):
                act.wait_ge(s_rstd, n + 1)
                for t in range(ACT_TILES):
                    A(xn[:, t, :], x[:, t, :], ACT.Identity, scale=rstd[:, t:t + 1]).then_inc(s_xn_act, 1)

            def norm_out(l, which, scale, shift):
                act.wait_ge(s_scale, 2 * l + (2 if which == "norm2" else 1))
                for k in range(0, KD, 2):
                    out(T, l, f"{which}.{k}", hT[:, k, 0:SAMPLE], bank(T, f"{which}.{k}"), scale=scale[:, k, 1:2], bias=shift[:, k, 1:2])
                job = f"{which}.{KD}"
                T.wait(act, l, job)
                for k in range(4):
                    ins = A(hT[:, k, SAMPLE:NTOK], bank(T, job)[:, k * P:(k + 1) * P], ACT.Identity, scale=scale[:, k, 0:1], bias=shift[:, k, 0:1])
                T.take(ins, job)

            def mod_rows_out(l, u):
                out(N, l, f"mod.{u}", mod_rows[:, u % 2, :], bank(N, f"mod.{u}")[:, 0:GW])

            def mod_out(l, u):
                job = f"modc.{u}"
                N.wait(act, l, job)
                for c in range(NG):
                    j = NG * u + c
                    kw = dict(bias=par("bmod")[:, j:j + 1]) if u >= MOD_FIRST else {}
                    ins = A(modT[:, j, :], bank(N, job)[:, 2 * c:2 * c + 2], ACT.Identity, **kw)
                N.take(ins, job)

            def modulation(l, lo, hi):
                for which, u in mod_order(lo, hi):
                    (mod_rows_out if which == "mod" else mod_out)(l, u)

            def rows_out(l, g, dst, func=ACT.Identity):
                out(W, l, f"{g}.s", dst[:, 0:TS, :], bank(W, f"{g}.s").rearrange("p (t n) -> p t n", t=TS), func)
                out(W, l, f"{g}.p", dst[:, CTX, :], bank(W, f"{g}.p")[:, 0:GW], func)

            def turned_rows_out(l, name, chunk, gain=None):
                for c in range(NG):
                    kw = {} if gain is None else dict(scale=gain[:, c:c + 1])
                    out(T, l, f"{name}.{c}", yT[:, chunk + c, 0:SAMPLE], bank(T, f"{name}.{c}"), **kw)
                T.wait(act, l, f"{name}.p")
                for c in range(NG):
                    kw = {} if gain is None else dict(scale=gain[:, c:c + 1])
                    ins = A(yT[:, chunk + c, SAMPLE:NTOK], bank(T, f"{name}.p")[:, c * P:(c + 1) * P], ACT.Identity, **kw)
                T.take(ins, f"{name}.p")

            def decays(l):
                A(lgt[:, 0, :], par("dec"), ACT.Exp, scale=float(np.log(2.0))).then_inc(s_dexp, 1)
                act.wait_ge(s_dec, l + 1)
                A(lgt[:, 4, :], lgt[:, 1, :], ACT.Ln).then_inc(s_dlog, 1)

            def ret_tables(l):
                act.wait_ge(s_lg, l + 1)
                lg = lgt[:, 5, :]
                A(kd, kd, ACT.Exp)
                A(cdec.rearrange("p a b -> p (a b)"), lg[:, 8:12], ACT.Exp, scale=float(P))
                for d in range(2):
                    for c in range(NG):
                        for half in range(2):
                            h = 2 * c + half
                            A(masks[:, d, half, c * P:(c + 1) * P], con("expo", 2, P)[:, d, :], ACT.Exp, scale=lg[:, d * HEADS + h:d * HEADS + h + 1])
                        ins = A(qdec[:, d, c, :], con("qpos", 2, P)[:, d, :], ACT.Exp, scale=lg[:, 8 + NG * d + c:9 + NG * d + c])
                ins.then_inc(s_tab, 1)

            def softmax_exp(l, i):
                h, t = BLOCKS[i]
                job = f"s.{i}"
                act.wait_ge(s_nmax, l * len(BLOCKS) + i + 1)
                if i >= 2:
                    T.wait(act, l, f"pt.{i - 2}b")
                o = bank(W, job)
                if h == "ctx":
                    for h in range(HEADS):
                        ins = A(prob[:, i % 2, h * P:(h + 1) * P], o[:, h * P:(h + 1) * P], ACT.Exp, scale=ATT_SCALE, bias=nmax[:, i % 2, h:h + 1], accum_out=rsum[:, i % 2, h:h + 1])
                else:
                    ins = A(prob[:, i % 2, :], o[:, 0:NTOK], ACT.Exp, scale=ATT_SCALE, bias=nmax[:, i % 2, 0:1], accum_out=rsum[:, i % 2, 0:1])
                W.take(ins, job)

            def last_prob_out(l, i):
                if BLOCKS[i][0] == "ctx":
                    return
                if i >= 2:
                    N.wait(act, l, f"pv.{i - 2}")
                out(T, l, f"pt.{i}b", probT[:, i % 2, 4 * P:5 * P], bank(T, f"pt.{i}b")[:, 0:P])

            act.wait_ge(s_cond, 16)
            A(sT.rearrange("p k s -> p (k s)"), sT.rearrange("p k s -> p (k s)"), ACT.Silu).then_inc(s_cond_ready, 1)
            act.wait_ge(s_consts, 16)
            act.wait_ge(s_x, 32)
            for j in range(COMBINE):
                half_squares(j)
            norm_std(0)
            modulation(-1, 0, MOD_FIRST)
            with act.Fori(0, DEPTH) as l:
                for s in STEPS:
                    kind, _, arg = s.partition(":")
                    if kind == "mod":
                        modulation(l, *map(int, arg.split("-")))
                    elif kind == "norm1":
                        normalised(2 * l)
                        act.wait_ge(s_params, 16 * l + 16)
                        norm_out(l, "norm1", A1, modT[:, 0:KD, :])
                        decays(l)
                    elif kind == "in":
                        if arg == "mla":
                            out(W, l, "mla_a.s", mla[:, 0:TS, 0:GW], bank(W, "mla_a.s").rearrange("p (t n) -> p t n", t=TS))
                            out(W, l, "mla_a.p", mla[:, CTX, 0:GW], bank(W, "mla_a.p")[:, 0:GW])
                            out(W, l, "mla_b", mla[:, :, GW:MLA_IN], bank(W, "mla_b")[:, 0:NT * MLA_B].rearrange("p (t n) -> p t n", t=NT))
                        elif arg == "ca":
                            for c in range(NG):
                                job = f"ca.{c}"
                                W.wait(act, l, job)
                                A(glu[:, c, PAD:PAD + SAMPLE], bank(W, job)[:, 0:SAMPLE], ACT.Identity)
                                W.take(A(glu[:, c, CPROMPT + PAD:CPROMPT + PAD + PROMPT], bank(W, job)[:, SAMPLE:NTOK], ACT.Identity), job)
                        elif arg == "cg":
                            for c in range(NG):
                                out(W, l, f"cg.{c}", cscr[:, c, :], bank(W, f"cg.{c}")[:, 0:NTOK], ACT.Sigmoid)
                        elif arg in ("u", "rq", "rk"):
                            dst = dict(u=uT, rq=qT, rk=kT)[arg]
                            for c in range(NG):
                                out(W, l, f"{arg}.{c}", dst[:, c, :], bank(W, f"{arg}.{c}")[:, 0:NTOK])
                            if arg == "rk":
                                for i in range(2):
                                    out(T, l, f"ktok.{i}", ktok[:, 2 * i:2 * i + 2, :], bank(T, f"ktok.{i}").rearrange("p (t n) -> p t n", t=2))
                                out(T, l, "ktok.p", ktok[:, CTX, :], bank(T, "ktok.p")[:, 0:GW])
                        elif arg == "vg":
                            rows_out(l, "vg", vg)
                            act.wait_ge(s_vss, l + 1)
                            A(vstd, vss, ACT.Sqrt, scale=1.0 / GW, bias=con("eps")).then_inc(s_vstd, 1)
                        elif arg == "rv":
                            rows_out(l, "rv", rv)
                        elif arg in ("rgf", "rgb"):
                            rows_out(l, arg, gates[:, int(arg == "rgb")], ACT.Silu)
                        if arg == "mla":
                            act.wait_ge(s_mss, l + 1)
                            A(mstd[:, 0, :], mss[:, 0, :], ACT.Sqrt, scale=1.0 / QL, bias=con("eps"))
                            A(mstd[:, 1, :], mss[:, 1, :], ACT.Sqrt, scale=1.0 / KL, bias=con("eps")).then_inc(s_mstd, 1)
                    elif kind == "latents":
                        act.wait_ge(s_lat, l + 1)
                        act.dma_start(io["new_ckv"][0, bass.ds(l, 1)].rearrange("l p n -> (l p) n"), ctxt[:, CTX, 0:KL]).then_inc(s_ctx_out, 16)
                        act.dma_start(io["new_kpe"][0, bass.ds(l, 1)].rearrange("l p n -> (l p) n"), ctxt[:, CTX, KL:KL + ROPE]).then_inc(s_ctx_out, 16)
                        out(T, l, "cq.0", cqT[:, 0, 0:SAMPLE], bank(T, "cq.0"))
                        out(T, l, "cq.1", cqT[0:QL - P, 1, 0:SAMPLE], bank(T, "cq.1", QL - P))
                        T.wait(act, l, "cq.p")
                        A(cqT[:, 0, SAMPLE:NTOK], bank(T, "cq.p")[:, 0:P], ACT.Identity)
                        T.take(A(cqT[0:QL - P, 1, SAMPLE:NTOK], bank(T, "cq.p", QL - P)[:, P:2 * P], ACT.Identity), "cq.p")
                        out(T, l, "ckv.0", ckvT[:, 0:512], bank(T, "ckv.0"))
                        out(T, l, "ckv.1", ckvT[:, 512:NKEY], bank(T, "ckv.1")[:, 0:NKEY - 512])
                        for i, (lo, hi) in enumerate(((0, 512), (512, NKEY))):
                            src = bank(T, f"kpe.{i}")[NOPE:QK, 0:hi - lo].unsqueeze(1).broadcast_to([ROPE, HEADS, hi - lo])
                            out(T, l, f"kpe.{i}", khT[NOPE:QK, :, lo:hi], src)
                    elif kind == "mla_q":
                        for j, n in enumerate((2, 2, 1)):
                            src = bank(W, f"q.{j}").rearrange("p (t n) -> p t n", t=2)[:, 0:n, 0:HEADS * QK]
                            out(W, l, f"q.{j}", qtok[:, 2 * j:2 * j + n, :], src)
                    elif kind == "mla_kv":
                        for h in range(HEADS):
                            out(W, l, f"kh.{h}", khT[0:NOPE, h, :], bank(W, f"kh.{h}", NOPE)[:, 0:NKEY])
                        for j, n in enumerate((4, 2)):
                            out(W, l, f"v.{j}", vall[:, 4 * j:4 * j + n, :], bank(W, f"v.{j}")[:, 0:n * GW].rearrange("p (t n) -> p t n", t=n))
                        for h in range(HEADS):
                            out(T, l, f"qh.{h}", qhT[:, h, 0:SAMPLE], bank(T, f"qh.{h}", QK))
                        out(T, l, "qh.p", qhT[:, :, SAMPLE:NTOK], bank(T, "qh.p", QK).rearrange("p (h n) -> p h n", h=HEADS))
                    elif kind == "conv_mean":
                        W.taken(act, l, "mean")
                        A(csq, cscr, ACT.Square).then_inc(s_csq, 1)
                    elif kind == "conv_var":
                        out(N, l, "var", cstd, bank(N, "var")[:, 0:NT], ACT.Sqrt, bias=con("eps"))
                        W.taken(act, l, "cstd")
                        for c in range(NG):
                            A(zT[:, c, :], cscr[:, c, :], ACT.Silu, scale=par("lng")[:, c:c + 1], bias=par("lnb")[:, c:c + 1]).then_inc(s_z, 1)
                    elif kind == "conv_out":
                        for c in range(NG):
                            out(W, l, f"pw.{c}", yT[:, NG + c, :], bank(W, f"pw.{c}")[:, 0:NTOK])
                    elif kind == "ret_tables":
                        ret_tables(l)
                    elif kind == "att":
                        i = int(arg)
                        softmax_exp(l, i)
                        if i:
                            last_prob_out(l, i - 1)
                    elif kind == "att_end":
                        turned_rows_out(l, "yd", 3 * NG)
                    elif kind == "rows_g1":
                        for s_, job in ((1, "g1.s"), (0, "g1.p")):
                            out(W, l, job, g1b[:, s_, :], bank(W, job))
                    elif kind == "retention":
                        for t in range(NT):
                            dirs = [d for d in range(2) if t == CTX or (t < TS - 1 if d == 0 else t > 0)]
                            lo, hi = dirs[0] * NG * NOPE, (dirs[-1] + 1) * NG * NOPE
                            out(N, l, f"kv.{t}", kvs[:, t].rearrange("p d n -> p (d n)")[:, lo:hi], bank(N, f"kv.{t}")[:, lo:hi])
                        N.taken(act, l, f"kv.{CTX}")
                        for d in range(2):
                            dst = io["new_state"][0, bass.ds(l, 1), d].rearrange("l (c f) k e -> (l f k) c e", f=2)
                            act.dma_start(dst, kvs[:, CTX, d].rearrange("p (c e) -> p c e", c=NG)).then_inc(s_st_out, 16)
                        def ret_std(t):
                            act.wait_ge(s_ovar, l * NT + t + 1)
                            A(rdev[:, t, :], rvar[:, t, :], ACT.Sqrt, scale=1.0 / NOPE, bias=con("eps")).then_inc(s_ostd, 1)

                        for t in range(NT):
                            for half in range(2):
                                out(T, l, f"ro.{t}.{half}", otok[:, t, half * GW:(half + 1) * GW], bank(T, f"ro.{t}.{half}")[:, 0:GW])
                            act.wait_ge(s_ocen, l * NT + t + 1)
                            A(osq[:, t, :], otok[:, t, :], ACT.Square).then_inc(s_osq, 1)
                            if t:
                                ret_std(t - 1)
                        ret_std(NT - 1)
                        turned_rows_out(l, "yc", 2 * NG, par("gng"))
                    elif kind == "out":
                        u = int(arg)
                        act.wait_ge(s_res, 8 * l + 2 * u + 2)
                        if u:
                            act.wait_ge(s_unit_sq, 4 * l + u)
                        for t in range(NT):
                            ins = A(squares[:, t, :], x[:, t, u * GW:(u + 1) * GW], ACT.Square, accum_out=ss_unit[:, t, u:u + 1])
                        ins.then_inc(s_unit_sq, 1)
                    elif kind == "norm2":
                        norm_std(2 * l + 1)
                        normalised(2 * l + 1)
                        norm_out(l, "norm2", A2, modT[:, 3 * KD:4 * KD, :])
                    elif kind == "router":
                        N.wait(act, l, "logits")
                        A(lgT[:, 0:P], bank(N, "logits")[:, 0:P], ACT.Identity)
                        N.take(A(lgT[0:STRIP, P:2 * P], bank(N, "logits", STRIP)[:, P:2 * P], ACT.Identity), "logits")
                        T.taken(act, l, "logits.t")
                        A(aff, aff, ACT.Exp).then_inc(s_lexp, 1)
                    elif kind == "rows_g2":
                        out(W, l, "g2.s", g2b, bank(W, "g2.s"))
                        out(W, l, "g2.p", g2q, bank(W, "g2.p")[:, 0:QW])
                out(T, l, "slots", slotT, bank(T, "slots")[:, 0:NT * EXPERTS].rearrange("p (t e) -> p t e", t=NT))
                for i, (R, jobs) in enumerate(RINGS):
                    if "spare" in R.at:
                        out(R, l, "spare", spare[:, i], bank(R, "spare")[:, 0:2])

                def take_all(e, job, dst, src):
                    T.wait(act, l, job, e)
                    T.take(A(dst, src, ACT.Identity), job)

                def gathered(e, at, parts):
                    scale, shift = A2, modT[:, 3 * KD:4 * KD, :]
                    for job, i in zip(at, parts):
                        T.wait(act, l, job, e)
                        o = bank(T, job)
                        for k in (range(4 * i, 4 * i + 4) if i < 2 else range(KD)):
                            if i < 2:
                                dst, src, s_ = xeT[:, k].rearrange("p x c -> p (x c)"), o[:, (k % 4) * P:(k % 4 + 1) * P], 1
                            else:
                                dst, src, s_ = xpT[:, k, 0:4:3, :], o[:, k * STRIP:(k + 1) * STRIP].rearrange("p (x c) -> p x c", x=2), 0
                            ins = A(dst, src, ACT.Identity, scale=scale[:, k, s_:s_ + 1], bias=shift[:, k, s_:s_ + 1])
                        T.take(ins, job)

                def silu(m):
                    act.wait_ge(s_gu_used, (m + 1) * KD)
                    A(hm, psW[:, 0, 0:HALFW], ACT.Silu).then_inc(s_silu, 1)
                    A(hmp, psW[:, 1, 0:QW], ACT.Silu).then_inc(s_silu, 1)

                def hidden_out(m):
                    act.wait_ge(s_turned, 2 * m + 1)
                    A(hmT.rearrange("p j c -> p (j c)"), psW[:, 0, 0:HALFW], ACT.Identity).then_inc(s_hT, 1)
                    act.wait_ge(s_turned, 2 * m + 2)
                    A(hmpT.rearrange("p j c -> p (j c)"), psW[:, 1, 0:QW], ACT.Identity).then_inc(s_hT, 1)

                def pair(e, n, last):
                    silu(2 * n)
                    hidden_out(2 * n)
                    for d in range(2):
                        take_all(e, SELECT + d, G[:, d, :], bank(T, SELECT + d))
                    take_all(e, SELECT + 2, Gp, bank(T, SELECT + 2)[:, 0:P])
                    silu(2 * n + 1)
                    if not last:
                        gathered(e, (NEXT,), (0,))
                    hidden_out(2 * n + 1)
                    if not last:
                        gathered(e, (NEXT + 1, NEXT + 2), (1, 2))

                act.wait_ge(s_zeros, l + 1)
                gathered(0, range(GATHERED), range(GATHERED))
                with act.Fori(0, PAIRS - 1) as e:
                    pair(e, l * PAIRS + e, False)
                pair(PAIRS - 1, l * PAIRS + PAIRS - 1, True)
                for j in range(COMBINE):
                    T.taken(act, l, COMBINED - GATHERED + j, PAIRS - 1)
                    half_squares(j)
                norm_std(2 * l + 2)


        @block.vector
        def _(dve):
            V = nc.vector
            chain = Chain(dve, s_dve, DVE_LINKS)
            link, mark = chain.link, chain.mark

            def add_squares(l):
                dve.wait_ge(s_half_sq, l + 1)
                V.tensor_reduce(ss, ss_unit[:, :, 0:2], AX.X, ALU.add).then_inc(s_ss, 1)

            def normalised(l, n, first):
                if first:
                    add_squares(l)
                dve.wait_ge(s_std, n + 1)
                V.reciprocal(rstd, std).then_inc(s_rstd, 1)
                dve.wait_ge(s_rstd, n + 1)
                for t in range(ACT_TILES, NT):
                    V.tensor_scalar(xn[:, t, :], x[:, t, :], rstd[:, t:t + 1], None, ALU.mult).then_inc(s_xn, 1)

            def scales(l, dst, sc, gain):
                V.scalar_tensor_tensor(dst, sc, 1.0, gain.unsqueeze(2).broadcast_to([P, KD, 2]), ALU.add, ALU.mult).then_inc(s_scale, 1)

            def norm_out(l, which, scale, shift):
                dve.wait_ge(s_scale, 2 * l + (2 if which == "norm2" else 1))
                for k in range(1, KD, 2):
                    job = f"{which}.{k}"
                    T.wait(dve, l, job)
                    T.take(V.tensor_scalar(hT[:, k, 0:SAMPLE], bank(T, job), scale[:, k, 1:2], shift[:, k, 1:2], ALU.mult, ALU.add), job)
                job = f"{which}.{KD + 1}"
                T.wait(dve, l, job)
                for k in range(4):
                    ins = V.tensor_scalar(hT[:, 4 + k, SAMPLE:NTOK], bank(T, job)[:, k * P:(k + 1) * P], scale[:, 4 + k, 0:1], shift[:, 4 + k, 0:1], ALU.mult, ALU.add)
                T.take(ins, job)

            def decays(l):
                dve.wait_ge(s_dexp, l + 1)
                y, u, d, z, ln, lg = (lgt[:, i, :] for i in range(6))
                V.tensor_scalar(u, y, -1.0, 1.0, ALU.mult, ALU.add).then_inc(s_dec, 1)
                dve.wait_ge(s_dec, l + 1)
                link(V.tensor_scalar(d, u, -1.0, None, ALU.add))
                link(V.tensor_scalar(z, d, 0.0, None, ALU.is_equal))
                link(V.tensor_tensor(d, d, z, ALU.subtract))
                link(V.reciprocal(d, d))
                dve.wait_ge(s_dlog, l + 1)
                link(V.tensor_tensor(d, d, ln, ALU.mult))
                link(V.tensor_tensor(d, d, z, ALU.add))
                link(V.scalar_tensor_tensor(lg, y, -1.0, d, ALU.mult, ALU.mult))
                V.tensor_scalar(kd[:, 0:HEADS], lg[:, 0:HEADS], con("kpos")[:, 0:1], None, ALU.mult)
                V.tensor_scalar(kd[:, HEADS:2 * HEADS], lg[:, HEADS:2 * HEADS], con("kpos")[:, 1:2], None, ALU.mult).then_inc(s_lg, 1)

            def latents(l):
                W.taken(dve, l, "mla_a.p")
                W.taken(dve, l, "mla_b")
                link(V.tensor_tensor(lat_sq, mla[:, :, 0:QL + KL], mla[:, :, 0:QL + KL], ALU.mult))
                V.tensor_reduce(mss[:, 0, :], lat_sq[:, :, 0:QL], AX.X, ALU.add)
                V.tensor_reduce(mss[:, 1, :], lat_sq[:, :, QL:QL + KL], AX.X, ALU.add).then_inc(s_mss, 1)
                kp = mla[:, 0:TS, QL + KL:MLA_IN]
                kpv = kp.rearrange("p t (a b e) -> p t a b e", a=2, b=2)
                sinv = con("sin", TS, ROPE).rearrange("p t (a b e) -> p t a b e", a=2, b=2)
                rot = rot_k.rearrange("p t (a b e) -> p t a b e", a=2, b=2)
                for b in range(2):
                    V.tensor_tensor(rot[:, :, :, b, :], kpv[:, :, :, 1 - b, :], sinv[:, :, :, b, :], ALU.mult)
                link(V.tensor_tensor(ctxt[:, 0:TS, KL:KL + ROPE], kp, con("cos", TS, ROPE), ALU.mult))
                V.tensor_tensor(ctxt[:, 0:TS, KL:KL + ROPE], ctxt[:, 0:TS, KL:KL + ROPE], rot_k, ALU.add)
                V.tensor_copy(ctxt[:, CTX, KL:KL + ROPE], mla[:, CTX, QL + KL:MLA_IN])
                dve.wait_ge(s_mstd, l + 1)
                link(V.reciprocal(mrstd, mstd))
                V.tensor_tensor(mla[:, :, 0:QL], mla[:, :, 0:QL], mrstd[:, 0, :].unsqueeze(2).broadcast_to([P, NT, QL]), ALU.mult)
                link(V.tensor_tensor(ctxt[:, :, 0:KL], mla[:, :, QL:QL + KL], mrstd[:, 1, :].unsqueeze(2).broadcast_to([P, NT, KL]), ALU.mult))
                V.tensor_tensor(mla[:, :, 0:QL], mla[:, :, 0:QL], par("qg").unsqueeze(1).broadcast_to([P, NT, QL]), ALU.mult)
                V.tensor_tensor(ctxt[:, :, 0:KL], ctxt[:, :, 0:KL], par("kvg").unsqueeze(1).broadcast_to([P, NT, KL]), ALU.mult).then_inc(s_lat, 1)

            def rotate_queries(l):
                W.taken(dve, l, "q.0")
                W.taken(dve, l, "q.1")
                q = carve(ring_r, KT0, TS, HEADS, QK)[:, :, :, NOPE:QK]
                shape = [P, TS, HEADS, ROPE // 4]
                for i in range(4):
                    lo, other = i * (ROPE // 4), (i ^ 1) * (ROPE // 4)
                    sin = con("sin", TS, ROPE)[:, :, lo:lo + ROPE // 4].unsqueeze(2).broadcast_to(shape)
                    ins = V.tensor_tensor(rot_q[:, :, :, lo:lo + ROPE // 4], q[:, :, :, other:other + ROPE // 4], sin, ALU.mult)
                link(ins)
                link(V.tensor_tensor(q, q, con("cos", TS, ROPE).unsqueeze(2).broadcast_to([P, TS, HEADS, ROPE]), ALU.mult))
                V.tensor_tensor(q, q, rot_q, ALU.add).then_inc(s_qrot, 1)

            def gate_conv(l):
                for c in range(NG):
                    W.taken(dve, l, f"cg.{c}")
                    for lo, n, at in ((PAD, SAMPLE, 0), (CPROMPT + PAD, PROMPT, SAMPLE)):
                        ins = V.tensor_tensor(glu[:, c, lo:lo + n], glu[:, c, lo:lo + n], cscr[:, c, at:at + n], ALU.mult)
                link(ins)

            def taps(l):
                dve.wait_ge(s_pads, l + 1)
                w = par("convw", NG, TAPS)
                last = [0, 0]
                for k in range(TAPS):
                    for c in range(NG):
                        src = glu[:, c, k:k + CVAL]
                        if k == 0:
                            last[c] = mark(V.tensor_scalar(cacc[:, c, :], src, w[:, c, 0:1], par("convb")[:, c:c + 1], ALU.mult, ALU.add))
                            continue
                        chain.wait(last[c])
                        ins = V.scalar_tensor_tensor(cacc[:, c, :], src, w[:, c, k:k + 1], cacc[:, c, :], ALU.mult, ALU.add)
                        if k == TAPS - 1 and c == NG - 1:
                            ins.then_inc(s_conv, 1)
                        else:
                            last[c] = mark(ins)

            def spatial_norm(l):
                W.taken(dve, l, "vg.s")
                W.taken(dve, l, "vg.p")
                sq = carve(ring_r, KT0 + NG * NTOK, NT, GW)
                T.wait(dve, l, "qh.p")
                link(V.tensor_tensor(sq, vg, vg, ALU.mult))
                V.tensor_reduce(vss, sq, AX.X, ALU.add).then_inc(s_vss, 1)
                dve.wait_ge(s_vstd, l + 1)
                link(V.reciprocal(vrstd, vstd))
                V.tensor_tensor(vg, vg, vrstd.unsqueeze(2).broadcast_to([P, NT, GW]), ALU.mult).then_inc(s_vn, 1)

            def conv_centre(l):
                W.wait(dve, l, "mean")
                o = bank(W, "mean")
                V.tensor_tensor(cscr[:, :, 0:SAMPLE], cacc[:, :, 0:SAMPLE], o[:, 0:SAMPLE].unsqueeze(1).broadcast_to([P, NG, SAMPLE]), ALU.subtract)
                W.take(V.tensor_tensor(cscr[:, :, SAMPLE:NTOK], cacc[:, :, CPROMPT:CPROMPT + PROMPT], o[:, SAMPLE:NTOK].unsqueeze(1).broadcast_to([P, NG, PROMPT]), ALU.subtract), "mean")

            def conv_normalise(l):
                N.taken(dve, l, "var")
                V.reciprocal(crstd, cstd).then_inc(s_crs, 1)
                W.wait(dve, l, "cstd")
                W.take(V.tensor_tensor(cscr, cscr, bank(W, "cstd")[:, 0:NTOK].unsqueeze(1).broadcast_to([P, NG, NTOK]), ALU.mult), "cstd")

            def mix_out(l):
                sgb = par("sgb", NG, P)
                W.taken(dve, l, "u.0")
                W.taken(dve, l, "u.1")
                for c in range(NG):
                    job = f"mix.{c}"
                    W.wait(dve, l, job)
                    src = bank(W, job)[:, 0:NTOK].rearrange("p (t n) -> p t n", t=NT)
                    dst = yT[:, c, :].rearrange("p (t n) -> p t n", t=NT)
                    W.take(V.scalar_tensor_tensor(dst, src, par("sgg")[:, c:c + 1], sgb[:, c, :].unsqueeze(1).broadcast_to([P, NT, P]), ALU.mult, ALU.add), job)
                for c in range(NG):
                    W.taken(dve, l, f"mix.{c}")
                    V.tensor_tensor(yT[:, c, :], yT[:, c, :], uT[:, c, :], ALU.mult).then_inc(s_mixed, 1)

            def score_max(l, i):
                h, t = BLOCKS[i]
                W.wait(dve, l, f"s.{i}")
                o = bank(W, f"s.{i}")
                nh = HEADS if h == "ctx" else 1
                src = o[:, 0:HEADS * P].rearrange("p (h n) -> p h n", h=HEADS) if h == "ctx" else o[:, 0:NTOK]
                link(V.tensor_reduce(nmax[:, i % 2, 0:nh], src, AX.X, ALU.max, negate=True))
                V.tensor_scalar(nmax[:, i % 2, 0:nh], nmax[:, i % 2, 0:nh], ATT_SCALE, None, ALU.mult).then_inc(s_nmax, 1)

            inv_at = {}

            def probs_out(l, i):
                h, t = BLOCKS[i]
                nh = HEADS if h == "ctx" else 1
                W.taken(dve, l, f"s.{i}")
                inv_at[i] = mark(V.reciprocal(rinv[:, i % 2, 0:nh], rsum[:, i % 2, 0:nh]))
                T.wait(dve, l, f"pt.{i}")
                if i >= 2:
                    N.wait(dve, l, f"pv.{i - 2}")
                T.take(V.tensor_copy(probT[:, i % 2, 0:4 * P], bank(T, f"pt.{i}")), f"pt.{i}")

            def values_out(l, i):
                h, t = BLOCKS[i]
                N.wait(dve, l, f"pv.{i}")
                chain.wait(inv_at[i])
                if h == "ctx":
                    src = bank(N, f"pv.{i}")[:, 0:GW].rearrange("p (h n) -> p h n", h=HEADS)
                    ins = V.tensor_tensor(ydt[:, CTX, :].rearrange("p (h n) -> p h n", h=HEADS), src, rinv[:, i % 2, :].unsqueeze(2).broadcast_to([P, HEADS, NOPE]), ALU.mult)
                else:
                    ins = V.tensor_scalar(ydt[:, t, h * NOPE:(h + 1) * NOPE], bank(N, f"pv.{i}")[:, 0:NOPE], rinv[:, i % 2, 0:1], None, ALU.mult)
                N.take(ins, f"pv.{i}")

            def ret_masks(l):
                dve.wait_ge(s_tab, l + 1)
                for d in range(2):
                    v = masks[:, d].rearrange("p f (c n) -> p (f c) n", c=NG)
                    V.tensor_tensor(v, v, con("mask", 2, P)[:, d, :].unsqueeze(1).broadcast_to([P, HEADS, P]), ALU.mult)
                V.tensor_scalar(kd, kd, float(NOPE) ** -0.5, None, ALU.mult).then_inc(s_msk, 1)

            def masked_scores(l, t):
                if t == 0:
                    dve.wait_ge(s_msk, l + 1)
                if t >= 2:
                    T.wait(dve, l, f"ro.{t - 2}.1")
                for half in range(2):
                    job = f"rs.{t}.{half}"
                    N.wait(dve, l, job)
                    for d in range(2):
                        ins = V.tensor_tensor(sm[:, t % 2, d, half * GW:(half + 1) * GW], bank(N, job)[:, 0:GW], masks[:, d, half], ALU.mult)
                    N.take(ins, job)

            def states(l):
                for t in range(TS):
                    N.taken(dve, l, f"kv.{t}")
                s0 = par("s0", 2, NG, NOPE)
                for i in range(TS - 1):
                    for d in range(2):
                        t = i if d == 0 else TS - 1 - i
                        nt = t + 1 if d == 0 else t - 1
                        for c in range(NG):
                            old = s0[:, d, c, :] if i == 0 else sret[:, t, d, c, :]
                            ins = V.scalar_tensor_tensor(sret[:, nt, d, c, :], old, cdec[:, d, c:c + 1], kvs[:, t, d, c * NOPE:(c + 1) * NOPE], ALU.mult, ALU.add)
                    if i < TS - 2:
                        link(ins)
                ins.then_inc(s_sret, 1)

            def heads(t):
                return otok[:, t, :].rearrange("p (g e) -> p g e", g=8)

            def centre(l, t):
                for half in range(2):
                    T.taken(dve, l, f"ro.{t}.{half}")
                link(V.tensor_reduce(rsums[:, t, :], heads(t), AX.X, ALU.add, negate=True))
                V.scalar_tensor_tensor(heads(t), rsums[:, t, :].unsqueeze(2).broadcast_to([P, 8, NOPE]), 1.0 / NOPE, heads(t), ALU.mult, ALU.add).then_inc(s_ocen, 1)

            def variance(l, t):
                dve.wait_ge(s_osq, l * NT + t + 1)
                ins = V.tensor_reduce(rvar[:, t, :], osq[:, t, :].rearrange("p (g e) -> p g e", g=8), AX.X, ALU.add)
                ins.then_inc(s_ovar, 1)

            def ret_finish(l, t):
                dve.wait_ge(s_ostd, l * NT + t + 1)
                link(V.reciprocal(rrstd[:, t, :], rdev[:, t, :]))
                link(V.tensor_tensor(heads(t), heads(t), rrstd[:, t, :].unsqueeze(2).broadcast_to([P, 8, NOPE]), ALU.mult))
                o = otok[:, t, :].rearrange("p (f d c e) -> p f d c e", f=2, d=2, c=NG)
                for d in range(2):
                    ins = V.tensor_tensor(o[:, :, d], o[:, :, d], gates[:, d, t, :].rearrange("p (c f e) -> p f c e", c=NG, f=2), ALU.mult)
                link(ins)
                V.tensor_tensor(yct[:, t, :].rearrange("p (c f e) -> p f c e", c=NG, f=2), o[:, :, 0], o[:, :, 1], ALU.add).then_inc(s_yc, 1)

            def retention(l):
                masked_scores(l, 0)
                states(l)
                for t in range(NT):
                    if t + 1 < NT:
                        masked_scores(l, t + 1)
                    centre(l, t)
                    if t:
                        variance(l, t - 1)
                    if t > 1:
                        ret_finish(l, t - 2)
                variance(l, NT - 1)
                ret_finish(l, NT - 2)
                ret_finish(l, NT - 1)

            def residual(l, u):
                if u == 0:
                    W.taken(dve, l, "g1.s")
                    W.taken(dve, l, "g1.p")
                lo, hi = u * GW, (u + 1) * GW
                for which, s_, tiles, n in (("s", 1, slice(0, TS), TS), ("p", 0, slice(CTX, NT), 1)):
                    job = f"o.{u}.{which}"
                    W.wait(dve, l, job)
                    tmp = (otmp[:, 0:n * GW] if s_ else otmp_p).rearrange("p (t n) -> p t n", t=n)
                    if u:
                        dve.wait_ge(s_res, 8 * l + 2 * u - s_)
                    W.take(V.tensor_tensor(tmp, bank(W, job)[:, 0:n * GW].rearrange("p (t n) -> p t n", t=n), g1b[:, s_, lo:hi].unsqueeze(1).broadcast_to([P, n, GW]), ALU.mult), job)
                    W.taken(dve, l, job)
                    V.tensor_tensor(x[:, tiles, lo:hi], x[:, tiles, lo:hi], tmp, ALU.add).then_inc(s_res, 1)

            def affinity(l):
                T.wait(dve, l, "logits.t")
                lgts = bank(T, "logits.t")[:, 0:NT * STRIP].rearrange("p (t e) -> p t e", t=NT)[:, :, 0:EXPERTS]
                link(V.tensor_reduce(amax, lgts, AX.X, ALU.max))
                T.take(V.tensor_tensor(aff, lgts, amax.unsqueeze(2).broadcast_to([P, NT, EXPERTS]), ALU.subtract), "logits.t")
                dve.wait_ge(s_lexp, l + 1)
                link(V.tensor_reduce(asum, aff, AX.X, ALU.add))
                link(V.reciprocal(arec, asum))
                V.tensor_tensor(aff, aff, arec.unsqueeze(2).broadcast_to([P, NT, EXPERTS]), ALU.mult).then_inc(s_aff, 1)
            def choose(l):
                for job, lo, hi, cap in (("afft.s", 0, SAMPLE, CAPS), ("afft.p", SAMPLE, NTOK, CAPP)):
                    w, c = work[:, lo:hi], cum[:, lo:hi]
                    T.wait(dve, l, job)
                    T.take(V.tensor_copy(w, bank(T, job, EXPERTS)[:, 0:hi - lo]), job)
                    T.taken(dve, l, job)
                    for _ in range(cap // 8):
                        settle(dve)
                        link(V.max(top8[0:EXPERTS, :], w))
                        settle(dve)
                        link(V.match_replace(w, top8[0:EXPERTS, :], w, -1.0))
                    link(V.tensor_scalar(w, w, 0.0, None, ALU.is_lt))
                    link(V.tensor_tensor_scan(c, w, w, 0.0, ALU.add, ALU.max))
                    V.tensor_tensor(w, c, w, ALU.mult).then_inc(s_slotcode, 1)

            def select(l, e):
                code = slotT[:, :, bass.ds(e * 2, 2)]
                V.tensor_tensor(S, con("iota").unsqueeze(1).unsqueeze(1).broadcast_to([P, TS, 2, CAPS]), code[:, 0:TS].unsqueeze(3).broadcast_to([P, TS, 2, CAPS]), ALU.is_equal)
                V.tensor_tensor(Sp, con("iota")[:, 0:CAPP].unsqueeze(1).broadcast_to([P, 2, CAPP]), code[:, CTX].unsqueeze(2).broadcast_to([P, 2, CAPP]), ALU.is_equal).then_inc(s_S, 1)

            def weigh(l, e, n):
                gates_ = aff[:, :, bass.ds(e * 2, 2)]
                for x_ in range(2):
                    V.tensor_tensor(Sw[:, :, x_, :], S[:, :, 1 - x_, :], gates_[:, 0:TS, 1 - x_:2 - x_].broadcast_to([P, TS, CAPS]), ALU.mult).then_inc(s_swap, 1)
                dve.wait_ge(s_swap, 2 * n + 2)
                V.tensor_tensor(S, S, gates_[:, 0:TS].unsqueeze(3).broadcast_to([P, TS, 2, CAPS]), ALU.mult)
                V.tensor_tensor(Spw, Sp.unsqueeze(1).broadcast_to([P, 4, 2, CAPP]), gates_[:, CTX].unsqueeze(1).unsqueeze(3).broadcast_to([P, 4, 2, CAPP]), ALU.mult).then_inc(s_weighed, 1)

            def hidden(m, i):
                h, up = ((hm, psW[:, 0, HALFW:2 * HALFW]), (hmp, psW[:, 1, QW:2 * QW]))[i]
                dve.wait_ge(s_silu, START + 2 * m + i + 1)
                V.tensor_tensor(h, h, up, ALU.mult).then_inc(s_hm, 1)

            def rows_out(m, i):
                dve.wait_ge(s_dn_used, 4 * m + 4)
                for c in range(2):
                    h = c ^ i
                    p = slice(c * 64, c * 64 + 64)
                    V.tensor_tensor(ye[p, h, :], psN[p, h, :], g2b[p, h * HALFW:(h + 1) * HALFW], ALU.mult).then_inc(s_ye, 1)
                if i:
                    for q in range(4):
                        p = slice(q * STRIP, (q + 1) * STRIP)
                        ins = V.tensor_tensor(yep[p, (q % 2) * QW:(q % 2 + 1) * QW], psW[p, 1, HALFW:HALFW + QW], g2q[p, :], ALU.mult)
                    ins.then_inc(s_yep, 1)

            def combined(l, e, at, jobs=range(COMBINE)):
                for j in jobs:
                    half, t = divmod(j, NT)
                    xs = x[:, t, half * HALFW:(half + 1) * HALFW]
                    T.wait(dve, l, at + j, e)
                    T.take(V.tensor_tensor(xs, xs, bank(T, at + j), ALU.add), at + j)

            def pair(l, e, n, first, last):
                hidden(2 * n, 0)
                if not first:
                    combined(l, e, COMBINED - T_PAIR, range(0, 1))
                hidden(2 * n, 1)
                if not first:
                    combined(l, e, COMBINED - T_PAIR, range(1, COMBINE))
                if not last:
                    T.wait(dve, l, SELECT + 2, e)
                    settle(dve)
                    select(l, e + 1)
                rows_out(2 * n, 0)
                hidden(2 * n + 1, 0)
                hidden(2 * n + 1, 1)
                if not last:
                    T.wait(dve, l, NEXT + 2, e)
                    settle(dve)
                    weigh(l, e + 1, n + 1)
                rows_out(2 * n + 1, 1)
                if last:
                    combined(l, e, COMBINED - GATHERED)

            l_ = [0]
            dve.wait_ge(s_consts, 16)
            dve.wait_ge(s_x, 32)
            with dve.Fori(0, DEPTH) as l:
                l_[0] = l
                chain.start_layer(l)
                normalised(l, 2 * l, True)
                dve.wait_ge(s_params, 16 * l + 16)
                for s in STEPS:
                    kind, _, arg = s.partition(":")
                    if kind == "norm1":
                        for u in (MOD_FIRST - 2, MOD_FIRST - 1):
                            N.taken(dve, l, before(N, f"modc.{u}"))
                        link(V.tensor_tensor(modT[:, 0:2 * KD, :], modT[:, 0:2 * KD, :], par("bmod")[:, 0:2 * KD].unsqueeze(2).broadcast_to([P, 2 * KD, 2]), ALU.add))
                        scales(l, A1, modT[:, KD:2 * KD, :], par("n1g"))
                        norm_out(l, "norm1", A1, modT[:, 0:KD, :])
                        decays(l)
                    elif s == "in:mla":
                        latents(l)
                    elif s == "in:cg":
                        gate_conv(l)
                    elif kind == "mla_q":
                        rotate_queries(l)
                    elif kind == "mla_kv":
                        taps(l)
                    elif s == "in:vg":
                        spatial_norm(l)
                    elif kind == "conv_mean":
                        conv_centre(l)
                    elif kind == "conv_var":
                        conv_normalise(l)
                    elif kind == "mix":
                        mix_out(l)
                    elif kind == "ret_tables":
                        ret_masks(l)
                    elif kind == "att":
                        score_max(l, int(arg))
                        if int(arg) > 1:
                            values_out(l, int(arg) - 2)
                        if int(arg):
                            probs_out(l, int(arg) - 1)
                    elif kind == "att_end":
                        values_out(l, len(BLOCKS) - 2)
                        probs_out(l, len(BLOCKS) - 1)
                        values_out(l, len(BLOCKS) - 1)
                    elif kind == "retention":
                        retention(l)
                    elif kind == "out":
                        residual(l, int(arg))
                    elif kind == "norm2":
                        dve.wait_ge(s_unit_sq, 4 * l + 4)
                        V.tensor_reduce(ss, ss_unit, AX.X, ALU.add).then_inc(s_ss, 1)
                        normalised(l, 2 * l + 1, False)
                        N.taken(dve, l, "modc.18")
                        N.taken(dve, l, "modc.19")
                        scales(l, A2, modT[:, 4 * KD:5 * KD, :], par("n2g"))
                        norm_out(l, "norm2", A2, modT[:, 3 * KD:4 * KD, :])
                    elif kind == "router":
                        affinity(l)
                    elif kind == "rows_g2":
                        choose(l)
                chain.end_layer()
                T.taken(dve, l, "slots")
                dve.wait_ge(s_aff, l + 1)
                settle(dve)
                select(l, 0)
                T.wait(dve, l, GATHERED - 1)
                dve.wait_ge(s_S, l * PAIRS + 1)
                settle(dve)
                weigh(l, 0, l * PAIRS)
                for j in ("g2.s", "g2.p"):
                    W.taken(dve, l, j)
                dve.wait_ge(s_zeros, l + 1)
                settle(dve)
                pair(l, 0, l * PAIRS, True, False)
                with dve.Fori(1, PAIRS - 1) as e:
                    pair(l, e, l * PAIRS + e, False, False)
                pair(l, PAIRS - 1, l * PAIRS + PAIRS - 1, False, True)
            add_squares(DEPTH)
            dve.wait_ge(s_std, 2 * DEPTH + 1)
            V.reciprocal(rstd, std).then_inc(s_dve, 1)
            dve.wait_ge(s_dve, DEPTH * DVE_LINKS + 1)
            dve.wait_ge(s_fg, 16)
            for t in range(NT):
                V.scalar_tensor_tensor(xn[:, t, :], x[:, t, :], rstd[:, t:t + 1], stream_r[:, 0:D], ALU.mult, ALU.mult).then_inc(s_y, 1)

        @block.gpsimd
        def _(pool):
            Q = nc.gpsimd

            with pool.Fori(0, DEPTH) as l:
                W.wait(pool, l, "mla_a.s")
                settle(pool)
                for c in range(NG):
                    for lo, n in ((0, PAD), (PAD + SAMPLE, 2 * PAD), (CROW - PAD, PAD)):
                        ins = Q.memset(glu[:, c, lo:lo + n], 0.0)
                ins.then_inc(s_pads, 1)
                pool.wait_ge(s_tab, l + 1)
                W.wait(pool, l, "rgb.p")
                for d in range(2):
                    Q.tensor_tensor(qTd[:, d].rearrange("p c (t n) -> p c t n", t=TS), qT[:, :, 0:SAMPLE].rearrange("p c (t n) -> p c t n", t=TS),
                                    qdec[:, d].unsqueeze(2).broadcast_to([P, NG, TS, P]), ALU.mult).then_inc(s_qtd, 1)
                W.wait(pool, l, f"s.{len(BLOCKS) - 1}")
                pool.wait_ge(s_msk, l + 1)
                for j in ("ktok.1", "ktok.p"):
                    T.taken(pool, l, j)
                for d in range(2):
                    Q.tensor_tensor(kdk[:, d].rearrange("p t (h n) -> p t h n", h=HEADS), ktok.rearrange("p t (h n) -> p t h n", h=HEADS),
                                    kd[:, d * HEADS:(d + 1) * HEADS].unsqueeze(1).unsqueeze(3).broadcast_to([P, NT, HEADS, NOPE]), ALU.mult).then_inc(s_kdk, 1)
                T.wait(pool, l, "slots")
                settle(pool)
                Q.memset(zeroed, 0.0).then_inc(s_zeros, 1)


_OUT_SHAPES = (("y_prompt", (1, PROMPT, D)), ("y_sample", (1, SAMPLE, D)), ("new_ckv", (1, DEPTH, P, KL)),
               ("new_kpe", (1, DEPTH, P, ROPE)), ("new_state", (1, DEPTH, 2, HEADS, NOPE, NOPE)))
_BIG = ("x_prompt", "x_sample", "w_mod", "w_in", "w_out", "w_gate", "w_up", "w_down")


def _constants():
    c = np.zeros((P, NCONST), np.float32)

    def put(name, v):
        lo, hi = CAT[name]
        c[:, lo:hi] = np.asarray(v, np.float32).reshape(-1, hi - lo)

    j, i = np.arange(P)[:, None], np.arange(P)[None, :]
    put("ident", np.eye(P))
    put("mean", np.full((P, P), 1.0 / GW))
    put("expo", np.concatenate([np.maximum(i - j, 0), np.maximum(j - i, 0)], 1))
    put("mask", np.concatenate([i >= j, j >= i], 1) * float(NOPE) ** -0.5)
    put("qpos", np.concatenate([np.tile(i + 1, (P, 1)), np.tile(P - i, (P, 1))], 1))
    put("kpos", np.concatenate([P - 1 - j, j], 1))
    tok = np.arange(SAMPLE)
    inv = (np.float32(10000.0) ** (-np.arange(0, ROPE // 2, 2, dtype=np.float32) / np.float32(ROPE // 2))).astype(np.float32)
    ra, ca = ((v.astype(np.float32)[:, None] * inv) for v in (tok // 64, tok % 64))
    ang = np.concatenate([ra, ra, ca, ca], 1).reshape(TS, P, ROPE).transpose(1, 0, 2)
    sign = np.repeat(np.array([-1.0, 1.0, -1.0, 1.0], np.float32), ROPE // 4)
    put("cos", np.cos(ang))
    put("sin", np.sin(ang) * sign)
    put("iota", np.tile(np.arange(1, CAPS + 1), (P, 1)))
    put("strips", np.tile(np.eye(STRIP)[:, 0:2], (P // STRIP, 1)))
    put("eps", np.full((P, 1), EPS))
    return c


def _params(a):
    out = np.zeros((DEPTH, P, NPARAM), np.float32)

    def put(name, v, rows=slice(0, P), cols=None):
        lo, hi = PAT[name]
        lo, hi = (lo, hi) if cols is None else (lo + cols[0], lo + cols[1])
        out[:, rows, lo:hi] = v.reshape(DEPTH, -1, hi - lo)

    def columns(v):
        return v.reshape(DEPTH, -1, P).transpose(0, 2, 1)

    def everywhere(v):
        return np.repeat(v.reshape(DEPTH, 1, -1), P, axis=1)

    for name, key in (("n1g", "norm1_g"), ("n2g", "norm2_g"), ("bmod", "b_mod"), ("sgg", "sg_norm_g"), ("convb", "conv_b"),
                      ("lng", "conv_ln_g"), ("lnb", "conv_ln_b"), ("gng", "ret_gn_g")):
        put(name, columns(a[key]))
    rt = np.zeros((DEPTH, P, KD, STRIP), np.float32)
    rt[..., 0:EXPERTS] = a["router"].reshape(DEPTH, KD, P, EXPERTS).transpose(0, 2, 1, 3)
    put("router", rt)
    df, db = a["ret_decay_f"], a["ret_decay_b"]
    put("dec", everywhere(df), cols=(0, 4))
    put("dec", everywhere(db), cols=(4, 8))
    for half in range(2):
        rows = slice(64 * half, 64 * half + 64)
        put("dec", everywhere(df[:, half::2])[:, :64], rows, (8, 10))
        put("dec", everywhere(db[:, half::2])[:, :64], rows, (10, 12))
        put("sgb", everywhere(a["sg_b"][:, half::2])[:, :64], rows)
    put("convw", a["conv_w"].reshape(DEPTH, TAPS, NG, P).transpose(0, 3, 2, 1))
    put("sgw", a["sg_w"].transpose(0, 3, 1, 2))
    put("pw", a["conv_pw"].reshape(DEPTH, NG, P, GW).transpose(0, 2, 1, 3))
    put("qg", everywhere(a["q_norm_g"]))
    put("kvg", everywhere(a["kv_norm_g"]))
    put("wuq", a["w_uq"][:, 0:P], cols=(0, HEADS * QK))
    put("wuq", a["w_uq"][:, P:QL], slice(0, QL - P), (HEADS * QK, 2 * HEADS * QK))
    put("wukv", a["w_ukv"])
    put("cache", a["cache_mla_ckv"][0], cols=(0, KL))
    put("cache", a["cache_mla_kpe"][0], cols=(KL, KL + ROPE))
    put("s0", a["state_ret"][0].reshape(DEPTH, 2, NG, P, NOPE).transpose(0, 3, 1, 2, 4))
    return out


def kernel(**inputs):
    import concourse.bacc as bacc
    from concourse.bass_utils import run_bass_kernel_spmd

    a = {k: np.ascontiguousarray(v) for k, v in inputs.items()}
    arrays = {k: a[k] for k in _BIG}
    cond = np.zeros((P, KD, STRIP), np.float32)
    cond[:, :, 0:2] = np.stack([a["c_ctx"], a["c"][0]]).reshape(2, KD, P).transpose(2, 1, 0)
    arrays["cond"] = cond.reshape(P, KD * STRIP)
    arrays["params"], arrays["consts"] = _params(a), _constants()
    arrays["final_g"] = a["final_norm_g"]
    nc = bacc.Bacc("TRN2", target_bir_lowering=False, num_devices=1)
    io = {k: nc.dram_tensor(k, v.shape, F32, kind="ExternalInput").ap() for k, v in arrays.items()}
    for name, shape in _OUT_SHAPES:
        io[name] = nc.dram_tensor(name, shape, F32, kind="ExternalOutput").ap()
    build(nc, io)
    r = run_bass_kernel_spmd(nc, [arrays], core_ids=[0])
    return tuple(r.results[0][name] for name, _ in _OUT_SHAPES)
```
